# Optimizing a Trainium2 kernel written in Bass

```python
import math
import jax, jax.numpy as jnp
from jax import lax
import numpy as np

D_MODEL = 1024
BATCH = 1
SEQ = 256
DEPTH = 1

MEM_LEN = 256
EPS = 1e-6
DA_HEADS = 4
DA_QK_DIM = 64
DA_V_DIM = 2 * DA_QK_DIM
DA_WIDTH = DA_HEADS * DA_V_DIM
QK_WIDTH = DA_HEADS * 2 * DA_QK_DIM
POOL_WINDOWS = (2, 4, 8, 16)
POOL_GROUPS = len(POOL_WINDOWS)
POOL_WIDTH = D_MODEL - DA_WIDTH
POOL_GROUP_DIM = POOL_WIDTH // POOL_GROUPS
MIX_WIDTH = DA_WIDTH + POOL_WIDTH
IN_WIDTH = 2 * QK_WIDTH + DA_WIDTH + POOL_WIDTH
ROPE_THETA = 500000.0
ROPE_DIM = DA_QK_DIM // 4
BLOCK_Q = 128
X_HEADS = 4
X_HEAD_DIM = D_MODEL // X_HEADS
D_FF = -(-(8 * D_MODEL) // (3 * 256)) * 256
def _lambda_init(layer_idx):
    return 0.8 - 0.6 * math.exp(-0.3 * (layer_idx - 1))


def rmsnorm(x, g):
    xf = x.astype(jnp.float32)
    y = xf * lax.rsqrt(jnp.mean(xf * xf, axis=-1, keepdims=True) + EPS)
    return (y * g.astype(jnp.float32)).astype(x.dtype)

def rope_tables(positions, dtype):
    inv_freq = ROPE_THETA ** (-jnp.arange(0, ROPE_DIM, 2, dtype=jnp.float32) / ROPE_DIM)
    ang = positions.astype(jnp.float32)[..., None] * inv_freq
    return jnp.cos(ang).astype(dtype), jnp.sin(ang).astype(dtype)

def apply_partial_rope(t, cos, sin):
    cos = cos[:, :, None, None, :]
    sin = sin[:, :, None, None, :]
    half = ROPE_DIM // 2
    t1 = t[..., :half]
    t2 = t[..., half:ROPE_DIM]
    rest = t[..., ROPE_DIM:]
    return jnp.concatenate([t1 * cos - t2 * sin, t2 * cos + t1 * sin, rest], axis=-1)

def diff_attention(q, k, v, lam):
    seq = q.shape[3]
    scale = DA_QK_DIM ** -0.5
    outs = []
    for i in range(seq // BLOCK_Q):
        q0 = i * BLOCK_Q
        kend = q0 + BLOCK_Q
        qb = q[:, :, :, q0:kend]
        kb = k[:, :, :, :kend]
        vb = v[:, :, :kend]
        s = jnp.einsum('bhmqd,bhmkd->bhmqk', qb, kb).astype(jnp.float32) * scale
        mask = (q0 + jnp.arange(BLOCK_Q))[:, None] >= jnp.arange(kend)[None, :]
        s = jnp.where(mask, s, -jnp.inf)
        p = jax.nn.softmax(s, axis=-1)
        a = p[:, :, 0] - lam * p[:, :, 1]
        outs.append(jnp.einsum('bhqk,bhkd->bhqd', a.astype(v.dtype), vb))
    return jnp.concatenate(outs, axis=2)

def causal_multiscale_pool(u):
    b, s, _ = u.shape
    uf = u.astype(jnp.float32).reshape(b, s, POOL_GROUPS, POOL_GROUP_DIM)
    c = jnp.cumsum(uf, axis=1)
    t1 = jnp.arange(1, s + 1, dtype=jnp.float32)
    groups = []
    for g, w in enumerate(POOL_WINDOWS):
        cg = c[:, :, g]
        shifted = jnp.pad(cg, ((0, 0), (w, 0), (0, 0)))[:, :s]
        count = jnp.minimum(t1, float(w))[None, :, None]
        groups.append((cg - shifted) / count - uf[:, :, g])
    return jnp.stack(groups, axis=2).astype(u.dtype)

def first_inputs(seed: int = 0) -> dict:
    key = jax.random.key(seed)
    ks = jax.random.split(key, 32)
    f32 = jnp.float32

    def w(k, shape, fan_in):
        return jax.random.normal(k, shape, f32) * (fan_in ** -0.5)

    def gain(k, n):
        return 1.0 + 0.02 * jax.random.normal(k, (n,), f32)

    return {
        "x": jax.random.normal(ks[0], (BATCH, SEQ, D_MODEL), f32),
        "mem": jax.random.normal(ks[1], (BATCH, MEM_LEN, D_MODEL), f32),
        "positions": jnp.broadcast_to(jnp.arange(SEQ, dtype=jnp.int32), (BATCH, SEQ)),
        "g_mix_pre": gain(ks[2], D_MODEL),
        "w_in": w(ks[3], (D_MODEL, IN_WIDTH), D_MODEL),
        "lambda_q1": 0.1 * jax.random.normal(ks[4], (DA_QK_DIM,), f32),
        "lambda_k1": 0.1 * jax.random.normal(ks[5], (DA_QK_DIM,), f32),
        "lambda_q2": 0.1 * jax.random.normal(ks[6], (DA_QK_DIM,), f32),
        "lambda_k2": 0.1 * jax.random.normal(ks[7], (DA_QK_DIM,), f32),
        "g_subln": gain(ks[8], DA_V_DIM),
        "w_pool": w(ks[9], (POOL_GROUPS, POOL_GROUP_DIM, POOL_GROUP_DIM), POOL_GROUP_DIM),
        "pool_scale": 1.0 + 0.1 * jax.random.normal(ks[10], (POOL_WIDTH,), f32),
        "w_out": w(ks[11], (MIX_WIDTH, D_MODEL), MIX_WIDTH),
        "g_mix_post": gain(ks[12], D_MODEL),
        "g_x_pre": gain(ks[13], D_MODEL),
        "g_mem": gain(ks[14], D_MODEL),
        "w_xq": w(ks[15], (D_MODEL, X_HEADS * X_HEAD_DIM), D_MODEL),
        "w_xkv": w(ks[16], (D_MODEL, 2 * X_HEADS * X_HEAD_DIM), D_MODEL),
        "w_xo": w(ks[17], (X_HEADS * X_HEAD_DIM, D_MODEL), X_HEADS * X_HEAD_DIM),
        "g_x_post": gain(ks[18], D_MODEL),
        "g_ffn_pre": gain(ks[19], D_MODEL),
        "w_gate": w(ks[20], (D_MODEL, D_FF), D_MODEL),
        "w_up": w(ks[21], (D_MODEL, D_FF), D_MODEL),
        "w_down": w(ks[22], (D_FF, D_MODEL), D_FF),
        "g_ffn_post": gain(ks[23], D_MODEL),
    }

def first_block(x, mem, positions, g_mix_pre, w_in, lambda_q1, lambda_k1, lambda_q2,
              lambda_k2, g_subln, w_pool, pool_scale, w_out, g_mix_post, g_x_pre,
              g_mem, w_xq, w_xkv, w_xo, g_x_post, g_ffn_pre, w_gate, w_up, w_down,
              g_ffn_post):
    b, s, _ = x.shape
    cos, sin = rope_tables(positions, x.dtype)
    mem_n = rmsnorm(mem, g_mem)

    for layer in range(DEPTH):
        lam_init = _lambda_init(layer + 1)

        h = rmsnorm(x, g_mix_pre)
        proj = h @ w_in
        q = proj[..., :QK_WIDTH].reshape(b, s, DA_HEADS, 2, DA_QK_DIM)
        k = proj[..., QK_WIDTH:2 * QK_WIDTH].reshape(b, s, DA_HEADS, 2, DA_QK_DIM)
        v = proj[..., 2 * QK_WIDTH:2 * QK_WIDTH + DA_WIDTH].reshape(b, s, DA_HEADS, DA_V_DIM)
        u = proj[..., 2 * QK_WIDTH + DA_WIDTH:]

        q = apply_partial_rope(q, cos, sin).transpose(0, 2, 3, 1, 4)
        k = apply_partial_rope(k, cos, sin).transpose(0, 2, 3, 1, 4)
        v = v.transpose(0, 2, 1, 3)
        lam = (jnp.exp(jnp.sum(lambda_q1.astype(jnp.float32) * lambda_k1.astype(jnp.float32)))
               - jnp.exp(jnp.sum(lambda_q2.astype(jnp.float32) * lambda_k2.astype(jnp.float32)))
               + lam_init)
        da = diff_attention(q, k, v, lam)
        da = rmsnorm(da, g_subln) * (1.0 - lam_init)
        da = da.transpose(0, 2, 1, 3).reshape(b, s, DA_WIDTH)

        pooled = causal_multiscale_pool(u)
        po = jnp.einsum('bsgc,gcd->bsgd', pooled, w_pool).reshape(b, s, POOL_WIDTH)
        po = po * pool_scale

        mix = jnp.concatenate([da, po], axis=-1) @ w_out
        x = x + rmsnorm(mix, g_mix_post)

        hq = rmsnorm(x, g_x_pre)
        xq = (hq @ w_xq).reshape(b, s, X_HEADS, X_HEAD_DIM)
        kv = (mem_n @ w_xkv).reshape(b, MEM_LEN, 2, X_HEADS, X_HEAD_DIM)
        sc = jnp.einsum('bshd,bmhd->bhsm', xq, kv[:, :, 0]).astype(jnp.float32) * (X_HEAD_DIM ** -0.5)
        pm = jax.nn.softmax(sc, axis=-1).astype(x.dtype)
        xo = jnp.einsum('bhsm,bmhd->bshd', pm, kv[:, :, 1]).reshape(b, s, X_HEADS * X_HEAD_DIM)
        x = x + rmsnorm(xo @ w_xo, g_x_post)

        hf = rmsnorm(x, g_ffn_pre)
        ff = (jax.nn.silu(hf @ w_gate) * (hf @ w_up)) @ w_down
        x = x + rmsnorm(ff, g_ffn_post)

    return x


DEPTH_2 = 2

RET_HEADS = 4
RET_DK = 128
RET_DV = 128
RET_CHUNK = 128
ROPE_BASE = 10000.0
NSA_HEADS = 8
NSA_KV_GROUPS = 2
NSA_HPG = NSA_HEADS // NSA_KV_GROUPS
NSA_HD = 64
CMP_BLOCK = 32
CMP_STRIDE = 16
SLC_BLOCK = 64
N_SELECT = 8
FORCED_LOCAL = 2
FORCE_BONUS = 1.0e4
WINDOW = 512
Q_BLOCK = 128
HGRN_HEADS = 8
HGRN_DK = D_MODEL // HGRN_HEADS
HGRN_DV = D_MODEL // HGRN_HEADS
HGRN_CHUNK = 64
D_FF_2 = -(-8 * D_MODEL // (3 * 256)) * 256

EVEN_SIZES = ([RET_HEADS * RET_DK] * 2 + [RET_HEADS * RET_DV] * 2 + [NSA_HEADS * NSA_HD]
              + [NSA_KV_GROUPS * NSA_HD] * 6 + [3 * NSA_HEADS])
EVEN_IN = sum(EVEN_SIZES)
EVEN_MIX = RET_HEADS * RET_DV + NSA_HEADS * NSA_HD
ODD_SIZES = [HGRN_HEADS * HGRN_DK] * 2 + [HGRN_HEADS * HGRN_DV] * 2
ODD_IN = sum(ODD_SIZES)
ODD_MIX = HGRN_HEADS * HGRN_DV
N_EVEN = (DEPTH_2 + 1) // 2
N_ODD = DEPTH_2 // 2


def _split(a, sizes):
    return jnp.split(a, list(np.cumsum(sizes)[:-1]), axis=-1)

def rmsnorm_2(x, g):
    xf = x.astype(jnp.float32)
    y = xf * lax.rsqrt(jnp.mean(xf * xf, axis=-1, keepdims=True) + EPS)
    return (y * g.astype(jnp.float32)).astype(x.dtype)

def rotary(x):
    S, d = x.shape[-2], x.shape[-1]
    half = d // 2
    inv = ROPE_BASE ** (-jnp.arange(half, dtype=jnp.float32) / half)
    ang = jnp.arange(S, dtype=jnp.float32)[:, None] * inv[None, :]
    cos, sin = jnp.cos(ang), jnp.sin(ang)
    x1, x2 = x[..., :half], x[..., half:]
    return jnp.concatenate([x1 * cos - x2 * sin, x1 * sin + x2 * cos], axis=-1)

def masked_softmax(s, mask):
    s = jnp.where(mask, s, -jnp.inf)
    m = jnp.max(s, axis=-1, keepdims=True)
    m = jnp.where(jnp.isfinite(m), m, 0.0)
    p = jnp.exp(s - m)
    return p / jnp.maximum(jnp.sum(p, axis=-1, keepdims=True), 1e-30)

def retention_chunkwise(q, k, v):
    B, H, S, dk = q.shape
    dv = v.shape[-1]
    C = min(RET_CHUNK, S)
    NC = S // C
    log_gamma = jnp.log(1.0 - 2.0 ** (-5.0 - jnp.arange(H, dtype=jnp.float32)))
    q = q.reshape(B, H, NC, C, dk)
    k = k.reshape(B, H, NC, C, dk)
    v = v.reshape(B, H, NC, C, dv)
    idx = jnp.arange(C, dtype=jnp.float32)
    diff = idx[:, None] - idx[None, :]
    causal = diff >= 0
    dmat = jnp.where(causal, jnp.exp(log_gamma[:, None, None] * jnp.where(causal, diff, 0.0)), 0.0)
    scores = jnp.einsum('bhncd,bhnsd->bhncs', q, k) * dmat[None, :, None]
    o_inner = jnp.einsum('bhncs,bhnse->bhnce', scores, v)
    k_dec = k * jnp.exp(log_gamma[:, None] * (C - 1 - idx)[None, :])[None, :, None, :, None]
    chunk_kv = jnp.einsum('bhncd,bhnce->nbhde', k_dec, v)
    gamma_c = jnp.exp(log_gamma * C)[None, :, None, None]

    def step(state, kv):
        return gamma_c * state + kv, state

    _, r_prev = lax.scan(step, jnp.zeros((B, H, dk, dv), jnp.float32), chunk_kv)
    q_dec = q * jnp.exp(log_gamma[:, None] * (idx + 1.0)[None, :])[None, :, None, :, None]
    o_cross = jnp.einsum('bhncd,nbhde->bhnce', q_dec, r_prev)
    return (o_inner + o_cross).reshape(B, H, S, dv)

def nsa_compress(kv, pos_emb, w1, w2):
    B, G, S, d = kv.shape
    r = CMP_BLOCK // CMP_STRIDE
    parts = kv.reshape(B, G, S // CMP_STRIDE, CMP_STRIDE, d)
    n = S // CMP_STRIDE - r + 1
    blocks = jnp.concatenate([parts[:, :, j:j + n] for j in range(r)], axis=3)
    flat = (blocks + pos_emb.astype(jnp.float32)).reshape(B, G, n, CMP_BLOCK * d)
    return jax.nn.gelu(flat @ w1.astype(jnp.float32)) @ w2.astype(jnp.float32)

def nsa_attention(q, k_cmp, v_cmp, k_slc, v_slc, k_win, v_win, gates):
    B, G, HPG, S, d = q.shape
    scale = d ** -0.5
    n_cmp = k_cmp.shape[2]
    n_slc = S // SLC_BLOCK
    n_sel = min(N_SELECT, n_slc)
    cs = np.arange(n_cmp) * CMP_STRIDE
    ce = cs + CMP_BLOCK - 1
    ss = np.arange(n_slc) * SLC_BLOCK
    se = ss + SLC_BLOCK - 1
    overlap = jnp.asarray(((cs[:, None] <= se[None, :]) & (ce[:, None] >= ss[None, :])).astype(np.float32))
    cmp_end = jnp.asarray(ce.astype(np.int32))
    ks_blocks = k_slc.reshape(B, G, n_slc, SLC_BLOCK, d)
    vs_blocks = v_slc.reshape(B, G, n_slc, SLC_BLOCK, d)
    kw_pad = jnp.pad(k_win, ((0, 0), (0, 0), (WINDOW, 0), (0, 0)))
    vw_pad = jnp.pad(v_win, ((0, 0), (0, 0), (WINDOW, 0), (0, 0)))
    bi = jnp.arange(B)[:, None, None, None]
    gi = jnp.arange(G)[None, :, None, None]
    jblk = jnp.arange(n_slc)
    offs = jnp.arange(SLC_BLOCK)

    def block(i):
        q0 = i * Q_BLOCK
        t = q0 + jnp.arange(Q_BLOCK)
        qb = lax.dynamic_slice_in_dim(q, q0, Q_BLOCK, axis=3)
        s_c = jnp.einsum('bghqd,bgnd->bghqn', qb, k_cmp) * scale
        p_c = masked_softmax(s_c, cmp_end[None, :] <= t[:, None])
        o_c = jnp.einsum('bghqn,bgnd->bghqd', p_c, v_cmp)
        imp = jnp.einsum('bgqn,nj->bgqj', jnp.sum(p_c, axis=2), overlap)
        bt = (t // SLC_BLOCK)[:, None]
        valid_s = jblk[None, :] <= bt
        forced = (jblk[None, :] == 0) | ((bt - jblk[None, :] >= 0) & (bt - jblk[None, :] < FORCED_LOCAL))
        score = jnp.where(valid_s, imp + jnp.where(forced, FORCE_BONUS, 0.0), -1e30)
        _, idx = lax.top_k(score, n_sel)
        kg = ks_blocks[bi, gi, idx].reshape(B, G, Q_BLOCK, n_sel * SLC_BLOCK, d)
        vg = vs_blocks[bi, gi, idx].reshape(B, G, Q_BLOCK, n_sel * SLC_BLOCK, d)
        kpos = (idx[..., None] * SLC_BLOCK + offs).reshape(B, G, Q_BLOCK, n_sel * SLC_BLOCK)
        s_s = jnp.einsum('bghqd,bgqkd->bghqk', qb, kg) * scale
        p_s = masked_softmax(s_s, (kpos <= t[None, None, :, None])[:, :, None])
        o_s = jnp.einsum('bghqk,bgqkd->bghqd', p_s, vg)
        kw = lax.dynamic_slice_in_dim(kw_pad, q0, WINDOW + Q_BLOCK, axis=2)
        vw = lax.dynamic_slice_in_dim(vw_pad, q0, WINDOW + Q_BLOCK, axis=2)
        spos = q0 - WINDOW + jnp.arange(WINDOW + Q_BLOCK)
        dist = t[:, None] - spos[None, :]
        valid_w = (dist >= 0) & (dist < WINDOW) & (spos[None, :] >= 0)
        s_w = jnp.einsum('bghqd,bgkd->bghqk', qb, kw) * scale
        o_w = jnp.einsum('bghqk,bgkd->bghqd', masked_softmax(s_w, valid_w), vw)
        gb = lax.dynamic_slice_in_dim(gates, q0, Q_BLOCK, axis=4)[..., None]
        return gb[0] * o_c + gb[1] * o_s + gb[2] * o_w

    out = lax.map(block, jnp.arange(S // Q_BLOCK))
    return jnp.transpose(out, (1, 2, 3, 0, 4, 5)).reshape(B, G * HPG, S, d)

def retention_nsa_mixer(h, w_in, w_out, pos_k, w1_k, w2_k, pos_v, w1_v, w2_v):
    B, S, _ = h.shape
    proj = (h @ w_in).astype(jnp.float32)
    (rq, rk, rv, rg, nq, kc, vc, ks, vs, kw, vw, ng) = _split(proj, EVEN_SIZES)
    heads = lambda a, n: jnp.transpose(a.reshape(B, S, n, -1), (0, 2, 1, 3))
    q_r = rotary(heads(rq, RET_HEADS))
    k_r = rotary(heads(rk, RET_HEADS)) * RET_DK ** -0.5
    o_r = retention_chunkwise(q_r, k_r, heads(rv, RET_HEADS))
    mu = jnp.mean(o_r, axis=-1, keepdims=True)
    var = jnp.mean(jnp.square(o_r - mu), axis=-1, keepdims=True)
    o_r = (o_r - mu) * lax.rsqrt(var + 1e-5)
    o_r = jnp.transpose(o_r, (0, 2, 1, 3)).reshape(B, S, RET_HEADS * RET_DV) * jax.nn.silu(rg)
    q_n = jnp.transpose(nq.reshape(B, S, NSA_KV_GROUPS, NSA_HPG, NSA_HD), (0, 2, 3, 1, 4))
    kvh = lambda a: jnp.transpose(a.reshape(B, S, NSA_KV_GROUPS, NSA_HD), (0, 2, 1, 3))
    k_cmp = nsa_compress(kvh(kc), pos_k, w1_k, w2_k)
    v_cmp = nsa_compress(kvh(vc), pos_v, w1_v, w2_v)
    gates = jnp.transpose(jax.nn.sigmoid(ng).reshape(B, S, 3, NSA_KV_GROUPS, NSA_HPG), (2, 0, 3, 4, 1))
    o_n = nsa_attention(q_n, k_cmp, v_cmp, kvh(ks), kvh(vs), kvh(kw), kvh(vw), gates)
    o_n = jnp.transpose(o_n, (0, 2, 1, 3)).reshape(B, S, NSA_HEADS * NSA_HD)
    mixed = jnp.concatenate([o_r, o_n], axis=-1).astype(h.dtype)
    return mixed @ w_out

def hgrn2_chunkwise(q, k, v, log_f):
    B, H, S, dk = q.shape
    dv = v.shape[-1]
    C = min(HGRN_CHUNK, S)
    NC = S // C
    to_chunks = lambda a: jnp.moveaxis(a.reshape(B, H, NC, C, a.shape[-1]), 2, 0)
    causal = jnp.tril(jnp.ones((C, C), dtype=bool))[:, :, None]

    def step(state, xs):
        qc, kc, vc, gc = xs
        b = jnp.cumsum(gc, axis=2)
        diff = b[:, :, :, None, :] - b[:, :, None, :, :]
        decay = jnp.exp(jnp.where(causal, diff, -jnp.inf))
        attn = jnp.sum(qc[:, :, :, None, :] * decay * kc[:, :, None, :, :], axis=-1)
        o = (jnp.einsum('bhnm,bhme->bhne', attn, vc)
             + jnp.einsum('bhnd,bhde->bhne', qc * jnp.exp(b), state))
        b_last = b[:, :, -1:, :]
        new_state = (jnp.exp(b_last[:, :, 0, :])[..., None] * state
                     + jnp.einsum('bhmd,bhme->bhde', kc * jnp.exp(b_last - b), vc))
        return new_state, o

    _, o = lax.scan(step, jnp.zeros((B, H, dk, dv), jnp.float32),
                    (to_chunks(q), to_chunks(k), to_chunks(v), to_chunks(log_f)))
    return jnp.moveaxis(o, 0, 2).reshape(B, H, S, dv)

def hgrn2_mixer(h, w_in, w_out, norm_g, lb):
    B, S, _ = h.shape
    proj = (h @ w_in).astype(jnp.float32)
    qp, fp, ip, gp = _split(proj, ODD_SIZES)
    heads = lambda a: jnp.transpose(a.reshape(B, S, HGRN_HEADS, -1), (0, 2, 1, 3))
    lb = jnp.maximum(lb, 0.0)
    log_f = jnp.logaddexp(jnp.log(lb), jnp.log1p(-lb) + jax.nn.log_sigmoid(fp))
    k = (1.0 - lb) * jax.nn.sigmoid(-fp)
    q = jax.nn.silu(qp) * HGRN_DK ** -0.5
    o = hgrn2_chunkwise(heads(q), heads(k), heads(ip), heads(log_f))
    o = o * lax.rsqrt(jnp.mean(o * o, axis=-1, keepdims=True) + EPS) * norm_g.astype(jnp.float32)
    o = jnp.transpose(o, (0, 2, 1, 3)).reshape(B, S, ODD_MIX) * jax.nn.sigmoid(gp)
    return o.astype(h.dtype) @ w_out

def swiglu(h, w1, w3, w2):
    return (jax.nn.silu(h @ w1) * (h @ w3)) @ w2

def second_inputs(seed: int = 0) -> dict:
    key = jax.random.key(seed)
    ks = jax.random.split(key, 20)
    nrm = lambda k, shape, s: jax.random.normal(k, shape, jnp.float32) * s
    return {
        "x": nrm(ks[0], (BATCH, SEQ, D_MODEL), 1.0),
        "norm_mix_g": 1.0 + nrm(ks[1], (DEPTH_2, D_MODEL), 0.05),
        "norm_ffn_g": 1.0 + nrm(ks[2], (DEPTH_2, D_MODEL), 0.05),
        "final_norm_g": 1.0 + nrm(ks[3], (D_MODEL,), 0.05),
        "even_w_in": nrm(ks[4], (N_EVEN, D_MODEL, EVEN_IN), D_MODEL ** -0.5),
        "even_w_out": nrm(ks[5], (N_EVEN, EVEN_MIX, D_MODEL), EVEN_MIX ** -0.5),
        "cmp_pos_k": nrm(ks[6], (N_EVEN, CMP_BLOCK, NSA_HD), 0.1),
        "cmp_w1_k": nrm(ks[7], (N_EVEN, CMP_BLOCK * NSA_HD, NSA_HD), (CMP_BLOCK * NSA_HD) ** -0.5),
        "cmp_w2_k": nrm(ks[8], (N_EVEN, NSA_HD, NSA_HD), NSA_HD ** -0.5),
        "cmp_pos_v": nrm(ks[9], (N_EVEN, CMP_BLOCK, NSA_HD), 0.1),
        "cmp_w1_v": nrm(ks[10], (N_EVEN, CMP_BLOCK * NSA_HD, NSA_HD), (CMP_BLOCK * NSA_HD) ** -0.5),
        "cmp_w2_v": nrm(ks[11], (N_EVEN, NSA_HD, NSA_HD), NSA_HD ** -0.5),
        "odd_w_in": nrm(ks[12], (N_ODD, D_MODEL, ODD_IN), D_MODEL ** -0.5),
        "odd_w_out": nrm(ks[13], (N_ODD, ODD_MIX, D_MODEL), ODD_MIX ** -0.5),
        "hgrn_norm_g": 1.0 + nrm(ks[14], (N_ODD, HGRN_DV), 0.05),
        "hgrn_lb_logits": nrm(ks[15], (N_ODD, HGRN_HEADS * HGRN_DK), 1.0),
        "ffn_w1": nrm(ks[16], (DEPTH_2, D_MODEL, D_FF_2), D_MODEL ** -0.5),
        "ffn_w3": nrm(ks[17], (DEPTH_2, D_MODEL, D_FF_2), D_MODEL ** -0.5),
        "ffn_w2": nrm(ks[18], (DEPTH_2, D_FF_2, D_MODEL), D_FF_2 ** -0.5),
    }

def second_block(x, norm_mix_g, norm_ffn_g, final_norm_g, even_w_in, even_w_out,
              cmp_pos_k, cmp_w1_k, cmp_w2_k, cmp_pos_v, cmp_w1_v, cmp_w2_v,
              odd_w_in, odd_w_out, hgrn_norm_g, hgrn_lb_logits,
              ffn_w1, ffn_w3, ffn_w2):
    lb_sm = jax.nn.softmax(hgrn_lb_logits.astype(jnp.float32), axis=0)
    lb_all = jnp.cumsum(lb_sm, axis=0) - lb_sm[0:1]
    for layer in range(DEPTH_2):
        h = rmsnorm_2(x, norm_mix_g[layer])
        j = layer // 2
        if layer % 2 == 0:
            mix = retention_nsa_mixer(h, even_w_in[j], even_w_out[j],
                                      cmp_pos_k[j], cmp_w1_k[j], cmp_w2_k[j],
                                      cmp_pos_v[j], cmp_w1_v[j], cmp_w2_v[j])
        else:
            mix = hgrn2_mixer(h, odd_w_in[j], odd_w_out[j], hgrn_norm_g[j], lb_all[j])
        x = x + mix.astype(x.dtype)
        h = rmsnorm_2(x, norm_ffn_g[layer])
        x = x + swiglu(h, ffn_w1[layer], ffn_w3[layer], ffn_w2[layer]).astype(x.dtype)
    return rmsnorm_2(x, final_norm_g)


def setup_inputs(seed=0):
    out = dict(first_inputs(seed))
    for name, value in second_inputs(seed + 1).items():
        if name != "x":
            out[name + "_2"] = value
    return out


def reference(
    x, mem, positions, g_mix_pre, w_in, lambda_q1, lambda_k1, lambda_q2, lambda_k2, g_subln,
    w_pool, pool_scale, w_out, g_mix_post, g_x_pre, g_mem, w_xq, w_xkv, w_xo, g_x_post,
    g_ffn_pre, w_gate, w_up, w_down, g_ffn_post, norm_mix_g_2, norm_ffn_g_2, final_norm_g_2,
    even_w_in_2, even_w_out_2, cmp_pos_k_2, cmp_w1_k_2, cmp_w2_k_2, cmp_pos_v_2, cmp_w1_v_2,
    cmp_w2_v_2, odd_w_in_2, odd_w_out_2, hgrn_norm_g_2, hgrn_lb_logits_2, ffn_w1_2, ffn_w3_2,
    ffn_w2_2,
):
    x = first_block(
        x, mem, positions, g_mix_pre, w_in, lambda_q1, lambda_k1, lambda_q2, lambda_k2, g_subln,
        w_pool, pool_scale, w_out, g_mix_post, g_x_pre, g_mem, w_xq, w_xkv, w_xo, g_x_post,
        g_ffn_pre, w_gate, w_up, w_down, g_ffn_post,
    )
    return second_block(
        x, norm_mix_g_2, norm_ffn_g_2, final_norm_g_2, even_w_in_2, even_w_out_2, cmp_pos_k_2,
        cmp_w1_k_2, cmp_w2_k_2, cmp_pos_v_2, cmp_w1_v_2, cmp_w2_v_2, odd_w_in_2, odd_w_out_2,
        hgrn_norm_g_2, hgrn_lb_logits_2, ffn_w1_2, ffn_w3_2, ffn_w2_2,
    )


_drawn_inputs = setup_inputs


def setup_inputs(seed=0):
    import zlib

    import numpy as np

    out = dict(_drawn_inputs(seed))
    spreads = {}
    factors = {'lambda_k1': 2.851,
     'lambda_q2': 3.004,
     'g_subln': 4.361,
     'g_mix_post': 3.166,
     'g_x_pre': 3.662,
     'g_x_post': 11.748,
     'g_ffn_pre': 9.649,
     'g_ffn_post': 20.283,
     'cmp_pos_k_2': 33.501,
     'cmp_w1_k_2': 3.064,
     'cmp_w2_k_2': 2.983,
     'cmp_pos_v_2': 18.45,
     'hgrn_norm_g_2': 67.453,
     'norm_mix_g_2': 2.974,
     'norm_ffn_g_2': 7.033}
    for name, (base, spread) in spreads.items():
        noise = np.random.default_rng([zlib.crc32(name.encode()), seed]).standard_normal(out[name].shape)
        drawn = base * np.exp(spread * noise) if base else spread * noise
        out[name] = __import__('jax').numpy.asarray(drawn.astype(out[name].dtype))
    for name, factor in factors.items():
        out[name] = (out[name] * factor).astype(out[name].dtype)
    return out
```

```python
import math
from contextlib import ExitStack

import numpy as np
import concourse.bass as bass
from concourse import mybir

ALU = mybir.AluOpType
ACT = mybir.ActivationFunctionType
AX = mybir.AxisListType.X
F32 = mybir.dt.float32
F32R = mybir.dt.float32r
I32 = mybir.dt.int32

P = 128
D = 1024
S = 256
NT = S // P
KT = D // P
EPS = 1e-6
NEG = -1.0e30
BIG_NEG = -3.0e38
FF = 2816
FT = FF // P
UNIT = 2048
RING = 4
HEADS_DA, HEADS_X, HEADS_RET, HEADS_NSA, HEADS_HG = 4, 4, 4, 8, 8
LAM_INIT = 0.8 - 0.6 * math.exp(-0.3 * 0)
NCMP = S // 16 - 1
POOL_WINDOWS = (2, 4, 8, 16)
LEVELS = (1, 2, 4, 8, 16, 32, 64)
DK_HG = 128

GU, DN = 2 * (FF // 256), FF // 256
PHASES = [("in", 8), ("kv", 8), ("out", 4), ("xq", 4), ("xo", 4), ("gu0", GU), ("dn0", DN),
          ("ev", 14), ("eo", 4), ("gu1", GU), ("dn1", DN), ("od", 16), ("oo", 4),
          ("gu2", GU), ("dn2", DN)]
BASE = {}
N_UNITS = 0
for _name, _n in PHASES:
    BASE[_name] = N_UNITS
    N_UNITS += _n
NG_UNIT = BASE["ev"] + 13
NG_COLS = 3 * HEADS_NSA

POWS = ["x0", "mem", "subln", "p_mix", "x1", "p_x", "x2", "p_ffn", "e0", "gn", "f0", "o0", "hg", "f1",
        "fin"]
POW_N = {n: 2 for n in POWS} | {"subln": 8, "gn": 8, "hg": 16}

CONST = {}
_at = 0
for _name, _n in [("ident", 128), ("zeros", 128), ("causal", 128), ("cmpmask", NT * NCMP), ("cmpvalid", NT),
                  ("rot64", 128), ("rot128", 128), ("invfreq", 1), ("half", 16)]:
    CONST[_name] = (_at, _n)
    _at += _n
N_CONST = _at
GAIN = {}
_at = 0
for _name, _n in [("g_mix_pre", KT), ("g_x_pre", KT), ("g_mem", KT), ("g_ffn_pre", KT), ("mix0", KT),
                  ("mix1", KT), ("ffn0", KT), ("ffn1", KT), ("g_subln", 1), ("hgrn", 1), ("pool_scale", 4),
                  ("lam", 256)]:
    GAIN[_name] = (_at, _n)
    _at += _n
N_GAIN = _at


def bank_reads(u):
    n = [0, 0]
    at = 0
    for name, count in PHASES:
        if not name.startswith(("gu", "dn")):
            for j in range(min(max(u - at, 0), count)):
                n[j % 2] += 1
        at += count
    return n


def build(nc, stream, x_in, mem_in, pos_in, gains_in, rows_in, consts_in, poolm_in, wpool_in, retm_in,
          hgm_in, cmpw_in, cmps_in, out):
    ctx = ExitStack()
    sems = {}

    def sem(name):
        if name not in sems:
            sems[name] = ctx.enter_context(nc.semaphore(name))
        return sems[name]

    def sb(stack, name, shape, dt=F32):
        return stack.enter_context(nc.sbuf_tensor("s_" + name, shape, dt))

    with ctx:
        raw = sb(ctx, "raw", [P, RING, UNIT])
        whi = sb(ctx, "whi", [P, RING, UNIT], F32R)
        wlo = sb(ctx, "wlo", [P, RING, UNIT], F32R)
        xn = sb(ctx, "xn", [P, NT, D])
        y = sb(ctx, "y", [P, NT, D])
        xTh = sb(ctx, "xTh", [P, KT, S], F32R)
        xTl = sb(ctx, "xTl", [P, KT, S], F32R)
        cst = sb(ctx, "cst", [P, N_CONST])
        gains = sb(ctx, "gains", [P, N_GAIN])
        gb = sb(ctx, "gb", [P, D])
        ms = sb(ctx, "ms", [P, len(POWS), 16])
        rstd = sb(ctx, "rstd", [P, len(POWS), 16])
        ss = sb(ctx, "ss", [P, 64])
        small = sb(ctx, "small", [P, 64])
        junk = sb(ctx, "junk", [P, 512])

        def const(name):
            a, n = CONST[name]
            return cst[:, a:a + n]

        def gain(name, k=0):
            a, _ = GAIN[name]
            return gains[:, a + k:a + k + 1]

        ident = const("ident")
        mask_full = cst[:, CONST["zeros"][0]:CONST["zeros"][0] + 256]

        a_ = ExitStack()
        memTh = sb(a_, "memTh", [P, KT, S], F32R)
        memTl = sb(a_, "memTl", [P, KT, S], F32R)
        kxT = sb(a_, "kxT", [P, KT, S])
        vx = sb(a_, "vx", [P, NT, D])
        a2 = ExitStack()
        qT = sb(a2, "qT", [P, 4, S])
        kT = sb(a2, "kT", [P, 4, S])
        vn = sb(a2, "vn", [P, NT, 512])
        un = sb(a2, "un", [P, NT, 512])
        cosT = sb(a2, "cosT", [P, S])
        sinT = sb(a2, "sinT", [P, S])
        qraw = sb(a2, "qraw", [P, 2, 512])
        sm = sb(a2, "sm", [P, 2, 2, S])
        aT = sb(a2, "aT", [P, 2, 256])
        poolm = sb(a2, "poolm", [P, 4, 3 * P])
        wpool = aT[:].rearrange("p a (b n) -> p (a b) n", n=P)
        posi = sb(a2, "posi", [P, S], I32)
        a2.close()
        a3 = ExitStack()
        xqT = sb(a3, "xqT", [P, KT, S])
        px = sb(a3, "px", [P, 2, 2, S])
        pxT = sb(a3, "pxT", [P, 2, 2, S])
        a3.close()
        a_.close()
        f_ = ExitStack()
        hTh = sb(f_, "hTh", [P, FT, S], F32R)
        hTl = sb(f_, "hTl", [P, FT, S], F32R)
        sg = sb(f_, "sg", [P, 2, 512])
        hb = sb(f_, "hb", [P, 2, 512])
        f_.close()
        b_ = ExitStack()
        rqT = sb(b_, "rqT", [P, 4, S])
        rkT = sb(b_, "rkT", [P, 4, S])
        rv = sb(b_, "rv", [P, NT, 512])
        rg = sb(b_, "rg", [P, NT, 512])
        nqT = sb(b_, "nqT", [P, 4, S])
        kcT = sb(b_, "kcT", [P, 2, S])
        ksT = sb(b_, "ksT", [P, 2, 2, S])
        vsw = sb(b_, "vsw", [P, NT, 256])
        gat = sb(b_, "gat", [P, NT, NG_COLS])
        cmps = sb(b_, "cmps", [P, 64 + 128])
        hid = sb(b_, "hid", [64, 2, 2, 16])
        kcm = sb(b_, "kcm", [P, 2, 16])
        vcm = sb(b_, "vcm", [16, 2, 64])
        pc = sb(b_, "pc", [P, HEADS_NSA * NT, NCMP])
        braw = sb(b_, "braw", [P, 2, 512])
        rcos = sb(b_, "rcos", [P, S])
        rsin = sb(b_, "rsin", [P, S])
        retd = sb(b_, "retd", [P, 4, 384])
        on = sb(b_, "on", [P, NT * 4, P])
        rp = sb(b_, "rp", [P, 2, 384])
        b2 = ExitStack()
        w1 = sb(b2, "w1", [P, 2, 32, 64])
        blk = y[:].rearrange("p t n -> p (t n)")[:, 0:2 * NCMP * 32].rearrange("p (k n j) -> p k n j", k=2, j=32)
        b2.close()
        b4 = ExitStack()
        nsm = sb(b4, "nsm", [P, 2, 2, S])
        npT = sb(b4, "npT", [P, 2, 2, 384])
        pcT = y[0:16, :, :].rearrange("p t (k n) -> p (t k) n", n=P)
        b4.close()
        osq = braw[:].rearrange("p a (b n) -> p (a b) n", n=P)
        b_.close()
        c_ = ExitStack()
        qd = sb(c_, "qd", [P, 8, S])
        kd = sb(c_, "kd", [P, 8, S])
        fT = sb(c_, "fT", [P, 8 * S])
        tot = sb(c_, "tot", [P, 8 * S // 2 + 8 * S // 4])
        vh = sb(c_, "vh", [P, NT, D])
        gh = sb(c_, "gh", [P, NT, D])
        hgm = sb(c_, "hgm", [P, 8, P], I32)
        at = sb(c_, "at", [P, 8, 3, P])
        oh = qd[:].rearrange("p (t a) (b n) -> p t (a b) n", t=NT, n=P)
        c_.close()

        G = [ctx.enter_context(nc.psum_tensor(f"G{i}", [P, 512], F32)) for i in range(2)]
        DB = [ctx.enter_context(nc.psum_tensor(f"D{i}", [P, 512], F32)) for i in range(4)]
        TB = [ctx.enter_context(nc.psum_tensor(f"T{i}", [P, 512], F32)) for i in range(2)]

        hi_ready, lo_ready, unit_done = sem("hi_ready"), sem("lo_ready"), sem("unit_done")
        landed = [sem(f"raw_landed{i}") for i in range(RING)]
        bank_read = [sem("bank_read0"), sem("bank_read1")]
        ms_ready, rstd_ready, x_ready = sem("ms_ready"), sem("rstd_ready"), sem("x_ready")
        NORMS = [("g_mix_pre", "x0", None), ("g_mem", "mem", None), ("g_x_pre", "x1", 1),
                 ("g_ffn_pre", "x2", 2), ("mix0", "e0", 3), ("ffn0", "f0", 4), ("mix1", "o0", 5),
                 ("ffn1", "f1", 6)]

        def halves(ap):
            return ap.rearrange("p (a b) -> p a b", a=2)

        def same_rows(ap, n):
            return ap.rearrange("p (a b) -> p a b", a=1).broadcast_to([P, n, ap.shape[-1]])

        def same_cols(ap, n):
            return ap.rearrange("p (a b) -> p a b", b=1).broadcast_to([P, ap.shape[-1], n])

        def bank(u):
            base = max(b for b in BASE.values() if b <= u)
            return (u - base) % 2

        def pow_at(name):
            return POWS.index(name)

        block = ctx.enter_context(nc.Block())

        @block.sync
        def _(sp):
            sp.dma_start(xn[:], x_in.rearrange("(t p) d -> p t d", p=P)).then_inc(sem("x_in"), 16)
            for j in range(RING):
                sp.dma_start(raw[:, j, :], stream[j, :, :]).then_inc(landed[j], 16)
            with sp.Fori(1, N_UNITS // RING) as i:
                for j in range(RING):
                    sp.wait_ge(lo_ready, i * RING + (j - RING + 1))
                    sp.dma_start(raw[:, j, :], stream[bass.ds(i * RING + j, 1), :, :]
                                 .rearrange("a p n -> p (a n)")).then_inc(landed[j], 16)
            for u in range(N_UNITS // RING * RING, N_UNITS):
                sp.wait_ge(lo_ready, u - RING + 1)
                sp.dma_start(raw[:, u % RING, :], stream[u, :, :]).then_inc(landed[u % RING], 16)
            for t in range(NT):
                sp.wait_ge(sem("out_ready"), t + 1)
                sp.dma_start(out[t * P:(t + 1) * P, :], y[:, t, :]).then_inc(sem("stored"), 16)
            sp.wait_ge(sem("stored"), 16 * NT)

        @block.gpsimd
        def _(pool):
            pool.dma_start(cst[:], consts_in).then_inc(sem("cst_in"), 16)
            pool.dma_start(gains[:], gains_in).then_inc(sem("gains_in"), 16)
            pool.dma_start(posi[:], pos_in.partition_broadcast(P)).then_inc(sem("pos_in"), 16)
            pool.dma_start(gb[:], rows_in[0, :].partition_broadcast(P)).then_inc(sem("gb_in"), 16)
            pool.wait_ge(sem("cst_in"), 16)

            def power(name):
                k, n = pow_at(name), POW_N[name]
                pool.wait_ge(ms_ready, k + 1)
                nc.gpsimd.tensor_tensor(rstd[:, k, 0:n], ms[:, k, 0:n], const("half")[:, 0:n],
                                        ALU.pow).then_inc(rstd_ready, 1)

            def load_row(r, version):
                pool.wait_ge(x_ready, version)
                pool.dma_start(gb[:], rows_in[r, :].partition_broadcast(P)).then_inc(sem("gb_in"), 16)

            power("x0")
            pool.wait_ge(sem("norm_tr"), 4)
            pool.dma_start(y[:], mem_in.rearrange("(t p) d -> p t d", p=P)).then_inc(sem("mem_in"), 16)
            pool.dma_start(poolm[:], poolm_in).then_inc(sem("poolm_in"), 16)
            pool.dma_start(wpool, wpool_in).then_inc(sem("wpool_in"), 16)
            power("mem")
            power("subln")
            power("p_mix")
            load_row(1, 1)
            power("x1")
            power("p_x")
            load_row(2, 2)
            power("x2")
            power("p_ffn")
            load_row(3, 3)
            pool.dma_start(rcos[:], retm_in[:, 0:S]).then_inc(sem("rcos_in"), 16)
            pool.dma_start(rsin[:], retm_in[:, S:2 * S]).then_inc(sem("rsin_in"), 16)
            pool.dma_start(retd[:], retm_in[:, 2 * S:].rearrange("p (h n) -> p h n", h=4))\
                .then_inc(sem("retd_in"), 16)
            pool.dma_start(w1[:], cmpw_in).then_inc(sem("w1_in"), 16)
            pool.dma_start(cmps[:], cmps_in).then_inc(sem("cmps_in"), 16)
            power("e0")
            power("gn")
            power("f0")
            pool.wait_ge(x_ready, 5)
            pool.dma_start(hgm[:], hgm_in).then_inc(sem("hgm_in"), 16)
            power("o0")
            power("hg")
            power("f1")
            power("fin")

        @block.scalar
        def _(act):
            def split(u, i=None):
                if u >= N_UNITS:
                    return
                k = 0 if i is None else i
                act.wait_ge(landed[u % RING], k * 16 + 16 * (u // RING + 1))
                if u >= RING:
                    act.wait_ge(unit_done, k * RING + (u - RING + 1))
                n = KT * NG_COLS if u == NG_UNIT else UNIT
                nc.scalar.activation(whi[:, u % RING, 0:n], raw[:, u % RING, 0:n], ACT.Copy)\
                    .then_inc(hi_ready, 1)

            def norm_square(n, src, scratch):
                nc.scalar.activation(scratch, src[:, 0, :], ACT.Square, accum_out=ss[:, 2 * n:2 * n + 1])\
                    .then_inc(sem("norm_sq"), 1)

            def norm_hi(n, dst):
                for kt in range(KT):
                    if kt % 2 == 0:
                        act.wait_ge(sem("norm_tr"), 4 * n + kt // 2 + 1)
                    nc.scalar.activation(dst[:, kt, :], halves(DB[kt // 2][:])[:, kt % 2, :], ACT.Copy,
                                         scale=gain(NORMS[n][0], kt)).then_inc(sem("norm_hi"), 1)

            def norm(n):
                act.wait_ge(x_ready, NORMS[n][2])
                norm_square(n, xn, y[:, 0, :])
                norm_hi(n, xTh)

            def evac(u, dst, func=ACT.Copy, scale=1.0):
                act.wait_ge(unit_done, u + 1)
                nc.scalar.activation(dst, halves(G[bank(u)][:]), func, scale=scale)\
                    .then_inc(bank_read[bank(u)], 1)

            def rope_raw(j, u, buf, which):
                act.wait_ge(unit_done, u + 1)
                if j >= 2:
                    act.wait_ge(sem("rope_done" + which), j - 1)
                nc.scalar.activation(buf[:, j % 2, :], G[bank(u)][:], ACT.Copy)\
                    .then_inc(sem("rope_raw" + which), 1)

            def post_squares(u0, k0):
                for j in range(4):
                    act.wait_ge(unit_done, u0 + j + 1)
                    if 4 * k0 + j >= 1:
                        act.wait_ge(sem("post_sq"), 4 * k0 + j)
                    for t in range(NT):
                        ins = nc.scalar.activation(junk[:, 256 * t:256 * t + 256], halves(G[bank(u0 + j)][:])[:, t, :],
                                                   ACT.Square, accum_out=ss[:, 16 + 4 * t + j:17 + 4 * t + j])
                    ins.then_inc(sem("post_sq"), 1)
                    split(u0 + j + RING)

            def mlp(f):
                u0, p0 = BASE[f"gu{f}"], f * (GU // 2)

                def pair(q, i=None):
                    k = 0 if i is None else i
                    act.wait_ge(unit_done, k * 4 + (u0 + 2 * q + 1))
                    if i is not None or p0 + q >= 2:
                        act.wait_ge(sem("h_made"), k * 2 + (p0 + q - 1))
                    nc.scalar.activation(sg[:, q % 2, :], G[0][:], ACT.Silu).then_inc(sem("silu_made"), 1)
                    split(u0 + 2 * q + RING, i)
                    split(u0 + 2 * q + 1 + RING, i)
                    act.wait_ge(sem("h_made"), k * 2 + (p0 + q + 1))
                    dst = hTh[:, 2 * q:2 * q + 2, :] if i is None else hTh[:, bass.ds(i * 4 + 2 * q, 2), :]
                    nc.scalar.activation(dst, halves(hb[:, q % 2, :]), ACT.Copy).then_inc(sem("h_hi"), 1)

                for q in range(2):
                    pair(q)
                with act.Fori(1, GU // 4) as i:
                    for q in range(2):
                        pair(q, i)
                for q in range(GU // 4 * 2, GU // 2):
                    pair(q)
                for d in range(DN):
                    split(BASE[f"dn{f}"] + d + RING)

            act.wait_ge(sem("x_in"), 16)
            norm_square(0, xn, y[:, 0, :])
            split(0)
            split(1)
            act.wait_ge(sem("gains_in"), 16)
            norm_hi(0, xTh)
            split(2)
            split(3)
            act.wait_ge(sem("angles"), 2)
            nc.scalar.activation(sinT[:], sinT[:], ACT.Sin).then_inc(sem("trig"), 1)
            nc.scalar.activation(cosT[:], cosT[:], ACT.Sin).then_inc(sem("trig"), 1)
            u0 = BASE["in"]
            for j in range(4):
                rope_raw(j, u0 + j, qraw, "_a")
                split(u0 + j + RING)
                if j == 1:
                    act.wait_ge(sem("mem_in"), 16)
                    norm_square(1, y, sm[:].rearrange("p a b n -> p (a b n)"))
            norm_hi(1, memTh)
            for j in range(2):
                evac(u0 + 4 + j, vn[:, :, 256 * j:256 * j + 256])
                split(u0 + 4 + j + RING)
            for j in range(2):
                evac(u0 + 6 + j, un[:, :, 256 * j:256 * j + 256])
                if j == 0:
                    split(u0 + 6 + RING)
            act.wait_ge(sem("rope_done_a"), 4)
            for gp in range(2):
                act.wait_ge(sem("pooled"), gp + 1)
                nc.scalar.activation(qraw[:, gp, :], DB[gp][:], ACT.Copy).then_inc(sem("pooled_out"), 1)
            for g in range(4):
                if g % 2 == 0:
                    act.wait_ge(sem("pool_mix"), g // 2 + 1)
                nc.scalar.activation(xTh[:, 4 + g, :], halves(DB[2 + g // 2][:])[:, g % 2, :], ACT.Copy,
                                     scale=gain("pool_scale", g)).then_inc(sem("pool_hi"), 1)
            split(u0 + 7 + RING)
            act.wait_ge(sem("lam_dots"), 1)
            nc.scalar.activation(small[:, 2:4], small[:, 0:2], ACT.Exp).then_inc(sem("lam_exp"), 1)

            def exps(s):
                kend = P * (s % 2 + 1)
                act.wait_ge(sem("da_max"), s + 1)
                for m in range(2):
                    ins = nc.scalar.activation(sm[:, s % 2, m, 0:kend], sm[:, s % 2, m, 0:kend], ACT.Exp,
                                               bias=small[:, 8 + 2 * (s % 2) + m:9 + 2 * (s % 2) + m],
                                               scale=0.125,
                                               accum_out=small[:, 12 + 2 * (s % 2) + m:13 + 2 * (s % 2) + m])
                ins.then_inc(sem("da_exp"), 1)

            kv0 = BASE["kv"]
            exps(0)
            for s in range(8):
                if s < 4:
                    evac(kv0 + s, kxT[:, 2 * s:2 * s + 2, :])
                else:
                    evac(kv0 + s, vx[:, :, 256 * (s - 4):256 * (s - 3)])
                act.wait_ge(sem("da_tr"), s + 1)
                if s >= 2:
                    act.wait_ge(sem("da_out"), s - 1)
                n = P * (s % 2 + 1)
                nc.scalar.activation(aT[:, s % 2, 0:n], TB[s % 2][:, 0:n], ACT.Copy).then_inc(sem("aT"), 1)
                if s < 7:
                    exps(s + 1)
                split(kv0 + s + RING)
            act.wait_ge(sem("da_nat"), 8)
            nc.scalar.activation(sm[:].rearrange("p a b n -> p (a b n)"), un[:].rearrange("p t n -> p (t n)"),
                                 ACT.Square).then_inc(sem("da_sq"), 1)
            for hp in range(2):
                act.wait_ge(sem("da_T"), hp + 1)
                nc.scalar.activation(xTh[:, 2 * hp:2 * hp + 2, :], halves(DB[hp][:]), ACT.Copy,
                                     scale=small[:, 20:21]).then_inc(sem("da_hi"), 1)
            post_squares(BASE["out"], 0)

            norm(2)
            u0 = BASE["xq"]

            def x_exp(h):
                act.wait_ge(sem("x_max"), h + 1)
                for t in range(NT):
                    ins = nc.scalar.activation(px[:, h % 2, t, :], halves(DB[h % 2][:])[:, t, :], ACT.Exp,
                                               bias=small[:, 24 + 2 * (h % 2) + t:25 + 2 * (h % 2) + t],
                                               scale=0.0625,
                                               accum_out=small[:, 28 + 2 * (h % 2) + t:29 + 2 * (h % 2) + t])
                ins.then_inc(sem("x_exp"), 1)

            def x_T(h):
                act.wait_ge(sem("x_tr"), h + 1)
                if h >= 2:
                    act.wait_ge(sem("x_out"), h - 1)
                nc.scalar.activation(pxT[:, h % 2, :, :], halves(TB[h % 2][:]), ACT.Copy)\
                    .then_inc(sem("x_pT"), 1)

            def x_hi(h):
                act.wait_ge(sem("x_out"), h + 1)
                nc.scalar.activation(xTh[:, 2 * h:2 * h + 2, :], halves(DB[2 + h % 2][:]), ACT.Copy)\
                    .then_inc(sem("x_hi"), 1)

            evac(u0, xqT[:, 0:2, :])
            split(u0 + RING)
            evac(u0 + 1, xqT[:, 2:4, :])
            split(u0 + 1 + RING)
            x_exp(0)
            evac(u0 + 2, xqT[:, 4:6, :])
            split(u0 + 2 + RING)
            x_exp(1)
            x_T(0)
            evac(u0 + 3, xqT[:, 6:8, :])
            split(u0 + 3 + RING)
            x_exp(2)
            x_T(1)
            x_hi(0)
            x_exp(3)
            x_T(2)
            x_hi(1)
            x_T(3)
            x_hi(2)
            x_hi(3)
            post_squares(BASE["xo"], 1)

            norm(3)
            mlp(0)
            act.wait_ge(unit_done, BASE["dn0"] + DN)
            for t in range(NT):
                for nh in range(2):
                    ins = nc.scalar.activation((sg, hb)[t][:, nh, :], DB[2 * t + nh][:], ACT.Square,
                                               accum_out=ss[:, 16 + 4 * t + nh:17 + 4 * t + nh])
            ins.then_inc(sem("post_sq"), 1)

            norm(4)
            u0 = BASE["ev"]
            for j in range(4):
                rope_raw(j, u0 + j, braw, "_b")
                split(u0 + j + RING)
            for j in range(2):
                evac(u0 + 4 + j, rv[:, :, 256 * j:256 * j + 256])
                split(u0 + 4 + j + RING)
            for j in range(2):
                evac(u0 + 6 + j, rg[:, :, 256 * j:256 * j + 256], ACT.Silu)
                split(u0 + 6 + j + RING)
            for j in range(2):
                evac(u0 + 8 + j, nqT[:, 2 * j:2 * j + 2, :])
                split(u0 + 8 + j + RING)
            evac(u0 + 10, kcT[:])
            split(u0 + 10 + RING)
            act.wait_ge(unit_done, u0 + 12)
            for half in range(2):
                for g in range(2):
                    ins = nc.scalar.activation(ksT[64 * half:64 * half + 64, :, g, :],
                                               halves(G[bank(u0 + 11)][64 * g:64 * g + 64, :]), ACT.Copy)
            ins.then_inc(bank_read[bank(u0 + 11)], 1)
            split(u0 + 11 + RING)
            evac(u0 + 12, vsw[:])
            split(u0 + 12 + RING)
            act.wait_ge(unit_done, u0 + 14)
            nc.scalar.activation(gat[:], halves(G[bank(u0 + 13)][:])[:, :, 0:NG_COLS], ACT.Sigmoid)\
                .then_inc(bank_read[bank(u0 + 13)], 1)
            split(u0 + 13 + RING)
            act.wait_ge(sem("gn_centred"), 1)
            nc.scalar.activation(osq, on[:], ACT.Square).then_inc(sem("gn_sq"), 1)
            act.wait_ge(sem("cmp_hid"), 1)
            for g in range(2):
                ins = nc.scalar.activation(hid[0:64, :, g, 0:NCMP],
                                           TB[g][0:64, 0:32].rearrange("p (k n) -> p k n", k=2)[:, :, 0:NCMP],
                                           ACT.Gelu_apprx_tanh)
            ins.then_inc(sem("cmp_gelu"), 1)
            for hp in range(2):
                act.wait_ge(sem("ret_T"), hp + 1)
                nc.scalar.activation(xTh[:, 2 * hp:2 * hp + 2, :], halves(DB[hp][:]), ACT.Copy)\
                    .then_inc(sem("ret_hi"), 1)
            act.wait_ge(sem("cmp_shift"), 1)
            nc.scalar.activation(pc[:], pc[:], ACT.Exp, scale=0.125).then_inc(sem("cmp_exp"), 1)

            def n_exp(s):
                t = s % 2
                kend = P * (t + 1)
                act.wait_ge(sem("n_max"), s + 1)
                for br in range(2):
                    ins = nc.scalar.activation(nsm[:, t, br, 0:kend], nsm[:, t, br, 0:kend], ACT.Exp,
                                               bias=small[:, 34 + 4 * t + br:35 + 4 * t + br], scale=0.125,
                                               accum_out=small[:, 44 + 4 * t + br:45 + 4 * t + br])
                ins.then_inc(sem("n_exp"), 1)

            def n_hi(hp):
                act.wait_ge(sem("n_out"), 2 * hp + 2)
                nc.scalar.activation(xTh[:, 4 + hp, :], DB[2 + hp % 2][:, 0:S], ACT.Copy)\
                    .then_inc(sem("n_hi"), 1)

            n_exp(0)
            for b in range(2):
                act.wait_ge(sem("cmp_tr"), b + 1)
                nc.scalar.activation(pcT[0:NCMP, 4 * b:4 * b + 4, :],
                                     DB[2 + b][0:NCMP, :].rearrange("p (k n) -> p k n", k=4), ACT.Copy)\
                    .then_inc(sem("pcT_a"), 1)
            for s in range(16):
                h = s // 2
                if s < 15:
                    n_exp(s + 1)
                if s % 2 == 1:
                    act.wait_ge(sem("n_tr"), s + 1)
                    if h >= 2:
                        act.wait_ge(sem("n_out"), h - 1)
                    nc.scalar.activation(npT[:, h % 2, 0, :], TB[0][:, 0:384], ACT.Copy)\
                        .then_inc(sem("npT_a"), 1)
                if s % 4 == 0 and s >= 4:
                    n_hi(s // 4 - 1)
            n_hi(3)
            u0 = BASE["eo"]
            for j in range(4):
                split(u0 + j + RING)

            norm(5)
            mlp(1)

            norm(6)
            u0 = BASE["od"]
            for j in range(4):
                evac(u0 + j, qd[:, 2 * j:2 * j + 2, :], ACT.Silu)
                split(u0 + j + RING)
            for j in range(4):
                u = u0 + 4 + j
                act.wait_ge(unit_done, u + 1)
                nc.scalar.activation(fT[:, 512 * j:512 * j + 512], G[bank(u)][:], ACT.Sigmoid)\
                    .then_inc(sem("f_made"), 1)
                evac(u, kd[:, 2 * j:2 * j + 2, :], ACT.Sigmoid, scale=-1.0)
                split(u + RING)
            for j in range(4):
                evac(u0 + 8 + j, vh[:, :, 256 * j:256 * j + 256], ACT.Copy, scale=DK_HG ** -0.5)
                split(u0 + 8 + j + RING)
            for j in range(4):
                evac(u0 + 12 + j, gh[:, :, 256 * j:256 * j + 256], ACT.Sigmoid)
                split(u0 + 12 + j + RING)
            for b in range(4):
                act.wait_ge(sem("hg_out"), b + 1)
                nc.scalar.activation(kd[:, 2 * b:2 * b + 2, :], halves(DB[b][:]), ACT.Square)\
                    .then_inc(sem("hg_sq"), 1)
            for b in range(4):
                act.wait_ge(sem("hg_T"), b + 1)
                nc.scalar.activation(xTh[:, 2 * b:2 * b + 2, :], halves(DB[b][:]), ACT.Copy,
                                     scale=gain("hgrn")).then_inc(sem("hg_hi"), 1)
            u0 = BASE["oo"]
            for j in range(4):
                split(u0 + j + RING)

            norm(7)
            mlp(2)
            act.wait_ge(x_ready, 7)
            norm_square(8, xn, y[:, 0, :])

        @block.vector
        def _(dve):
            chain = [0]

            def link(ins):
                chain[0] += 1
                ins.then_inc(sem("dve_chain"), 1)
                dve.wait_ge(sem("dve_chain"), chain[0])

            def split(u, i=None):
                if u >= N_UNITS:
                    return
                k = 0 if i is None else i
                dve.wait_ge(hi_ready, k * RING + (u + 1))
                n = KT * NG_COLS if u == NG_UNIT else UNIT
                nc.vector.tensor_tensor(wlo[:, u % RING, 0:n], raw[:, u % RING, 0:n],
                                        whi[:, u % RING, 0:n], ALU.subtract).then_inc(lo_ready, 1)

            def mean_square(k, sums, count, eps=EPS):
                nc.vector.tensor_scalar(ms[:, k, 0:sums.shape[-1]], sums, 1.0 / count, eps, ALU.mult, ALU.add)\
                    .then_inc(ms_ready, 1)

            def norm_stats(n, name, src, scratch):
                link(nc.vector.tensor_tensor_reduce(scratch, src[:, 1, :], src[:, 1, :], 1.0, 0.0,
                                                    ALU.mult, ALU.add, ss[:, 2 * n + 1:2 * n + 2]))
                dve.wait_ge(sem("norm_sq"), n + 1)
                mean_square(pow_at(name), ss[:, 2 * n:2 * n + 2], D)

            def norm_scale(name, src):
                k = pow_at(name)
                dve.wait_ge(rstd_ready, k + 1)
                for t in range(NT):
                    nc.vector.tensor_scalar(y[:, t, :], src[:, t, :], rstd[:, k, t:t + 1], None, ALU.mult)\
                        .then_inc(sem("rows_scaled"), 1)

            def norm_lo(n, dst_h, dst_l):
                for kt in range(KT):
                    if kt % 2 == 0:
                        dve.wait_ge(sem("norm_hi"), KT * n + kt + 2)
                    nc.vector.scalar_tensor_tensor(
                        dst_l[:, kt, :], halves(DB[kt // 2][:])[:, kt % 2, :], gain(NORMS[n][0], kt),
                        dst_h[:, kt, :], ALU.mult, ALU.subtract).then_inc(sem("xT_ready"), 1)

            def norm(n):
                _, name, version = NORMS[n]
                dve.wait_ge(x_ready, version)
                norm_stats(n, name, xn, y[:, 1, :])
                norm_scale(name, xn)
                norm_lo(n, xTh, xTl)

            def rope_turn(j, dst, buf, which):
                dve.wait_ge(sem("rope_rot" + which), j + 1)
                sin = sinT if which == "_a" else rsin
                link(nc.vector.tensor_tensor(halves(buf[:, j % 2, :]), halves(TB[j % 2][:]),
                                             same_rows(sin[:], 2), ALU.mult))
                nc.vector.tensor_tensor(dst, dst, halves(buf[:, j % 2, :]), ALU.add)\
                    .then_inc(sem("rope_done" + which), 1)

            def rope_cos(j, u, dst, which):
                dve.wait_ge(sem("rope_raw" + which), j + 1)
                cos = cosT if which == "_a" else rcos
                nc.vector.tensor_tensor(dst, halves(G[bank(u)][:]), same_rows(cos[:], 2), ALU.mult)\
                    .then_inc(bank_read[bank(u)], 1)

            def post_norm(k0, u0, name, version):
                dve.wait_ge(sem("gb_in"), 16 * (k0 + 1))
                for j in range(4):
                    dve.wait_ge(sem("post_sq"), 4 * k0 + j + 1)
                    nc.vector.tensor_tensor(y[:, :, 256 * j:256 * j + 256], halves(G[bank(u0 + j)][:]),
                                            same_rows(gb[:, 256 * j:256 * j + 256], 2), ALU.mult)\
                        .then_inc(bank_read[bank(u0 + j)], 1)
                    split(u0 + j + RING)
                finish_post(name, 4)

            def finish_post(name, parts):
                link(nc.vector.reduce_sum(ss[:, 24:26], ss[:, 16:24].rearrange("p (t j) -> p t j", t=2)
                                          [:, :, 0:parts], AX))
                mean_square(pow_at(name), ss[:, 24:26], D)
                dve.wait_ge(rstd_ready, pow_at(name) + 1)
                for t in range(NT):
                    ins = nc.vector.scalar_tensor_tensor(xn[:, t, :], y[:, t, :],
                                                         rstd[:, pow_at(name), t:t + 1],
                                                         xn[:, t, :], ALU.mult, ALU.add)
                ins.then_inc(x_ready, 1)

            def mlp(f):
                u0, p0 = BASE[f"gu{f}"], f * (GU // 2)

                def pair(q, i=None):
                    k = 0 if i is None else i
                    dve.wait_ge(sem("silu_made"), k * 2 + (p0 + q + 1))
                    dve.wait_ge(unit_done, k * 4 + (u0 + 2 * q + 2))
                    if i is not None or p0 + q >= 2:
                        dve.wait_ge(sem("h_hi"), k * 2 + (p0 + q - 1))
                    nc.vector.tensor_tensor(hb[:, q % 2, :], G[1][:], sg[:, q % 2, :], ALU.mult)\
                        .then_inc(sem("h_made"), 1)
                    split(u0 + 2 * q + RING, i)
                    split(u0 + 2 * q + 1 + RING, i)
                    dve.wait_ge(sem("h_hi"), k * 2 + (p0 + q + 1))
                    at_ = slice(2 * q, 2 * q + 2) if i is None else bass.ds(i * 4 + 2 * q, 2)
                    nc.vector.tensor_tensor(hTl[:, at_, :], halves(hb[:, q % 2, :]), hTh[:, at_, :],
                                            ALU.subtract).then_inc(sem("h_lo"), 1)

                for q in range(2):
                    pair(q)
                with dve.Fori(1, GU // 4) as i:
                    for q in range(2):
                        pair(q, i)
                for q in range(GU // 4 * 2, GU // 2):
                    pair(q)
                for d in range(DN):
                    split(BASE[f"dn{f}"] + d + RING)

            def add_down(f):
                dve.wait_ge(unit_done, BASE[f"dn{f}"] + DN)
                for t in range(NT):
                    for nh in range(2):
                        c = slice(512 * nh, 512 * nh + 512)
                        ins = nc.vector.tensor_tensor(xn[:, t, c], DB[2 * t + nh][:], xn[:, t, c], ALU.add)
                ins.then_inc(x_ready, 1)

            def add_units(u0):
                for j in range(4):
                    dve.wait_ge(unit_done, u0 + j + 1)
                    c = slice(256 * j, 256 * j + 256)
                    nc.vector.tensor_tensor(xn[:, :, c], halves(G[bank(u0 + j)][:]), xn[:, :, c], ALU.add)\
                        .then_inc(bank_read[bank(u0 + j)], 1)
                    split(u0 + j + RING)
                dve.wait_ge(bank_read[0], bank_reads(u0 + 4)[0])
                dve.wait_ge(bank_read[1], bank_reads(u0 + 4)[1])
                nc.vector.tensor_copy(small[:, 63:64], xn[:, 0, 0:1]).then_inc(x_ready, 1)

            dve.wait_ge(sem("x_in"), 16)
            norm_stats(0, "x0", xn, y[:, 1, :])
            norm_scale("x0", xn)
            split(0)
            dve.wait_ge(sem("gains_in"), 16)
            norm_lo(0, xTh, xTl)
            split(1)
            dve.wait_ge(sem("pos_in"), 16)
            dve.wait_ge(sem("cst_in"), 16)
            two_pi = 2.0 * math.pi
            c1, c2 = 201 / 32, 2029 / 2 ** 20
            c3 = two_pi - c1 - c2
            magic = 12582912.0
            ang, turns = qraw[:, 0, 0:S], qraw[:, 1, 0:S]
            link(nc.vector.tensor_copy(ang, posi[:]))
            link(nc.vector.tensor_scalar(ang, ang, const("invfreq"), None, ALU.mult))
            for out_, shift, turn in ((sinT, 0.0, 0.0), (cosT, math.pi / 2, 0.25)):
                link(nc.vector.tensor_scalar(turns, ang, 1.0 / two_pi, turn, ALU.mult, ALU.add))
                link(nc.vector.tensor_scalar(turns, turns, magic, None, ALU.add))
                link(nc.vector.tensor_scalar(turns, turns, -magic, None, ALU.add))
                link(nc.vector.scalar_tensor_tensor(out_[:], turns, -c1, ang, ALU.mult, ALU.add))
                link(nc.vector.scalar_tensor_tensor(out_[:], turns, -c2, out_[:], ALU.mult, ALU.add))
                link(nc.vector.scalar_tensor_tensor(out_[:], turns, -c3, out_[:], ALU.mult, ALU.add))
                link(nc.vector.tensor_scalar(out_[:], out_[:], shift, 3.1415925, ALU.add, ALU.min))
                nc.vector.tensor_scalar(out_[:], out_[:], -3.1415925, None, ALU.max).then_inc(sem("angles"), 1)
            lam = gains[:, GAIN["lam"][0]:GAIN["lam"][0] + 256]
            link(nc.vector.tensor_tensor(junk[:, 0:P], lam[:, 0:P], lam[:, P:2 * P], ALU.mult))
            nc.vector.reduce_sum(small[:, 0:2], halves(junk[:, 0:P]), AX).then_inc(sem("lam_dots"), 1)
            link(nc.vector.tensor_scalar(small[:, 20:21], gain("g_subln"), 1.0 - LAM_INIT, None, ALU.mult))
            split(2)
            split(3)

            u0 = BASE["in"]
            dve.wait_ge(sem("trig"), 2)
            qk = [qT[:, 0:2, :], qT[:, 2:4, :], kT[:, 0:2, :], kT[:, 2:4, :]]
            for j in range(4):
                rope_cos(j, u0 + j, qk[j], "_a")
                if j >= 1:
                    rope_turn(j - 1, qk[j - 1], qraw, "_a")
                split(u0 + j + RING)
                if j == 1:
                    dve.wait_ge(sem("mem_in"), 16)
                    norm_stats(1, "mem", y, kxT[:, 0:4, :].rearrange("p a n -> p (a n)"))
                    norm_scale("mem", y)
            norm_lo(1, memTh, memTl)
            rope_turn(3, qk[3], qraw, "_a")
            for j in range(3):
                split(u0 + 4 + j + RING)
            for g in range(4):
                if g % 2 == 0:
                    dve.wait_ge(sem("pool_hi"), g + 2)
                nc.vector.scalar_tensor_tensor(xTl[:, 4 + g, :], halves(DB[2 + g // 2][:])[:, g % 2, :],
                                               gain("pool_scale", g), xTh[:, 4 + g, :], ALU.mult,
                                               ALU.subtract).then_inc(sem("pool_lo"), 1)
            split(u0 + 7 + RING)
            dve.wait_ge(sem("lam_exp"), 1)
            link(nc.vector.scalar_tensor_tensor(small[:, 4:5], small[:, 3:4], -LAM_INIT, small[:, 2:3],
                                                ALU.add, ALU.subtract))

            def maxes(s):
                kend, b = P * (s % 2 + 1), s % 2
                dve.wait_ge(sem("da_scores"), s + 1)
                if s >= 2:
                    dve.wait_ge(sem("da_tr"), s - 1)
                for m in range(2):
                    ins = nc.vector.tensor_tensor_reduce(
                        sm[:, b, m, 0:kend], DB[2 * b + m][:, 0:kend], mask_full[:, 2 * P - kend:2 * P],
                        1.0, BIG_NEG, ALU.add, ALU.max, small[:, 6 + m:7 + m])
                link(ins)
                nc.vector.tensor_scalar(small[:, 8 + 2 * b:10 + 2 * b], small[:, 6:8], -0.125, None, ALU.mult)\
                    .then_inc(sem("da_max"), 1)

            kv0 = BASE["kv"]
            maxes(0)
            for s in range(8):
                h, t, b = s // 2, s % 2, s % 2
                kend = P * (t + 1)
                dve.wait_ge(sem("da_exp"), s + 1)
                link(nc.vector.reciprocal(small[:, 16:18], small[:, 12 + 2 * b:14 + 2 * b]))
                link(nc.vector.tensor_scalar(small[:, 18:19], small[:, 17:18], small[:, 4:5], None, ALU.mult))
                link(nc.vector.tensor_scalar(sm[:, b, 1, 0:kend], sm[:, b, 1, 0:kend], small[:, 18:19], None,
                                             ALU.mult))
                nc.vector.scalar_tensor_tensor(sm[:, b, 0, 0:kend], sm[:, b, 0, 0:kend], small[:, 16:17],
                                               sm[:, b, 1, 0:kend], ALU.mult, ALU.add)\
                    .then_inc(sem("da_probs"), 1)
                if s >= 1:
                    da_copy = (s - 1) // 2, (s - 1) % 2
                    dve.wait_ge(sem("da_out"), s)
                    nc.vector.tensor_copy(un[:, da_copy[1], P * da_copy[0]:P * da_copy[0] + P],
                                          TB[da_copy[1]][:, 256:384]).then_inc(sem("da_nat"), 1)
                if s < 7:
                    maxes(s + 1)
                split(kv0 + s + RING)
            dve.wait_ge(sem("da_out"), 8)
            nc.vector.tensor_copy(un[:, 1, 384:512], TB[1][:, 256:384]).then_inc(sem("da_nat"), 1)
            dve.wait_ge(sem("da_sq"), 1)
            heads = un[:].rearrange("p t (h n) -> p (t h) n", n=P)
            link(nc.vector.reduce_sum(ss[:, 32:40], sm[:].rearrange("p a b n -> p (a b n)")
                                      .rearrange("p (k n) -> p k n", n=P), AX))
            k = pow_at("subln")
            mean_square(k, ss[:, 32:40], P)
            dve.wait_ge(rstd_ready, k + 1)
            nc.vector.tensor_tensor(heads, heads, same_cols(rstd[:, k, 0:8], P), ALU.mult)\
                .then_inc(sem("da_normed"), 1)
            for hp in range(2):
                dve.wait_ge(sem("da_hi"), hp + 1)
                nc.vector.scalar_tensor_tensor(xTl[:, 2 * hp:2 * hp + 2, :], halves(DB[hp][:]),
                                               small[:, 20:21], xTh[:, 2 * hp:2 * hp + 2, :], ALU.mult,
                                               ALU.subtract).then_inc(sem("da_lo"), 1)
            post_norm(0, BASE["out"], "p_mix", 1)

            norm(2)
            u0 = BASE["xq"]

            def x_max(h):
                dve.wait_ge(sem("x_scores"), h + 1)
                link(nc.vector.reduce_max(small[:, 22:24], halves(DB[h % 2][:]), AX))
                nc.vector.tensor_scalar(small[:, 24 + 2 * (h % 2):26 + 2 * (h % 2)], small[:, 22:24], -0.0625,
                                        None, ALU.mult).then_inc(sem("x_max"), 1)

            def x_probs(h):
                b = h % 2
                dve.wait_ge(sem("x_exp"), h + 1)
                link(nc.vector.reciprocal(small[:, 32:34], small[:, 28 + 2 * b:30 + 2 * b]))
                for t in range(NT):
                    ins = nc.vector.tensor_scalar(px[:, b, t, :], px[:, b, t, :], small[:, 32 + t:33 + t],
                                                  None, ALU.mult)
                ins.then_inc(sem("x_probs"), 1)

            def x_lo(h):
                dve.wait_ge(sem("x_hi"), h + 1)
                nc.vector.tensor_tensor(xTl[:, 2 * h:2 * h + 2, :], halves(DB[2 + h % 2][:]),
                                        xTh[:, 2 * h:2 * h + 2, :], ALU.subtract).then_inc(sem("x_lo"), 1)

            split(u0 + RING)
            x_max(0)
            split(u0 + 1 + RING)
            x_probs(0)
            x_max(1)
            split(u0 + 2 + RING)
            x_probs(1)
            x_max(2)
            split(u0 + 3 + RING)
            x_probs(2)
            x_lo(0)
            x_max(3)
            x_probs(3)
            x_lo(1)
            x_lo(2)
            x_lo(3)
            post_norm(1, BASE["xo"], "p_x", 2)

            norm(3)
            mlp(0)
            dve.wait_ge(sem("gb_in"), 48)
            dve.wait_ge(sem("post_sq"), 9)
            for t in range(NT):
                for nh in range(2):
                    c = slice(512 * nh, 512 * nh + 512)
                    ins = nc.vector.tensor_tensor(y[:, t, c], DB[2 * t + nh][:], gb[:, c], ALU.mult)
            link(ins)
            finish_post("p_ffn", 2)

            norm(4)
            u0 = BASE["ev"]
            dve.wait_ge(sem("rcos_in"), 16)
            dve.wait_ge(sem("rsin_in"), 16)
            qk = [rqT[:, 0:2, :], rqT[:, 2:4, :], rkT[:, 0:2, :], rkT[:, 2:4, :]]
            for j in range(4):
                rope_cos(j, u0 + j, qk[j], "_b")
                if j >= 1:
                    rope_turn(j - 1, qk[j - 1], braw, "_b")
                split(u0 + j + RING)
            rope_turn(3, qk[3], braw, "_b")
            split(u0 + 4 + RING)
            split(u0 + 5 + RING)

            def ret_decay(h):
                dve.wait_ge(sem("ret_scores"), h + 1)
                if h >= 2:
                    dve.wait_ge(sem("ret_out"), h - 1)
                nc.vector.tensor_tensor(rp[:, h % 2, :], DB[h % 2][:, 0:384], retd[:, h, :], ALU.mult)\
                    .then_inc(sem("ret_probs"), 1)

            def ret_copy(h):
                dve.wait_ge(sem("ret_out"), h + 1)
                nc.vector.tensor_copy(on[:].rearrange("p (t h) n -> p h t n", t=2)[:, h, :, :],
                                      halves(DB[2 + h % 2][:, 0:256])).then_inc(sem("ret_nat"), 1)

            dve.wait_ge(sem("retd_in"), 16)
            ret_decay(0)
            split(u0 + 6 + RING)
            ret_decay(1)
            split(u0 + 7 + RING)
            ret_copy(0)
            ret_decay(2)
            split(u0 + 8 + RING)
            ret_copy(1)
            ret_decay(3)
            split(u0 + 9 + RING)
            ret_copy(2)
            ret_copy(3)
            dve.wait_ge(bank_read[bank(u0 + 10)], bank_reads(u0 + 11)[bank(u0 + 10)])
            dve.wait_ge(sem("cmps_in"), 16)
            for kind in range(2):
                tok = kcT[:, kind, :].rearrange("p (m b) -> p m b", b=16)
                for a in range(2):
                    ins = nc.vector.tensor_tensor(
                        blk[:, kind, :, 16 * a:16 * a + 16], tok[:, a:a + NCMP, :],
                        same_rows(cmps[:, 32 * kind + 16 * a:32 * kind + 16 * a + 16], NCMP), ALU.add)
            ins.then_inc(sem("cmp_blocks"), 1)
            split(u0 + 10 + RING)
            dve.wait_ge(sem("ret_nat"), 4)
            link(nc.vector.reduce_sum(ss[:, 40:48], on[:], AX))
            link(nc.vector.tensor_scalar(ss[:, 40:48], ss[:, 40:48], 1.0 / P, None, ALU.mult))
            nc.vector.tensor_tensor(on[:], on[:], same_cols(ss[:, 40:48], P), ALU.subtract)\
                .then_inc(sem("gn_centred"), 1)
            split(u0 + 11 + RING)
            split(u0 + 12 + RING)
            split(u0 + 13 + RING)
            dve.wait_ge(sem("gn_sq"), 1)
            link(nc.vector.reduce_sum(ss[:, 48:56], osq, AX))
            k = pow_at("gn")
            mean_square(k, ss[:, 48:56], P, 1e-5)
            dve.wait_ge(bank_read[1], bank_reads(u0 + 8)[1])
            dve.wait_ge(sem("gn_sq"), 1)
            link(nc.vector.tensor_tensor(on[:], on[:], rg[:].rearrange("p t (h n) -> p (t h) n", n=P),
                                         ALU.mult))
            dve.wait_ge(rstd_ready, k + 1)
            nc.vector.tensor_tensor(on[:], on[:], same_cols(rstd[:, k, 0:8], P), ALU.mult)\
                .then_inc(sem("ret_normed"), 1)
            dve.wait_ge(sem("cmp_kv"), 1)
            for half in range(2):
                nc.vector.tensor_copy(kcm[64 * half:64 * half + 64, :, 0:NCMP],
                                      TB[0][0:64, 64:64 + 32].rearrange("p (g n) -> p g n", g=2)[:, :, 0:NCMP])
            nc.vector.tensor_copy(vcm[0:NCMP, :, :],
                                  TB[1][0:NCMP, 64:192].rearrange("p (g n) -> p g n", g=2))\
                .then_inc(sem("cmp_out"), 1)
            for hp in range(2):
                dve.wait_ge(sem("ret_hi"), hp + 1)
                nc.vector.tensor_tensor(xTl[:, 2 * hp:2 * hp + 2, :], halves(DB[hp][:]),
                                        xTh[:, 2 * hp:2 * hp + 2, :], ALU.subtract).then_inc(sem("ret_lo"), 1)
            dve.wait_ge(sem("cmp_scores"), 1)
            a0 = CONST["cmpmask"][0]
            for par in range(2):
                ins = nc.vector.tensor_tensor(
                    pc[:, 8 * par:8 * par + 8, :].rearrange("p (h t) n -> p h (t n)", t=2),
                    TB[par][:, 256:256 + 8 * NCMP].rearrange("p (h n) -> p h n", h=4),
                    same_rows(cst[:, a0:a0 + 2 * NCMP], 4), ALU.add)
            link(ins)
            link(nc.vector.reduce_max(ms[:, 14, 0:16], pc[:], AX))
            nc.vector.tensor_tensor(pc[:], pc[:], same_cols(ms[:, 14, 0:16], NCMP), ALU.subtract)\
                .then_inc(sem("cmp_shift"), 1)
            dve.wait_ge(bank_read[bank(u0 + 13)], bank_reads(u0 + 14)[bank(u0 + 13)])
            gate0 = gat[:, :, 0:8]
            link(nc.vector.tensor_tensor(gate0, gate0, same_cols(const("cmpvalid"), 8), ALU.mult))
            dve.wait_ge(sem("cmp_exp"), 1)
            link(nc.vector.reduce_sum(ss[:, 0:16], pc[:], AX))
            link(nc.vector.reciprocal(ss[:, 0:16], ss[:, 0:16]))
            link(nc.vector.tensor_tensor(ss[:, 0:16].rearrange("p (a h t) -> p a h t", a=2, t=2),
                                         ss[:, 0:16].rearrange("p (a h t) -> p a h t", a=2, t=2),
                                         gate0.rearrange("p t (h a) -> p a h t", a=2), ALU.mult))
            nc.vector.tensor_tensor(pc[:], pc[:], same_cols(ss[:, 0:16], NCMP), ALU.mult)\
                .then_inc(sem("cmp_probs"), 1)

            def n_max(s):
                t = s % 2
                kend = P * (t + 1)
                dve.wait_ge(sem("n_scores"), s + 1)
                if s >= 2:
                    dve.wait_ge(sem("n_tr"), s - 1)
                for br in range(2):
                    ins = nc.vector.tensor_tensor_reduce(
                        nsm[:, t, br, 0:kend], DB[t][:, 256 * br:256 * br + kend],
                        mask_full[:, 2 * P - kend:2 * P], 1.0, BIG_NEG, ALU.add, ALU.max,
                        small[:, 56 + 2 * t + br:57 + 2 * t + br])
                link(ins)
                nc.vector.tensor_scalar(small[:, 34 + 4 * t:36 + 4 * t], small[:, 56 + 2 * t:58 + 2 * t], -0.125, None,
                                        ALU.mult).then_inc(sem("n_max"), 1)

            def n_lo(hp):
                dve.wait_ge(sem("n_hi"), hp + 1)
                nc.vector.tensor_tensor(xTl[:, 4 + hp, :], DB[2 + hp % 2][:, 0:S], xTh[:, 4 + hp, :],
                                        ALU.subtract).then_inc(sem("n_lo"), 1)

            for b in range(2):
                dve.wait_ge(sem("cmp_tr"), 3 + b)
                nc.vector.tensor_copy(pcT[0:NCMP, 8 + 4 * b:12 + 4 * b, :],
                                      DB[b][0:NCMP, :].rearrange("p (k n) -> p k n", k=4))\
                    .then_inc(sem("pcT_b"), 1)
            n_max(0)
            for s in range(16):
                h, t = s // 2, s % 2
                kend = P * (t + 1)
                if s < 15:
                    n_max(s + 1)
                dve.wait_ge(sem("n_exp"), s + 1)
                link(nc.vector.reciprocal(small[:, 52:54], small[:, 44 + 4 * t:46 + 4 * t]))
                link(nc.vector.tensor_tensor(
                    small[:, 54:56], small[:, 52:54],
                    gat[:, t, 8:24].rearrange("p (b h) -> p h b", b=2)[:, h, :], ALU.mult))
                for br in range(2):
                    ins = nc.vector.tensor_scalar(nsm[:, t, br, 0:kend], nsm[:, t, br, 0:kend],
                                                  small[:, 54 + br:55 + br], None, ALU.mult)
                ins.then_inc(sem("n_probs"), 1)
                if t == 1:
                    dve.wait_ge(sem("n_tr"), s + 1)
                    if h >= 2:
                        dve.wait_ge(sem("n_out"), h - 1)
                    nc.vector.tensor_copy(npT[:, h % 2, 1, :], TB[1][:, 0:384]).then_inc(sem("npT_b"), 1)
                if s % 4 == 0 and s >= 4:
                    n_lo(s // 4 - 1)
            n_lo(3)
            add_units(BASE["eo"])

            norm(5)
            mlp(1)
            add_down(1)

            norm(6)
            u0 = BASE["od"]
            nc.vector.memset(at[:], 0.0)
            for j in range(8):
                split(u0 + j + RING)
            dve.wait_ge(sem("hgm_in"), 16)
            t_of = {1: fT[:], 2: tot[:, 0:1024], 4: tot[:, 1024:1536], 8: tot[:, 0:256],
                    16: tot[:, 1024:1152], 32: tot[:, 0:64], 64: tot[:, 1024:1056]}

            def merge(idx, hg):
                dve.wait_ge(sem("hg_prod"), 2 * idx + hg + 1)
                q4, k4 = qd[:, 4 * hg:4 * hg + 4, :], kd[:, 4 * hg:4 * hg + 4, :]
                if idx == 0:
                    nc.vector.tensor_tensor(q4, q4, fT[:, 1024 * hg:1024 * hg + 1024]
                                            .rearrange("p (h n) -> p h n", h=4), ALU.mult)\
                        .then_inc(sem("hg_merged"), 1)
                    return
                s = LEVELS[idx - 1]
                nb = 1024 // (2 * s)
                tt = t_of[s][:, hg * 2 * nb:(hg + 1) * 2 * nb].rearrange("p (b two) -> p b two", two=2)
                qv = q4.rearrange("p h n -> p (h n)").rearrange("p (b two s) -> p b two s", two=2, s=s)
                kv = k4.rearrange("p h n -> p (h n)").rearrange("p (b two s) -> p b two s", two=2, s=s)
                nc.vector.tensor_tensor(qv[:, :, 1, :], qv[:, :, 1, :],
                                        tt[:, :, 0:1].broadcast_to([P, nb, s]), ALU.mult)
                if s < 64:
                    nc.vector.tensor_tensor(t_of[2 * s][:, hg * nb:(hg + 1) * nb], tt[:, :, 0], tt[:, :, 1],
                                            ALU.mult)
                nc.vector.tensor_tensor(kv[:, :, 0, :], kv[:, :, 0, :],
                                        tt[:, :, 1:2].broadcast_to([P, nb, s]), ALU.mult)\
                    .then_inc(sem("hg_merged"), 1)
                dve.wait_ge(sem("hg_merged"), 2 * idx + hg + 1)

            def keep(idx, hg):
                if idx == 8:
                    dve.wait_ge(sem("hg_prod"), 2 * idx + hg + 1)
                    nc.vector.tensor_copy(at[:, 4 * hg:4 * hg + 4, 2, :],
                                          DB[2 * hg][:].rearrange("p (h n) -> p h n", h=4))\
                        .then_inc(sem("hg_kept"), 1)
                    return
                for t in range(NT):
                    ins = nc.vector.copy_predicated(at[:, 4 * hg:4 * hg + 4, t, :],
                                                    same_rows(hgm[:, idx, :], 4),
                                                    DB[2 * hg + t][:].rearrange("p (h n) -> p h n", h=4))
                ins.then_inc(sem("hg_kept"), 1)

            for idx in range(9):
                for hg in range(2):
                    if idx < 8:
                        merge(idx, hg)
                    keep(idx, hg)
                if idx < 8:
                    split(u0 + 8 + idx + RING)
            for b in range(4):
                t, hh = b // 2, 4 * (b % 2)
                if b == 0:
                    dve.wait_ge(bank_read[0], bank_reads(u0 + 16)[0])
                    dve.wait_ge(bank_read[1], bank_reads(u0 + 16)[1])
                dve.wait_ge(sem("hg_sq"), b + 1)
                nc.vector.tensor_tensor(
                    oh[:, t, hh:hh + 4, :], DB[b][:].rearrange("p (h n) -> p h n", h=4),
                    gh[:, t, P * hh:P * hh + 512].rearrange("p (h n) -> p h n", h=4), ALU.mult)
                ins = nc.vector.reduce_sum(
                    ss[:, 4 * b:4 * b + 4], kd[:, 2 * b:2 * b + 2, :].rearrange("p a (c n) -> p (a c) n", n=P),
                    AX)
            link(ins)
            k = pow_at("hg")
            mean_square(k, ss[:, 0:16], P)
            dve.wait_ge(rstd_ready, k + 1)
            for t in range(NT):
                ins = nc.vector.tensor_tensor(oh[:, t, :, :], oh[:, t, :, :],
                                              same_cols(rstd[:, k, 8 * t:8 * t + 8], P), ALU.mult)
            ins.then_inc(sem("hg_normed"), 1)
            for b in range(4):
                dve.wait_ge(sem("hg_hi"), b + 1)
                nc.vector.scalar_tensor_tensor(xTl[:, 2 * b:2 * b + 2, :], halves(DB[b][:]), gain("hgrn"),
                                               xTh[:, 2 * b:2 * b + 2, :], ALU.mult, ALU.subtract)\
                    .then_inc(sem("hg_lo"), 1)
            add_units(BASE["oo"])

            norm(7)
            mlp(2)
            add_down(2)
            dve.wait_ge(x_ready, 7)
            norm_stats(8, "fin", xn, y[:, 1, :])
            dve.wait_ge(rstd_ready, pow_at("fin") + 1)
            dve.wait_ge(sem("gb_in"), 64)
            for t in range(NT):
                nc.vector.scalar_tensor_tensor(y[:, t, :], xn[:, t, :], rstd[:, pow_at("fin"), t:t + 1],
                                               gb[:], ALU.mult, ALU.mult).then_inc(sem("out_ready"), 1)

        @block.tensor
        def _(pe):
            def passes(out_, stat, mov, start, stop):
                (sh, sl), (mh, ml) = stat, mov
                nc.tensor.matmul(out_, sh, mh, start=start, stop=False)
                nc.tensor.matmul(out_, sh, ml, start=False, stop=False)
                return nc.tensor.matmul(out_, sl, mh, start=False, stop=stop)

            def wait_unit(u, i=None):
                k = 0 if i is None else i
                pe.wait_ge(lo_ready, k * RING + (u + 1))

            def wait_bank(u):
                n = bank_reads(u)[bank(u)]
                if n > 0:
                    pe.wait_ge(bank_read[bank(u)], n)

            def columns(u, act_h, act_l, ready=None):
                hi = whi[:, u % RING, :].rearrange("p (k n) -> p k n", k=KT)
                lo = wlo[:, u % RING, :].rearrange("p (k n) -> p k n", k=KT)
                for f in range(2):
                    for kt in range(KT):
                        if ready is not None and f == 0:
                            pe.wait_ge(ready[0], ready[1] + kt + 1)
                        c = slice(P * f, P * f + P)
                        ins = passes(G[bank(u)][:, S * f:S * f + S], (hi[:, kt, c], lo[:, kt, c]),
                                     (act_h[:, kt, :], act_l[:, kt, :]), kt == 0, kt == KT - 1)
                return ins

            def rows(u, act_h, act_l, n=256):
                hi = whi[:, u % RING, 0:KT * n].rearrange("p (k n) -> p k n", k=KT)
                lo = wlo[:, u % RING, 0:KT * n].rearrange("p (k n) -> p k n", k=KT)
                for t in range(NT):
                    for kt in range(KT):
                        c = slice(P * t, P * t + P)
                        ins = passes(G[bank(u)][:, 256 * t:256 * t + n], (act_h[:, kt, c], act_l[:, kt, c]),
                                     (hi[:, kt, :], lo[:, kt, :]), kt == 0, kt == KT - 1)
                return ins

            def unit(u, kind, act_h=None, act_l=None, **kw):
                act_h = xTh if act_h is None else act_h
                act_l = xTl if act_l is None else act_l
                wait_unit(u)
                wait_bank(u)
                kind(u, act_h, act_l, **kw).then_inc(unit_done, 1)

            def norm_transposes(n):
                pe.wait_ge(sem("rows_scaled"), 2 * n + 2)
                for kp in range(KT // 2):
                    for kt in (2 * kp, 2 * kp + 1):
                        for t in range(NT):
                            ins = nc.tensor.transpose(
                                DB[kp][:, S * (kt % 2) + P * t:S * (kt % 2) + P * t + P],
                                y[:, t, P * kt:P * kt + P], ident)
                    ins.then_inc(sem("norm_tr"), 1)

            def rotate(j, m, buf, which):
                pe.wait_ge(sem("rope_raw" + which), j + 1)
                if j >= 2:
                    pe.wait_ge(sem("rope_done" + which), j - 1)
                nc.tensor.matmul(TB[j % 2][:], const(m), buf[:, j % 2, :], start=True, stop=True)\
                    .then_inc(sem("rope_rot" + which), 1)

            def mlp(f):
                u0, p0, n = BASE[f"gu{f}"], f * (GU // 2), [3, 5, 7][f]

                def pair(q, i=None):
                    k = 0 if i is None else i
                    for c, read in ((0, "silu_made"), (1, "h_made")):
                        u = u0 + 2 * q + c
                        wait_unit(u, i)
                        if i is not None or p0 + q >= 1:
                            pe.wait_ge(sem(read), k * 2 + (p0 + q))
                        first = i is None and q == 0 and c == 0
                        columns(u, xTh, xTl, ready=(sem("xT_ready"), KT * n) if first else None)\
                            .then_inc(unit_done, 1)

                for q in range(2):
                    pair(q)
                with pe.Fori(1, GU // 4) as i:
                    for q in range(2):
                        pair(q, i)
                for q in range(GU // 4 * 2, GU // 2):
                    pair(q)
                for d in range(DN):
                    u = BASE[f"dn{f}"] + d
                    wait_unit(u)
                    pe.wait_ge(sem("h_lo"), p0 + d + 1)
                    hi = whi[:, u % RING, :].rearrange("p (k n) -> p k n", k=2)
                    lo = wlo[:, u % RING, :].rearrange("p (k n) -> p k n", k=2)
                    for kk in range(2):
                        ft = 2 * d + kk
                        for t in range(NT):
                            c = slice(P * t, P * t + P)
                            for nh in range(2):
                                w = slice(512 * nh, 512 * nh + 512)
                                ins = passes(DB[2 * t + nh][:], (hTh[:, ft, c], hTl[:, ft, c]),
                                             (hi[:, kk, w], lo[:, kk, w]), ft == 0, ft == FT - 1)
                    ins.then_inc(unit_done, 1)

            pe.wait_ge(sem("cst_in"), 16)
            norm_transposes(0)
            u0 = BASE["in"]
            unit(u0, columns, ready=(sem("xT_ready"), 0))
            unit(u0 + 1, columns)
            rotate(0, "rot64", qraw, "_a")
            unit(u0 + 2, columns)
            rotate(1, "rot64", qraw, "_a")
            unit(u0 + 3, columns)
            rotate(2, "rot64", qraw, "_a")
            norm_transposes(1)
            unit(u0 + 4, rows)
            rotate(3, "rot64", qraw, "_a")
            unit(u0 + 5, rows)
            unit(u0 + 6, rows)
            unit(u0 + 7, rows)
            for b in range(2):
                pe.wait_ge(bank_read[b], bank_reads(u0 + 8)[b])
            pe.wait_ge(sem("xT_ready"), 16)
            pe.wait_ge(sem("poolm_in"), 16)
            pe.wait_ge(sem("wpool_in"), 16)
            for g in range(4):
                c = slice(P * g, P * g + P)
                o = halves(DB[g // 2][:])[:, g % 2, :]
                nc.tensor.matmul(o[:, 0:P], un[:, 0, c], poolm[:, g, 0:P], start=True, stop=True)
                nc.tensor.matmul(o[:, P:S], un[:, 0, c], poolm[:, g, P:2 * P], start=True, stop=False)
                ins = nc.tensor.matmul(o[:, P:S], un[:, 1, c], poolm[:, g, 2 * P:], start=False, stop=True)
                if g % 2:
                    ins.then_inc(sem("pooled"), 1)
            for g in range(4):
                if g % 2 == 0:
                    pe.wait_ge(sem("pooled_out"), g // 2 + 1)
                ins = nc.tensor.matmul(halves(DB[2 + g // 2][:])[:, g % 2, :], wpool[:, g, :],
                                       halves(qraw[:, g // 2, :])[:, g % 2, :], start=True, stop=True)
                if g % 2:
                    ins.then_inc(sem("pool_mix"), 1)

            def da_scores(s):
                h, t = s // 2, s % 2
                kend = P * (t + 1)
                if s == 0:
                    pe.wait_ge(sem("rope_done_a"), 4)
                    pe.wait_ge(sem("pool_lo"), 4)
                if s >= 2:
                    pe.wait_ge(sem("da_max"), s - 1)
                for m in range(2):
                    r = slice(64 * m, 64 * m + 64)
                    ins = nc.tensor.matmul(DB[2 * t + m][:, 0:kend], qT[r, h, P * t:P * t + P],
                                           kT[r, h, 0:kend], start=True, stop=True)
                ins.then_inc(sem("da_scores"), 1)

            def da_transposes(s):
                t = s % 2
                pe.wait_ge(sem("da_probs"), s + 1)
                if s >= 2:
                    pe.wait_ge(sem("da_nat"), s - 1)
                for b in range(t + 1):
                    ins = nc.tensor.transpose(TB[t][:, P * b:P * b + P], sm[:, t, 0, P * b:P * b + P], ident)
                ins.then_inc(sem("da_tr"), 1)

            def da_out(s):
                h, t = s // 2, s % 2
                pe.wait_ge(sem("aT"), s + 1)
                for b in range(t + 1):
                    ins = nc.tensor.matmul(TB[t][:, 256:384], aT[:, t, P * b:P * b + P],
                                           vn[:, b, P * h:P * h + P], start=(b == 0), stop=(b == t))
                ins.then_inc(sem("da_out"), 1)

            kv0 = BASE["kv"]
            da_scores(0)
            for s in range(8):
                unit(kv0 + s, columns if s < 4 else rows, memTh, memTl)
                if s >= 1:
                    da_out(s - 1)
                da_transposes(s)
                if s < 7:
                    da_scores(s + 1)
            da_out(7)

            def head_transposes(src, waits, signal, pairs):
                pe.wait_ge(*waits)
                for hp in range(pairs):
                    for h in (2 * hp, 2 * hp + 1):
                        for t in range(NT):
                            ins = nc.tensor.transpose(DB[hp][:, S * (h % 2) + P * t:S * (h % 2) + P * t + P],
                                                      src(t, h), ident)
                    ins.then_inc(signal, 1)

            head_transposes(lambda t, h: un[:, t, P * h:P * h + P], (sem("da_normed"), 1), sem("da_T"), 2)
            pe.wait_ge(sem("da_lo"), 2)
            for j in range(4):
                unit(BASE["out"] + j, rows)

            norm_transposes(2)
            u0 = BASE["xq"]

            def x_scores(h):
                n = bank_reads(u0 + h + 1)
                pe.wait_ge(bank_read[bank(u0 + h)], n[bank(u0 + h)])
                if h == 0:
                    pe.wait_ge(sem("xT_ready"), 24)
                if h >= 2:
                    pe.wait_ge(sem("x_exp"), h - 1)
                for t in range(NT):
                    for dt in range(2):
                        ins = nc.tensor.matmul(halves(DB[h % 2][:])[:, t, :],
                                               xqT[:, 2 * h + dt, P * t:P * t + P], kxT[:, 2 * h + dt, :],
                                               start=(dt == 0), stop=(dt == 1))
                ins.then_inc(sem("x_scores"), 1)

            def x_transposes(h):
                pe.wait_ge(sem("x_probs"), h + 1)
                if h >= 2:
                    pe.wait_ge(sem("x_pT"), h - 1)
                for mt in range(2):
                    for t in range(NT):
                        ins = nc.tensor.transpose(TB[h % 2][:, S * mt + P * t:S * mt + P * t + P],
                                                  px[:, h % 2, t, P * mt:P * mt + P], ident)
                ins.then_inc(sem("x_tr"), 1)

            def x_out(h):
                pe.wait_ge(sem("x_pT"), h + 1)
                if h >= 2:
                    pe.wait_ge(sem("x_lo"), h - 1)
                for dt in range(2):
                    c = S * h + P * dt
                    for mt in range(2):
                        ins = nc.tensor.matmul(halves(DB[2 + h % 2][:])[:, dt, :], vx[:, mt, c:c + P],
                                               pxT[:, h % 2, mt, :], start=(mt == 0), stop=(mt == 1))
                ins.then_inc(sem("x_out"), 1)

            unit(u0, columns, ready=(sem("xT_ready"), 16))
            unit(u0 + 1, columns)
            x_scores(0)
            unit(u0 + 2, columns)
            x_scores(1)
            x_transposes(0)
            unit(u0 + 3, columns)
            x_scores(2)
            x_transposes(1)
            x_out(0)
            x_scores(3)
            x_transposes(2)
            x_out(1)
            x_transposes(3)
            x_out(2)
            x_out(3)
            pe.wait_ge(sem("x_lo"), 4)
            for j in range(4):
                unit(BASE["xo"] + j, rows)

            norm_transposes(3)
            mlp(0)

            norm_transposes(4)
            u0 = BASE["ev"]

            def ret_scores(h):
                if h >= 2:
                    pe.wait_ge(sem("ret_probs"), h - 1)
                nc.tensor.matmul(DB[h % 2][:, 0:256], rkT[:, h, 0:P], rqT[:, h, :], start=True, stop=True)
                nc.tensor.matmul(DB[h % 2][:, 256:384], rkT[:, h, P:S], rqT[:, h, P:S], start=True, stop=True)\
                    .then_inc(sem("ret_scores"), 1)

            def ret_out(h):
                pe.wait_ge(sem("ret_probs"), h + 1)
                if h >= 2:
                    pe.wait_ge(sem("ret_nat"), h - 1)
                c = slice(P * h, P * h + P)
                o = DB[2 + h % 2]
                nc.tensor.matmul(o[:, 0:P], rp[:, h % 2, 0:P], rv[:, 0, c], start=True, stop=True)
                nc.tensor.matmul(o[:, P:2 * P], rp[:, h % 2, P:2 * P], rv[:, 0, c], start=True, stop=False)
                nc.tensor.matmul(o[:, P:2 * P], rp[:, h % 2, 2 * P:3 * P], rv[:, 1, c], start=False, stop=True)\
                    .then_inc(sem("ret_out"), 1)

            unit(u0, columns, ready=(sem("xT_ready"), 32))
            unit(u0 + 1, columns)
            rotate(0, "rot128", braw, "_b")
            unit(u0 + 2, columns)
            rotate(1, "rot128", braw, "_b")
            unit(u0 + 3, columns)
            rotate(2, "rot128", braw, "_b")
            unit(u0 + 4, rows)
            rotate(3, "rot128", braw, "_b")
            unit(u0 + 5, rows)
            unit(u0 + 6, rows)
            pe.wait_ge(sem("rope_done_b"), 4)
            pe.wait_ge(bank_read[bank(u0 + 5)], bank_reads(u0 + 6)[bank(u0 + 5)])
            ret_scores(0)
            ret_scores(1)
            unit(u0 + 7, rows)
            ret_out(0)
            ret_scores(2)
            unit(u0 + 8, columns)
            ret_out(1)
            ret_scores(3)
            unit(u0 + 9, columns)
            ret_out(2)
            unit(u0 + 10, columns)
            ret_out(3)
            unit(u0 + 11, columns)
            unit(u0 + 12, rows)
            unit(u0 + 13, rows, n=NG_COLS)
            pe.wait_ge(sem("cmp_blocks"), 1)
            pe.wait_ge(sem("w1_in"), 16)
            for kind in range(2):
                for j in range(32):
                    for g in range(2):
                        r = slice(64 * g, 64 * g + 64)
                        ins = nc.tensor.matmul(TB[g][0:64, 16 * kind:16 * kind + NCMP], w1[r, kind, j, :],
                                               blk[r, kind, :, j], start=(j == 0), stop=(j == 31))
            ins.then_inc(sem("cmp_hid"), 1)
            head_transposes(lambda t, h: on[:, 4 * t + h, :], (sem("ret_normed"), 1), sem("ret_T"), 2)
            pe.wait_ge(sem("cmp_gelu"), 1)
            nc.tensor.matmul(TB[0][0:64, 64:96].rearrange("p (g n) -> p g n", g=2)[:, :, 0:NCMP],
                             cmps[0:64, 64:128], hid[0:64, 0, :, 0:NCMP], start=True, stop=True)
            for g in range(2):
                ins = nc.tensor.matmul(TB[1][0:NCMP, 64 + 64 * g:128 + 64 * g], hid[0:64, 1, g, 0:NCMP],
                                       cmps[0:64, 128:192], start=True, stop=True)
            ins.then_inc(sem("cmp_kv"), 1)
            pe.wait_ge(sem("cmp_out"), 1)
            for h in range(8):
                par, hp, g = h % 2, h // 2, h // 4
                r = slice(64 * par, 64 * par + 64)
                for t in range(NT):
                    c = 256 + (2 * hp + t) * NCMP
                    ins = nc.tensor.matmul(TB[par][:, c:c + NCMP], nqT[r, hp, P * t:P * t + P],
                                           kcm[r, g, 0:NCMP], start=True, stop=True)
            ins.then_inc(sem("cmp_scores"), 1)

            def n_scores(s):
                h, t = s // 2, s % 2
                kend, g = P * (t + 1), h // 4
                r = slice(64 * (h % 2), 64 * (h % 2) + 64)
                if s >= 2:
                    pe.wait_ge(sem("n_max"), s - 1)
                for br in range(2):
                    ins = nc.tensor.matmul(DB[t][:, 256 * br:256 * br + kend], nqT[r, h // 2, P * t:P * t + P],
                                           ksT[r, br, g, 0:kend], start=True, stop=True)
                ins.then_inc(sem("n_scores"), 1)

            def n_transposes(s):
                h, t = s // 2, s % 2
                pe.wait_ge(sem("n_probs"), s + 1)
                if t == 0 and h >= 1:
                    pe.wait_ge(sem("npT_a"), h)
                    pe.wait_ge(sem("npT_b"), h)
                for br in range(2):
                    for b in range(t + 1):
                        c = P * t + P * b
                        ins = nc.tensor.transpose(TB[br][:, c:c + P], nsm[:, t, br, P * b:P * b + P], ident)
                ins.then_inc(sem("n_tr"), 1)

            def n_out(h):
                g, hp, par = h // 4, h // 2, h % 2
                r = slice(64 * par, 64 * par + 64)
                pe.wait_ge(sem("npT_a"), h + 1)
                pe.wait_ge(sem("npT_b"), h + 1)
                if hp >= 2 and par == 0:
                    pe.wait_ge(sem("n_lo"), hp - 1)
                o = DB[2 + hp % 2]
                idx = 8 * par + 2 * hp
                for br in range(2):
                    c = P * br + 64 * g
                    nc.tensor.matmul(o[r, 0:S], vsw[:, 0, c:c + 64], npT[:, h % 2, br, 0:S],
                                     start=(br == 0), stop=False)
                    nc.tensor.matmul(o[r, P:S], vsw[:, 1, c:c + 64], npT[:, h % 2, br, S:S + P],
                                     start=False, stop=False)
                nc.tensor.matmul(o[r, 0:S], vcm[0:NCMP, g, :], pcT[0:NCMP, idx:idx + 2, :]
                                 .rearrange("p a n -> p (a n)"), start=False, stop=True)\
                    .then_inc(sem("n_out"), 1)

            pe.wait_ge(sem("cmp_probs"), 1)
            pe.wait_ge(sem("ret_lo"), 2)
            for b in range(4):
                o = DB[(2 + b) % 4]
                for k in range(4):
                    ins = nc.tensor.transpose(o[0:NCMP, P * k:P * k + P], pc[:, 4 * b + k, :], ident)
                ins.then_inc(sem("cmp_tr"), 1)
            pe.wait_ge(sem("pcT_b"), 1)
            n_scores(0)
            pe.wait_ge(sem("pcT_b"), 2)
            for s in range(16):
                if s < 15:
                    n_scores(s + 1)
                if s == 0:
                    pe.wait_ge(sem("pcT_a"), 2)
                n_transposes(s)
                if s % 2 == 0 and s >= 2:
                    n_out(s // 2 - 1)
            n_out(7)
            pe.wait_ge(sem("n_lo"), 4)
            for j in range(4):
                unit(BASE["eo"] + j, rows)

            norm_transposes(5)
            mlp(1)

            norm_transposes(6)
            u0 = BASE["od"]
            unit(u0, columns, ready=(sem("xT_ready"), 48))
            for j in range(1, 8):
                unit(u0 + j, columns)

            def level(idx, hg):
                if idx == 0 and hg == 0:
                    for b in range(2):
                        pe.wait_ge(bank_read[b], bank_reads(u0 + 8)[b])
                    pe.wait_ge(sem("xT_ready"), 56)
                if idx >= 1:
                    pe.wait_ge(sem("hg_merged"), 2 * (idx - 1) + hg + 1)
                    pe.wait_ge(sem("hg_kept"), 2 * (idx - 1) + hg + 1)
                for h in range(4 * hg, 4 * hg + 4):
                    c = P * (h % 4)
                    if idx == 8:
                        ins = nc.tensor.matmul(DB[2 * hg][:, c:c + P], kd[:, h, 0:P], qd[:, h, P:S],
                                               start=True, stop=True)
                    else:
                        for t in range(NT):
                            tk = slice(P * t, P * t + P)
                            ins = nc.tensor.matmul(DB[2 * hg + t][:, c:c + P], kd[:, h, tk], qd[:, h, tk],
                                                   start=True, stop=True)
                ins.then_inc(sem("hg_prod"), 1)

            for idx in range(9):
                for hg in range(2):
                    level(idx, hg)
                if idx < 8:
                    unit(u0 + 8 + idx, rows)
            pe.wait_ge(sem("hg_kept"), 18)
            for b in range(2):
                pe.wait_ge(bank_read[b], bank_reads(u0 + 16)[b])
            for b in range(4):
                t = b // 2
                for h in range(4 * (b % 2), 4 * (b % 2) + 4):
                    o, c = DB[b][:, P * (h % 4):P * (h % 4) + P], slice(P * h, P * h + P)
                    if t == 0:
                        ins = nc.tensor.matmul(o, at[:, h, 0, :], vh[:, 0, c], start=True, stop=True)
                    else:
                        nc.tensor.matmul(o, at[:, h, 2, :], vh[:, 0, c], start=True, stop=False)
                        ins = nc.tensor.matmul(o, at[:, h, 1, :], vh[:, 1, c], start=False, stop=True)
                ins.then_inc(sem("hg_out"), 1)
            head_transposes(lambda t, h: oh[:, t, h, :], (sem("hg_normed"), 1), sem("hg_T"), 4)
            pe.wait_ge(sem("hg_lo"), 4)
            for j in range(4):
                unit(BASE["oo"] + j, rows)

            norm_transposes(7)
            mlp(2)


def _constants():
    p = np.arange(P)
    cf = np.zeros((P, N_CONST), np.float32)

    def put(name, a):
        at, n = CONST[name]
        cf[:, at:at + n] = a

    put("ident", np.eye(P))
    put("causal", np.where(p[None, :] <= p[:, None], 0.0, NEG))
    t = np.arange(S)
    ends = np.arange(NCMP) * 16 + 31
    m = np.where(ends[None, :] <= t[:, None], 0.0, NEG).reshape(NT, P, NCMP)
    put("cmpmask", m.transpose(1, 0, 2).reshape(P, NT * NCMP))
    put("cmpvalid", (t >= 31).astype(np.float32).reshape(NT, P).T)
    r64, r128 = np.zeros((P, P)), np.zeros((P, P))
    for b in (0, 64):
        for i in range(8):
            r64[b + i + 8, b + i] = -1.0
            r64[b + i, b + i + 8] = 1.0
    for i in range(64):
        r128[i + 64, i] = -1.0
        r128[i, i + 64] = 1.0
    put("rot64", r64)
    put("rot128", r128)
    freq = np.zeros((P, 1), np.float32)
    inv = (np.float32(500000.0) ** (-np.arange(0, 16, 2, dtype=np.float32) / np.float32(16))).astype(np.float32)
    for b in (0, 8, 64, 72):
        freq[b:b + 8, 0] = inv
    put("invfreq", freq)
    put("half", -0.5)

    pool = np.zeros((P, 4, 3 * P))
    for g, w in enumerate(POOL_WINDOWS):
        s_, t_ = np.arange(S)[:, None], np.arange(S)[None, :]
        full = np.where((s_ <= t_) & (s_ > t_ - w), 1.0 / np.minimum(t_ + 1, w), 0.0) - (s_ == t_)
        pool[:, g, 0:P] = full[0:P, 0:P]
        pool[:, g, P:2 * P] = full[0:P, P:]
        pool[:, g, 2 * P:] = full[P:, P:]

    inv2 = (np.float32(10000.0) ** (-np.arange(64, dtype=np.float32) / np.float32(64))).astype(np.float32)
    ang = (np.arange(S, dtype=np.float32)[None, :] * np.tile(inv2, 2)[:, None]).astype(np.float32)
    ret = np.zeros((P, 2 * S + 4 * 384))
    ret[:, 0:S], ret[:, S:2 * S] = np.cos(ang.astype(np.float64)), np.sin(ang.astype(np.float64))
    for h in range(4):
        lg = np.log(1.0 - 2.0 ** (-5.0 - h))
        diff = p[None, :] - p[:, None]
        diag = np.where(diff >= 0, np.exp(lg * np.maximum(diff, 0)), 0.0)
        off = np.exp(lg * (diff + P))
        ret[:, 2 * S + 384 * h:2 * S + 384 * (h + 1)] = np.concatenate([diag, off, diag], 1) * 128 ** -0.5

    hg = np.zeros((P, 8, P), np.int32)
    hg[:, 0, :] = np.eye(P)
    for i, s_ in enumerate(LEVELS):
        kb, qb = p[:, None] // s_, p[None, :] // s_
        hg[:, i + 1, :] = (kb // 2 == qb // 2) & (kb % 2 == 0) & (qb % 2 == 1)
    return cf, pool.astype(np.float32), ret.astype(np.float32), hg


def _wide(w):
    n = w.shape[1] // 256
    return w.reshape(KT, P, n, 256).transpose(2, 1, 0, 3).reshape(n, P, UNIT)


def _down(w):
    return w.reshape(DN, 2, P, D).transpose(0, 2, 1, 3).reshape(DN, P, UNIT)


def _stream(i):
    def gate_up(g, u):
        return np.stack([_wide(g), _wide(u)], 1).reshape(GU, P, UNIT)

    def cols(w, *ranges):
        return np.concatenate([w[:, a:b] for a, b in ranges], 1)

    ev = i["even_w_in_2"][0]
    ng = np.zeros((1, P, UNIT), np.float32)
    ng[0, :, 0:KT * NG_COLS] = ev[:, 3328:].reshape(KT, P, NG_COLS).transpose(1, 0, 2).reshape(P, -1)
    parts = [
        _wide(i["w_in"]), _wide(i["w_xkv"]), _wide(i["w_out"]), _wide(i["w_xq"]), _wide(i["w_xo"]),
        gate_up(i["w_gate"], i["w_up"]), _down(i["w_down"]),
        _wide(ev[:, 0:2816]), _wide(cols(ev, (2816, 2944), (3072, 3200))),
        _wide(cols(ev, (2944, 3072), (3200, 3328))), ng,
        _wide(i["even_w_out_2"][0]), gate_up(i["ffn_w1_2"][0], i["ffn_w3_2"][0]), _down(i["ffn_w2_2"][0]),
        _wide(i["odd_w_in_2"][0]), _wide(i["odd_w_out_2"][0]),
        gate_up(i["ffn_w1_2"][1], i["ffn_w3_2"][1]), _down(i["ffn_w2_2"][1]),
    ]
    out = np.concatenate(parts, 0)
    assert out.shape == (N_UNITS, P, UNIT)
    return out


def kernel(**inputs):
    import concourse.bacc as bacc
    from concourse.bass_utils import run_bass_kernel_spmd

    i = {k: np.asarray(v) for k, v in inputs.items()}
    gains = np.zeros((P, N_GAIN), np.float32)

    def put(name, a):
        at, n = GAIN[name]
        gains[:, at:at + n] = a

    for name, g in (("g_mix_pre", i["g_mix_pre"]), ("g_x_pre", i["g_x_pre"]), ("g_mem", i["g_mem"]),
                    ("g_ffn_pre", i["g_ffn_pre"]), ("mix0", i["norm_mix_g_2"][0]),
                    ("mix1", i["norm_mix_g_2"][1]), ("ffn0", i["norm_ffn_g_2"][0]),
                    ("ffn1", i["norm_ffn_g_2"][1])):
        put(name, g.reshape(KT, P).T)
    put("g_subln", i["g_subln"][:, None])
    put("hgrn", i["hgrn_norm_g_2"][0][:, None])
    put("pool_scale", i["pool_scale"].reshape(4, P).T)
    put("lam", np.concatenate([i["lambda_q1"], i["lambda_q2"], i["lambda_k1"], i["lambda_k2"]])[None, :])
    cf, pool, ret, hg = _constants()

    def both(a):
        return np.concatenate([a, a], 0)

    cmpw = np.stack([both(i[k][0].reshape(32, 64, 64).transpose(1, 0, 2))
                     for k in ("cmp_w1_k_2", "cmp_w1_v_2")], 1)
    cmps = np.concatenate([both(i["cmp_pos_k_2"][0].T), both(i["cmp_pos_v_2"][0].T),
                           both(i["cmp_w2_k_2"][0]), both(i["cmp_w2_v_2"][0])], 1)
    arrays = {
        "stream": _stream(i), "x": i["x"][0], "mem": i["mem"][0], "pos": i["positions"][0], "gains": gains,
        "rows": np.stack([i["g_mix_post"], i["g_x_post"], i["g_ffn_post"], i["final_norm_g_2"]]),
        "consts": cf, "poolm": pool, "wpool": i["w_pool"].transpose(1, 0, 2), "retm": ret, "hgm": hg,
        "cmpw": cmpw, "cmps": cmps,
    }
    arrays = {f"in_{k}": np.ascontiguousarray(v) for k, v in arrays.items()}
    nc = bacc.Bacc("TRN2", target_bir_lowering=False, num_devices=1)
    args = [nc.dram_tensor(k, v.shape, mybir.dt.from_np(v.dtype), kind="ExternalInput").ap()
            for k, v in arrays.items()]
    out = nc.dram_tensor("out", (S, D), F32, kind="ExternalOutput").ap()
    build(nc, *args, out)
    r = run_bass_kernel_spmd(nc, [arrays], core_ids=[0])
    return r.results[0]["out"].reshape(1, S, D)
```

```python
import math
from contextlib import ExitStack

import numpy as np
import concourse.bass as bass
from concourse import mybir

ALU = mybir.AluOpType
ACT = mybir.ActivationFunctionType
AX = mybir.AxisListType.X
F32 = mybir.dt.float32
F32R = mybir.dt.float32r
I32 = mybir.dt.int32

P = 128
D = 1024
S = 256
NT = S // P
KT = D // P
EPS = 1e-6
NEG = -1.0e30
BIG_NEG = -3.0e38
FF = 2816
FT = FF // P
UNIT = 2048
RING = 4
HEADS_DA, HEADS_X, HEADS_RET, HEADS_NSA, HEADS_HG = 4, 4, 4, 8, 8
LAM_INIT = 0.8 - 0.6 * math.exp(-0.3 * 0)
NCMP = S // 16 - 1
POOL_WINDOWS = (2, 4, 8, 16)
LEVELS = (1, 2, 4, 8, 16, 32, 64)
DK_HG = 128

GU, DN = 2 * (FF // 256), FF // 256
PHASES = [("in", 8), ("kv", 8), ("out", 4), ("xq", 4), ("xo", 4), ("gu0", GU), ("dn0", DN),
          ("ev", 14), ("eo", 4), ("gu1", GU), ("dn1", DN), ("od", 16), ("oo", 4),
          ("gu2", GU), ("dn2", DN)]
BASE = {}
N_UNITS = 0
for _name, _n in PHASES:
    BASE[_name] = N_UNITS
    N_UNITS += _n
NG_UNIT = BASE["ev"] + 5
NG_COLS = 3 * HEADS_NSA
SUMS = {"out": ("G0", "G1", "D2", "D3"), "xo": ("G0", "G1", "D0", "D1"), "dn0": ("D0", "D1", "D2", "D3"),
        "eo": ("G0", "G1", "D2", "D3"), "dn1": ("D0", "D1", "D2", "D3"), "oo": ("G0", "G1", "T0", "T1"),
        "dn2": ("D0", "D1", "D2", "D3")}
PAIRS = {"out": (2, 3, 0, 1), "xo": (0, 1, 2, 3), "eo": (2, 3, 0, 1), "oo": (0, 1, 2, 3)}
N_OF = dict(PHASES)

POW_N = {"subln": 8, "gn": 8, "hg": 16}
POWS = []
for _name in ("x0", "mem", "subln", "p_mix", "x1", "p_x", "x2", "p_ffn", "e0", "gn", "f0", "o0", "hg", "f1",
              "fin"):
    POWS += [_name] if _name in POW_N else [_name + ".0", _name + ".1"]
POW_COL = {}
_at = 0
for _name in POWS:
    POW_COL[_name] = slice(_at, _at + POW_N.get(_name, 1))
    _at += POW_N.get(_name, 1)
N_POW = _at

CONST = {}
_at = 0
for _name, _n in [("ident", 128), ("zeros", 128), ("causal", 128), ("cmpmask", NT * NCMP), ("cmpvalid", NT),
                  ("rot64", 128), ("rot128", 128), ("invfreq", 1), ("half", 16)]:
    CONST[_name] = (_at, _n)
    _at += _n
N_CONST = _at
GAIN = {}
_at = 0
for _name, _n in [("g_mix_pre", KT), ("g_x_pre", KT), ("g_mem", KT), ("g_ffn_pre", KT), ("mix0", KT),
                  ("mix1", KT), ("ffn0", KT), ("ffn1", KT), ("g_subln", 1), ("hgrn", 1), ("pool_scale", 4),
                  ("lam", 256)]:
    GAIN[_name] = (_at, _n)
    _at += _n
N_GAIN = _at


def bank_reads(u):
    n = [0, 0]
    at = 0
    for name, count in PHASES:
        if not name.startswith("gu") and name not in SUMS:
            for j in range(min(max(u - at, 0), count)):
                n[j % 2] += 1
        at += count
    return n


def build(nc, stream, x_in, mem_in, pos_in, gains_in, rows_in, consts_in, poolm_in, wpool_in, retm_in,
          hgm_in, cmpw_in, cmps_in, out):
    ctx = ExitStack()
    sems = {}

    def sem(name):
        if name not in sems:
            sems[name] = ctx.enter_context(nc.semaphore(name))
        return sems[name]

    def sb(stack, name, shape, dt=F32):
        return stack.enter_context(nc.sbuf_tensor("s_" + name, shape, dt))

    with ctx:
        raw = sb(ctx, "raw", [P, RING, UNIT])
        whi = sb(ctx, "whi", [P, RING, UNIT], F32R)
        wlo = sb(ctx, "wlo", [P, RING, UNIT], F32R)
        xn = sb(ctx, "xn", [P, NT, D])
        y = sb(ctx, "y", [P, NT, D])
        xTh = sb(ctx, "xTh", [P, KT, S], F32R)
        xTl = sb(ctx, "xTl", [P, KT, S], F32R)
        cst = sb(ctx, "cst", [P, N_CONST])
        gains = sb(ctx, "gains", [P, N_GAIN])
        gb = sb(ctx, "gb", [P, D])
        ms = sb(ctx, "ms", [P, N_POW])
        rstd = sb(ctx, "rstd", [P, N_POW])
        cmax = sb(ctx, "cmax", [P, 16])
        ss = sb(ctx, "ss", [P, 64])
        small = sb(ctx, "small", [P, 64])
        diag = sb(ctx, "diag", [P, NT, P])

        def const(name):
            a, n = CONST[name]
            return cst[:, a:a + n]

        def gain(name, k=0):
            a, _ = GAIN[name]
            return gains[:, a + k:a + k + 1]

        ident = const("ident")
        mask_full = cst[:, CONST["zeros"][0]:CONST["zeros"][0] + 256]

        a_ = ExitStack()
        memTh = sb(a_, "memTh", [P, KT, S], F32R)
        memTl = sb(a_, "memTl", [P, KT, S], F32R)
        kxT = sb(a_, "kxT", [P, KT, S])
        vx = sb(a_, "vx", [P, NT, D])
        a2 = ExitStack()
        qT = sb(a2, "qT", [P, 4, S])
        kT = sb(a2, "kT", [P, 4, S])
        vn = sb(a2, "vn", [P, NT, 512])
        un = sb(a2, "un", [P, NT, 512])
        cosT = sb(a2, "cosT", [P, S])
        sinT = sb(a2, "sinT", [P, S])
        qraw = sb(a2, "qraw", [P, 2, 512])
        sm = sb(a2, "sm", [P, 2, 2, S])
        aT = sb(a2, "aT", [P, 2, 256])
        poolm = sb(a2, "poolm", [P, 4, 3 * P])
        wpool = aT[:].rearrange("p a (b n) -> p (a b) n", n=P)
        posi = sb(a2, "posi", [P, S], I32)
        a2.close()
        a3 = ExitStack()
        xqT = sb(a3, "xqT", [P, KT, S])
        px = sb(a3, "px", [P, 2, 2, S])
        pxT = sb(a3, "pxT", [P, 2, 2, S])
        a3.close()
        a_.close()
        f_ = ExitStack()
        hTh = sb(f_, "hTh", [P, FT, S], F32R)
        hTl = sb(f_, "hTl", [P, FT, S], F32R)
        sg = sb(f_, "sg", [P, 2, 512])
        hb = sb(f_, "hb", [P, 2, 512])
        f_.close()
        b_ = ExitStack()
        rqT = sb(b_, "rqT", [P, 4, S])
        rkT = sb(b_, "rkT", [P, 4, S])
        rv = sb(b_, "rv", [P, NT, 512])
        rg = sb(b_, "rg", [P, NT, 512])
        nqT = sb(b_, "nqT", [P, 4, S])
        kcT = sb(b_, "kcT", [P, 2, S])
        ksT = sb(b_, "ksT", [P, 2, 2, S])
        vsw = sb(b_, "vsw", [P, NT, 256])
        gat = sb(b_, "gat", [P, NT, NG_COLS])
        cmps = sb(b_, "cmps", [P, 64 + 128])
        hid = sb(b_, "hid", [64, 2, 2, 16])
        kcm = sb(b_, "kcm", [P, 2, 16])
        vcm = sb(b_, "vcm", [16, 2, 64])
        pc = sb(b_, "pc", [P, HEADS_NSA * NT, NCMP])
        braw = sb(b_, "braw", [P, 2, 512])
        rcos = sb(b_, "rcos", [P, S])
        rsin = sb(b_, "rsin", [P, S])
        retd = sb(b_, "retd", [P, 4, 384])
        on = sb(b_, "on", [P, NT * 4, P])
        rp = sb(b_, "rp", [P, 2, 384])
        b2 = ExitStack()
        w1 = sb(b2, "w1", [P, 2, 32, 64])
        blk = y[:].rearrange("p t n -> p (t n)")[:, 0:2 * NCMP * 32].rearrange("p (k n j) -> p k n j", k=2, j=32)
        b2.close()
        b4 = ExitStack()
        nsm = sb(b4, "nsm", [P, 2, 2, S])
        npT = sb(b4, "npT", [P, 2, 2, 384])
        nh = sb(b4, "nh", [P, 4, S], F32R)
        nl = sb(b4, "nl", [P, 4, S], F32R)
        pcT = y[0:16, :, :].rearrange("p t (k n) -> p (t k) n", n=P)
        b4.close()
        osq = braw[:].rearrange("p a (b n) -> p (a b) n", n=P)
        b_.close()
        c_ = ExitStack()
        qd = sb(c_, "qd", [P, 8, S])
        kd = sb(c_, "kd", [P, 8, S])
        fT = sb(c_, "fT", [P, 8 * S])
        tot = sb(c_, "tot", [P, 8 * S // 2 + 8 * S // 4])
        vh = sb(c_, "vh", [P, NT, D])
        gh = sb(c_, "gh", [P, NT, D])
        hgm = sb(c_, "hgm", [P, 8, P], I32)
        at = sb(c_, "at", [P, 8, 3, P])
        oh = qd[:].rearrange("p (t a) (b n) -> p t (a b) n", t=NT, n=P)
        c_.close()

        G = [ctx.enter_context(nc.psum_tensor(f"G{i}", [P, 512], F32)) for i in range(2)]
        DB = [ctx.enter_context(nc.psum_tensor(f"D{i}", [P, 512], F32)) for i in range(4)]
        TB = [ctx.enter_context(nc.psum_tensor(f"T{i}", [P, 512], F32)) for i in range(2)]

        hi_ready, lo_ready, unit_done = sem("hi_ready"), sem("lo_ready"), sem("unit_done")
        landed = [sem(f"raw_landed{i}") for i in range(RING)]
        bank_read = [sem("bank_read0"), sem("bank_read1")]
        ms_ready, rstd_ready = sem("ms_ready"), sem("rstd_ready")
        NORMS = [("g_mix_pre", "x0", None), ("g_mem", "mem", None), ("g_x_pre", "x1", 1),
                 ("g_ffn_pre", "x2", 2), ("mix0", "e0", 3), ("ffn0", "f0", 4), ("mix1", "o0", 5),
                 ("ffn1", "f1", 6)]

        def halves(ap):
            return ap.rearrange("p (a b) -> p a b", a=2)

        def same_rows(ap, n):
            return ap.rearrange("p (a b) -> p a b", a=1).broadcast_to([P, n, ap.shape[-1]])

        def same_cols(ap, n):
            return ap.rearrange("p (a b) -> p a b", b=1).broadcast_to([P, ap.shape[-1], n])

        def bank(u):
            base = max(b for b in BASE.values() if b <= u)
            return (u - base) % 2

        def pow_at(name):
            return POWS.index(name)

        banks = {f"{k}{i}": b[i] for k, b in (("G", G), ("D", DB), ("T", TB)) for i in range(len(b))}

        def sum_banks(ph):
            return [banks[k] for k in SUMS[ph]]

        def norm_banks(n):
            ph = {2: "out", 3: "xo", 4: "dn0", 5: "eo", 6: "dn1", 7: "oo"}.get(n)
            return DB if ph is None else [b for k, b in banks.items() if k not in SUMS[ph]]

        def wait_sum(eng, ph, c):
            if c < 3:
                eng.wait_ge(sem("sum_done"), 3 * list(SUMS).index(ph) + c + 1)
            else:
                eng.wait_ge(unit_done, BASE[ph] + N_OF[ph])

        def chunk(t_, c):
            return t_[:, c // 2, 512 * (c % 2):512 * (c % 2) + 512]

        block = ctx.enter_context(nc.Block())

        @block.sync
        def _(sp):
            sp.dma_start(xn[:], x_in.rearrange("(t p) d -> p t d", p=P)).then_inc(sem("x_in"), 16)
            for j in range(RING):
                sp.dma_start(raw[:, j, :], stream[j, :, :]).then_inc(landed[j], 16)
            with sp.Fori(1, N_UNITS // RING) as i:
                for j in range(RING):
                    sp.wait_ge(lo_ready, i * RING + (j - RING + 1))
                    sp.dma_start(raw[:, j, :], stream[bass.ds(i * RING + j, 1), :, :]
                                 .rearrange("a p n -> p (a n)")).then_inc(landed[j], 16)
            for u in range(N_UNITS // RING * RING, N_UNITS):
                sp.wait_ge(lo_ready, u - RING + 1)
                sp.dma_start(raw[:, u % RING, :], stream[u, :, :]).then_inc(landed[u % RING], 16)
            for t in range(NT):
                sp.wait_ge(sem("out_ready"), t + 1)
                sp.dma_start(out[t * P:(t + 1) * P, :], y[:, t, :]).then_inc(sem("stored"), 16)
            sp.wait_ge(sem("stored"), 16 * NT)

        @block.gpsimd
        def _(pool):
            pool.dma_start(cst[:], consts_in).then_inc(sem("cst_in"), 16)
            pool.dma_start(gains[:], gains_in).then_inc(sem("gains_in"), 16)
            pool.dma_start(posi[:], pos_in.partition_broadcast(P)).then_inc(sem("pos_in"), 16)
            pool.dma_start(gb[:], rows_in[0, :].partition_broadcast(P)).then_inc(sem("gb_in"), 16)
            pool.wait_ge(sem("cst_in"), 16)

            def power(name):
                c, n = POW_COL[name], POW_N.get(name, 1)
                pool.wait_ge(ms_ready, pow_at(name) + 1)
                nc.gpsimd.tensor_tensor(rstd[:, c], ms[:, c], const("half")[:, 0:n],
                                        ALU.pow).then_inc(rstd_ready, 1)

            def load_row(r, version):
                pool.wait_ge(sem("x_part"), 4 * version)
                pool.dma_start(gb[:], rows_in[r, :].partition_broadcast(P)).then_inc(sem("gb_in"), 16)

            power("x0.0")
            power("x0.1")
            pool.wait_ge(sem("norm_sq"), 4)
            pool.dma_start(y[:], mem_in.rearrange("(t p) d -> p t d", p=P)).then_inc(sem("mem_in"), 16)
            pool.dma_start(poolm[:], poolm_in).then_inc(sem("poolm_in"), 16)
            pool.dma_start(wpool, wpool_in).then_inc(sem("wpool_in"), 16)
            power("mem.0")
            power("mem.1")
            power("subln")
            power("p_mix.0")
            power("p_mix.1")
            load_row(1, 1)
            power("x1.0")
            power("x1.1")
            power("p_x.0")
            power("p_x.1")
            load_row(2, 2)
            power("x2.0")
            power("x2.1")
            power("p_ffn.0")
            power("p_ffn.1")
            load_row(3, 3)
            pool.dma_start(rcos[:], retm_in[:, 0:S]).then_inc(sem("rcos_in"), 16)
            pool.dma_start(rsin[:], retm_in[:, S:2 * S]).then_inc(sem("rsin_in"), 16)
            pool.dma_start(retd[:], retm_in[:, 2 * S:].rearrange("p (h n) -> p h n", h=4))\
                .then_inc(sem("retd_in"), 16)
            pool.dma_start(w1[:], cmpw_in).then_inc(sem("w1_in"), 16)
            pool.dma_start(cmps[:], cmps_in).then_inc(sem("cmps_in"), 16)
            power("e0.0")
            power("e0.1")
            power("gn")
            power("f0.0")
            power("f0.1")
            pool.wait_ge(sem("x_part"), 4 * 5)
            pool.dma_start(hgm[:], hgm_in).then_inc(sem("hgm_in"), 16)
            power("o0.0")
            power("o0.1")
            power("hg")
            power("f1.0")
            power("f1.1")
            power("fin.0")
            power("fin.1")

        @block.scalar
        def _(act):
            def split(u, i=None):
                if u >= N_UNITS:
                    return
                k = 0 if i is None else i
                act.wait_ge(landed[u % RING], k * 16 + 16 * (u // RING + 1))
                if u >= RING:
                    act.wait_ge(unit_done, k * RING + (u - RING + 1))
                n = KT * NG_COLS if u == NG_UNIT else UNIT
                nc.scalar.activation(whi[:, u % RING, 0:n], raw[:, u % RING, 0:n], ACT.Copy)\
                    .then_inc(hi_ready, 1)

            def norm_squares(n, src, scratch, version=None):
                for c in range(4):
                    if version is not None:
                        act.wait_ge(sem("x_part"), 4 * (version - 1) + c + 1)
                    nc.scalar.activation(scratch(c), chunk(src, c), ACT.Square, scale=D ** -0.5,
                                         accum_out=ss[:, 16 + c:17 + c]).then_inc(sem("norm_sq"), 1)

            def norm_hi(n, dst):
                for kt in range(KT):
                    if kt % 2 == 0:
                        act.wait_ge(sem("norm_tr"), 4 * n + kt // 2 + 1)
                    nc.scalar.activation(dst[:, kt, :], halves(norm_banks(n)[kt // 2][:])[:, kt % 2, :], ACT.Copy,
                                         scale=gain(NORMS[n][0], kt)).then_inc(sem("norm_hi"), 1)

            def norm(n, last):
                norm_squares(n, xn, lambda c: chunk(y, c), NORMS[n][2])
                norm_hi(n, xTh)
                split(last + RING)

            def evac(u, dst, func=ACT.Copy, scale=1.0):
                act.wait_ge(unit_done, u + 1)
                nc.scalar.activation(dst, halves(G[bank(u)][:]), func, scale=scale)\
                    .then_inc(bank_read[bank(u)], 1)

            def rope_raw(j, u, buf, which):
                act.wait_ge(unit_done, u + 1)
                if j >= 2:
                    act.wait_ge(sem("rope_done" + which), j - 1)
                nc.scalar.activation(buf[:, j % 2, :], G[bank(u)][:], ACT.Copy)\
                    .then_inc(sem("rope_raw" + which), 1)

            def post_squares(k0, ph):
                for c in range(4):
                    wait_sum(act, ph, c)
                    nc.scalar.activation(chunk(y, c), sum_banks(ph)[c][:], ACT.Square, scale=D ** -0.5,
                                         accum_out=ss[:, 24 + c:25 + c]).then_inc(sem("post_sq"), 1)

            def sum_splits(ph):
                for j in range(N_OF[ph] - 1):
                    split(BASE[ph] + j + RING)

            def mlp(f):
                u0, p0 = BASE[f"gu{f}"], f * (GU // 2)

                def pair(q, i=None):
                    k = 0 if i is None else i
                    act.wait_ge(unit_done, k * 4 + (u0 + 2 * q + 1))
                    if i is not None or p0 + q >= 2:
                        act.wait_ge(sem("h_made"), k * 2 + (p0 + q - 1))
                    nc.scalar.activation(sg[:, q % 2, :], G[0][:], ACT.Silu).then_inc(sem("silu_made"), 1)
                    split(u0 + 2 * q + RING, i)
                    split(u0 + 2 * q + 1 + RING, i)
                    act.wait_ge(sem("h_made"), k * 2 + (p0 + q + 1))
                    dst = hTh[:, 2 * q:2 * q + 2, :] if i is None else hTh[:, bass.ds(i * 4 + 2 * q, 2), :]
                    nc.scalar.activation(dst, halves(hb[:, q % 2, :]), ACT.Copy).then_inc(sem("h_hi"), 1)

                for q in range(2):
                    pair(q)
                with act.Fori(1, GU // 4) as i:
                    for q in range(2):
                        pair(q, i)
                for q in range(GU // 4 * 2, GU // 2):
                    pair(q)
                sum_splits(f"dn{f}")

            act.wait_ge(sem("x_in"), 16)
            norm_squares(0, xn, lambda c: chunk(y, c))
            split(0)
            split(1)
            act.wait_ge(sem("gains_in"), 16)
            norm_hi(0, xTh)
            split(2)
            split(3)
            act.wait_ge(sem("angles"), 2)
            nc.scalar.activation(sinT[:], sinT[:], ACT.Sin).then_inc(sem("trig"), 1)
            nc.scalar.activation(cosT[:], cosT[:], ACT.Sin).then_inc(sem("trig"), 1)
            u0 = BASE["in"]
            for j in range(4):
                rope_raw(j, u0 + j, qraw, "_a")
                split(u0 + j + RING)
                if j == 1:
                    act.wait_ge(sem("mem_in"), 16)
                    mem_scratch = kxT[:].rearrange("p (c k) n -> p c (k n)", c=4)
                    norm_squares(1, y, lambda c: mem_scratch[:, c, :])
            norm_hi(1, memTh)
            for j in range(2):
                evac(u0 + 4 + j, vn[:, :, 256 * j:256 * j + 256])
                split(u0 + 4 + j + RING)
            for j in range(2):
                evac(u0 + 6 + j, un[:, :, 256 * j:256 * j + 256])
                if j == 0:
                    split(u0 + 6 + RING)
            act.wait_ge(sem("rope_done_a"), 4)
            for gp in range(2):
                act.wait_ge(sem("pooled"), gp + 1)
                nc.scalar.activation(qraw[:, gp, :], DB[gp][:], ACT.Copy).then_inc(sem("pooled_out"), 1)
            for g in range(4):
                if g % 2 == 0:
                    act.wait_ge(sem("pool_mix"), g // 2 + 1)
                nc.scalar.activation(xTh[:, 4 + g, :], halves(DB[2 + g // 2][:])[:, g % 2, :], ACT.Copy,
                                     scale=gain("pool_scale", g)).then_inc(sem("pool_hi"), 1)
            split(u0 + 7 + RING)
            act.wait_ge(sem("lam_dots"), 1)
            nc.scalar.activation(small[:, 2:4], small[:, 0:2], ACT.Exp).then_inc(sem("lam_exp"), 1)

            def exps(s):
                kend = P * (s % 2 + 1)
                act.wait_ge(sem("da_max"), s + 1)
                for m in range(2):
                    ins = nc.scalar.activation(sm[:, s % 2, m, 0:kend], sm[:, s % 2, m, 0:kend], ACT.Exp,
                                               bias=small[:, 8 + 2 * (s % 2) + m:9 + 2 * (s % 2) + m],
                                               scale=0.125,
                                               accum_out=small[:, 12 + 2 * (s % 2) + m:13 + 2 * (s % 2) + m])
                ins.then_inc(sem("da_exp"), 1)

            kv0 = BASE["kv"]
            exps(0)
            for s in range(8):
                if s < 4:
                    evac(kv0 + s, kxT[:, 2 * s:2 * s + 2, :])
                else:
                    evac(kv0 + s, vx[:, :, 256 * (s - 4):256 * (s - 3)])
                act.wait_ge(sem("da_tr"), s + 1)
                if s >= 2:
                    act.wait_ge(sem("da_out"), s - 1)
                n = P * (s % 2 + 1)
                nc.scalar.activation(aT[:, s % 2, 0:n], TB[s % 2][:, 0:n], ACT.Copy).then_inc(sem("aT"), 1)
                if s < 7:
                    exps(s + 1)
                split(kv0 + s + RING)
            act.wait_ge(sem("da_nat"), 8)
            nc.scalar.activation(sm[:].rearrange("p a b n -> p (a b n)"), un[:].rearrange("p t n -> p (t n)"),
                                 ACT.Square).then_inc(sem("da_sq"), 1)
            for hp in range(2):
                act.wait_ge(sem("da_T"), hp + 1)
                nc.scalar.activation(xTh[:, 2 * hp:2 * hp + 2, :], halves(DB[hp][:]), ACT.Copy,
                                     scale=small[:, 20:21]).then_inc(sem("da_hi"), 1)
            for j in range(3):
                split(BASE["out"] + j + RING)
            post_squares(0, "out")

            norm(2, BASE["out"] + 3)
            u0 = BASE["xq"]

            def x_exp(h):
                act.wait_ge(sem("x_max"), h + 1)
                for t in range(NT):
                    ins = nc.scalar.activation(px[:, h % 2, t, :], halves(DB[h % 2][:])[:, t, :], ACT.Exp,
                                               bias=small[:, 24 + 2 * (h % 2) + t:25 + 2 * (h % 2) + t],
                                               scale=0.0625,
                                               accum_out=small[:, 28 + 2 * (h % 2) + t:29 + 2 * (h % 2) + t])
                ins.then_inc(sem("x_exp"), 1)

            def x_T(h):
                act.wait_ge(sem("x_tr"), h + 1)
                if h >= 2:
                    act.wait_ge(sem("x_out"), h - 1)
                nc.scalar.activation(pxT[:, h % 2, :, :], halves(TB[h % 2][:]), ACT.Copy)\
                    .then_inc(sem("x_pT"), 1)

            def x_hi(h):
                act.wait_ge(sem("x_out"), h + 1)
                nc.scalar.activation(xTh[:, 2 * h:2 * h + 2, :], halves(DB[2 + h % 2][:]), ACT.Copy)\
                    .then_inc(sem("x_hi"), 1)

            evac(u0, xqT[:, 0:2, :])
            split(u0 + RING)
            evac(u0 + 1, xqT[:, 2:4, :])
            split(u0 + 1 + RING)
            x_exp(0)
            evac(u0 + 2, xqT[:, 4:6, :])
            split(u0 + 2 + RING)
            x_exp(1)
            x_T(0)
            evac(u0 + 3, xqT[:, 6:8, :])
            split(u0 + 3 + RING)
            x_exp(2)
            x_T(1)
            x_hi(0)
            x_exp(3)
            x_T(2)
            x_hi(1)
            x_T(3)
            x_hi(2)
            x_hi(3)
            sum_splits("xo")
            post_squares(1, "xo")

            norm(3, BASE["xo"] + 3)
            mlp(0)
            post_squares(2, "dn0")

            norm(4, BASE["dn0"] + DN - 1)
            u0 = BASE["ev"]
            for j in range(2):
                evac(u0 + j, nqT[:, 2 * j:2 * j + 2, :])
                split(u0 + j + RING)
            evac(u0 + 2, kcT[:])
            split(u0 + 2 + RING)
            act.wait_ge(unit_done, u0 + 4)
            for half in range(2):
                for g in range(2):
                    ins = nc.scalar.activation(ksT[64 * half:64 * half + 64, :, g, :],
                                               halves(G[bank(u0 + 3)][64 * g:64 * g + 64, :]), ACT.Copy)
            ins.then_inc(bank_read[bank(u0 + 3)], 1)
            split(u0 + 3 + RING)
            evac(u0 + 4, vsw[:])
            split(u0 + 4 + RING)
            act.wait_ge(sem("cmp_hid"), 1)
            for g in range(2):
                ins = nc.scalar.activation(hid[0:64, :, g, 0:NCMP],
                                           TB[g][0:64, 0:32].rearrange("p (k n) -> p k n", k=2)[:, :, 0:NCMP],
                                           ACT.Gelu_apprx_tanh)
            ins.then_inc(sem("cmp_gelu"), 1)
            act.wait_ge(unit_done, u0 + 6)
            nc.scalar.activation(gat[:], halves(G[bank(u0 + 5)][:])[:, :, 0:NG_COLS], ACT.Sigmoid)\
                .then_inc(bank_read[bank(u0 + 5)], 1)
            split(u0 + 5 + RING)
            rope_raw(0, u0 + 6, braw, "_b")
            split(u0 + 6 + RING)

            def n_exp(s):
                t = s % 2
                kend = P * (t + 1)
                act.wait_ge(sem("n_max"), s + 1)
                for br in range(2):
                    ins = nc.scalar.activation(nsm[:, t, br, 0:kend], nsm[:, t, br, 0:kend], ACT.Exp,
                                               bias=small[:, 34 + 4 * t + br:35 + 4 * t + br], scale=0.125,
                                               accum_out=small[:, 44 + 4 * t + br:45 + 4 * t + br])
                ins.then_inc(sem("n_exp"), 1)

            def n_hi(hp):
                act.wait_ge(sem("n_out"), 2 * hp + 2)
                nc.scalar.activation(nh[:, hp, :], DB[2 + hp % 2][:, 0:S], ACT.Copy)\
                    .then_inc(sem("n_hi"), 1)

            def pcT_half(b):
                act.wait_ge(sem("cmp_tr"), b + 1)
                nc.scalar.activation(pcT[0:NCMP, 4 * b:4 * b + 4, :],
                                     DB[2 + b % 2][0:NCMP, :].rearrange("p (k n) -> p k n", k=4), ACT.Copy)\
                    .then_inc(sem("pcT"), 1)

            n_exp(0)
            n_exp(1)
            act.wait_ge(sem("cmp_shift"), 1)
            nc.scalar.activation(pc[:], pc[:], ACT.Exp, scale=0.125).then_inc(sem("cmp_exp"), 1)
            rope_raw(1, u0 + 7, braw, "_b")
            split(u0 + 7 + RING)
            pcT_half(0)
            pcT_half(1)
            for h in range(8):
                act.wait_ge(sem("n_tr"), 2 * h + 2)
                if h >= 2:
                    act.wait_ge(sem("n_out"), h - 1)
                nc.scalar.activation(npT[:, h % 2, 0, :], TB[0][:, 0:384], ACT.Copy)\
                    .then_inc(sem("npT_a"), 1)
                if h == 0:
                    pcT_half(2)
                    pcT_half(3)
                if h < 7:
                    n_exp(2 * h + 2)
                    n_exp(2 * h + 3)
                u = u0 + 8 + h
                if h < 2:
                    rope_raw(2 + h, u, braw, "_b")
                elif h < 4:
                    evac(u, rv[:, :, 256 * (h - 2):256 * (h - 1)])
                elif h < 6:
                    evac(u, rg[:, :, 256 * (h - 4):256 * (h - 3)], ACT.Silu)
                if h < 6:
                    split(u + RING)
                if h % 2 == 1:
                    n_hi(h // 2)
            split(BASE["eo"] + RING)
            act.wait_ge(sem("gn_centred"), 1)
            nc.scalar.activation(osq, on[:], ACT.Square).then_inc(sem("gn_sq"), 1)
            split(BASE["eo"] + 1 + RING)
            for hp in range(2):
                act.wait_ge(sem("ret_T"), hp + 1)
                nc.scalar.activation(xTh[:, 2 * hp:2 * hp + 2, :], halves(DB[hp][:]), ACT.Copy)\
                    .then_inc(sem("ret_hi"), 1)
            split(BASE["eo"] + 2 + RING)

            norm(5, BASE["eo"] + 3)
            mlp(1)

            norm(6, BASE["dn1"] + DN - 1)
            u0 = BASE["od"]
            for j in range(4):
                evac(u0 + j, qd[:, 2 * j:2 * j + 2, :], ACT.Silu)
                split(u0 + j + RING)
            for j in range(4):
                u = u0 + 4 + j
                act.wait_ge(unit_done, u + 1)
                nc.scalar.activation(fT[:, 512 * j:512 * j + 512], G[bank(u)][:], ACT.Sigmoid)\
                    .then_inc(sem("f_made"), 1)
                evac(u, kd[:, 2 * j:2 * j + 2, :], ACT.Sigmoid, scale=-1.0)
                split(u + RING)
            for j in range(4):
                evac(u0 + 8 + j, vh[:, :, 256 * j:256 * j + 256], ACT.Copy, scale=DK_HG ** -0.5)
                split(u0 + 8 + j + RING)
            for j in range(4):
                evac(u0 + 12 + j, gh[:, :, 256 * j:256 * j + 256], ACT.Sigmoid)
                split(u0 + 12 + j + RING)
            for b in range(4):
                act.wait_ge(sem("hg_out"), b + 1)
                nc.scalar.activation(kd[:, 2 * b:2 * b + 2, :], halves(DB[b][:]), ACT.Square)\
                    .then_inc(sem("hg_sq"), 1)
            for b in range(4):
                act.wait_ge(sem("hg_T"), b + 1)
                nc.scalar.activation(xTh[:, 2 * b:2 * b + 2, :], halves(DB[b][:]), ACT.Copy,
                                     scale=gain("hgrn")).then_inc(sem("hg_hi"), 1)
            sum_splits("oo")

            norm(7, BASE["oo"] + 3)
            mlp(2)
            norm_squares(8, xn, lambda c: chunk(y, c), 7)

        @block.vector
        def _(dve):
            chain = [0]

            def link(ins):
                chain[0] += 1
                ins.then_inc(sem("dve_chain"), 1)
                dve.wait_ge(sem("dve_chain"), chain[0])

            def split(u, i=None):
                if u >= N_UNITS:
                    return
                k = 0 if i is None else i
                dve.wait_ge(hi_ready, k * RING + (u + 1))
                n = KT * NG_COLS if u == NG_UNIT else UNIT
                nc.vector.tensor_tensor(wlo[:, u % RING, 0:n], raw[:, u % RING, 0:n],
                                        whi[:, u % RING, 0:n], ALU.subtract).then_inc(lo_ready, 1)

            def mean_square(name, sums, count, eps=EPS):
                nc.vector.tensor_scalar(ms[:, POW_COL[name]], sums, 1.0 / count, eps, ALU.mult, ALU.add)\
                    .then_inc(ms_ready, 1)

            def tile_mean(name, t, at_):
                nc.vector.scalar_tensor_tensor(ms[:, POW_COL[f"{name}.{t}"]], ss[:, at_ + 2 * t:at_ + 2 * t + 1],
                                               EPS, ss[:, at_ + 2 * t + 1:at_ + 2 * t + 2], ALU.add, ALU.add)\
                    .then_inc(ms_ready, 1)

            def norm_mean(n, name, t):
                dve.wait_ge(sem("norm_sq"), 4 * n + 2 * t + 2)
                tile_mean(name, t, 16)

            def norm_diag(name, t):
                k = POW_COL[f"{name}.{t}"]
                dve.wait_ge(rstd_ready, pow_at(f"{name}.{t}") + 1)
                nc.vector.tensor_scalar(diag[:, t, :], ident, rstd[:, k], None, ALU.mult)\
                    .then_inc(sem("diag_ready"), 1)

            def norm_lo(n, dst_h, dst_l):
                for kt in range(KT):
                    if kt % 2 == 0:
                        dve.wait_ge(sem("norm_hi"), KT * n + kt + 2)
                    nc.vector.scalar_tensor_tensor(
                        dst_l[:, kt, :], halves(norm_banks(n)[kt // 2][:])[:, kt % 2, :], gain(NORMS[n][0], kt),
                        dst_h[:, kt, :], ALU.mult, ALU.subtract).then_inc(sem("xT_ready"), 1)

            def norm_rest(n, last):
                name = NORMS[n][1]
                norm_mean(n, name, 1)
                norm_diag(name, 0)
                norm_diag(name, 1)
                norm_lo(n, xTh, xTl)
                split(last + RING)

            def rope_turn(j, dst, buf, which):
                dve.wait_ge(sem("rope_rot" + which), j + 1)
                sin = sinT if which == "_a" else rsin
                link(nc.vector.tensor_tensor(halves(buf[:, j % 2, :]), halves((TB if which == "_a" else G)[j % 2][:]),
                                             same_rows(sin[:], 2), ALU.mult))
                nc.vector.tensor_tensor(dst, dst, halves(buf[:, j % 2, :]), ALU.add)\
                    .then_inc(sem("rope_done" + which), 1)

            def rope_cos(j, u, dst, which):
                dve.wait_ge(sem("rope_raw" + which), j + 1)
                cos = cosT if which == "_a" else rcos
                nc.vector.tensor_tensor(dst, halves(G[bank(u)][:]), same_rows(cos[:], 2), ALU.mult)\
                    .then_inc(bank_read[bank(u)], 1)

            def post_norm(k0, ph, name, n):
                o = sum_banks(ph)

                def gained(c):
                    dve.wait_ge(sem("post_sq"), 4 * k0 + c + 1)
                    ins = nc.vector.tensor_tensor(chunk(y, c), o[c][:], gb[:, 512 * (c % 2):512 * (c % 2) + 512],
                                                  ALU.mult)
                    if c % 2:
                        link(ins)

                def update(c):
                    k = POW_COL[f"{name}.{c // 2}"]
                    dve.wait_ge(rstd_ready, pow_at(f"{name}.{c // 2}") + 1)
                    nc.vector.scalar_tensor_tensor(chunk(xn, c), chunk(y, c), rstd[:, k], chunk(xn, c),
                                                   ALU.mult, ALU.add).then_inc(sem("x_part"), 1)

                dve.wait_ge(sem("gb_in"), 16 * (k0 + 1))
                gained(0)
                dve.wait_ge(sem("post_sq"), 4 * k0 + 2)
                tile_mean(name, 0, 24)
                gained(1)
                gained(2)
                update(0)
                dve.wait_ge(sem("post_sq"), 4 * k0 + 4)
                tile_mean(name, 1, 24)
                update(1)
                gained(3)
                update(2)
                norm_mean(n, NORMS[n][1], 0)
                update(3)

            def add_sum(ph, n, name):
                for c in range(4):
                    wait_sum(dve, ph, c)
                    nc.vector.tensor_tensor(chunk(xn, c), sum_banks(ph)[c][:], chunk(xn, c), ALU.add)\
                        .then_inc(sem("x_part"), 1)
                    if c == 2:
                        norm_mean(n, name, 0)

            def sum_splits(ph):
                for j in range(N_OF[ph] - 1):
                    split(BASE[ph] + j + RING)

            def mlp(f):
                u0, p0 = BASE[f"gu{f}"], f * (GU // 2)

                def pair(q, i=None):
                    k = 0 if i is None else i
                    dve.wait_ge(sem("silu_made"), k * 2 + (p0 + q + 1))
                    dve.wait_ge(unit_done, k * 4 + (u0 + 2 * q + 2))
                    if i is not None or p0 + q >= 2:
                        dve.wait_ge(sem("h_hi"), k * 2 + (p0 + q - 1))
                    nc.vector.tensor_tensor(hb[:, q % 2, :], G[1][:], sg[:, q % 2, :], ALU.mult)\
                        .then_inc(sem("h_made"), 1)
                    split(u0 + 2 * q + RING, i)
                    split(u0 + 2 * q + 1 + RING, i)
                    dve.wait_ge(sem("h_hi"), k * 2 + (p0 + q + 1))
                    at_ = slice(2 * q, 2 * q + 2) if i is None else bass.ds(i * 4 + 2 * q, 2)
                    nc.vector.tensor_tensor(hTl[:, at_, :], halves(hb[:, q % 2, :]), hTh[:, at_, :],
                                            ALU.subtract).then_inc(sem("h_lo"), 1)

                for q in range(2):
                    pair(q)
                with dve.Fori(1, GU // 4) as i:
                    for q in range(2):
                        pair(q, i)
                for q in range(GU // 4 * 2, GU // 2):
                    pair(q)
                sum_splits(f"dn{f}")

            dve.wait_ge(sem("cst_in"), 16)
            norm_mean(0, "x0", 0)
            norm_mean(0, "x0", 1)
            norm_diag("x0", 0)
            norm_diag("x0", 1)
            split(0)
            dve.wait_ge(sem("gains_in"), 16)
            norm_lo(0, xTh, xTl)
            split(1)
            dve.wait_ge(sem("pos_in"), 16)
            two_pi = 2.0 * math.pi
            c1, c2 = 201 / 32, 2029 / 2 ** 20
            c3 = two_pi - c1 - c2
            magic = 12582912.0
            ang, turns = qraw[:, 0, 0:S], qraw[:, 1, 0:S]
            link(nc.vector.tensor_copy(ang, posi[:]))
            link(nc.vector.tensor_scalar(ang, ang, const("invfreq"), None, ALU.mult))
            for out_, shift, turn in ((sinT, 0.0, 0.0), (cosT, math.pi / 2, 0.25)):
                link(nc.vector.tensor_scalar(turns, ang, 1.0 / two_pi, turn, ALU.mult, ALU.add))
                link(nc.vector.tensor_scalar(turns, turns, magic, None, ALU.add))
                link(nc.vector.tensor_scalar(turns, turns, -magic, None, ALU.add))
                link(nc.vector.scalar_tensor_tensor(out_[:], turns, -c1, ang, ALU.mult, ALU.add))
                link(nc.vector.scalar_tensor_tensor(out_[:], turns, -c2, out_[:], ALU.mult, ALU.add))
                link(nc.vector.scalar_tensor_tensor(out_[:], turns, -c3, out_[:], ALU.mult, ALU.add))
                link(nc.vector.tensor_scalar(out_[:], out_[:], shift, 3.1415925, ALU.add, ALU.min))
                nc.vector.tensor_scalar(out_[:], out_[:], -3.1415925, None, ALU.max).then_inc(sem("angles"), 1)
            lam = gains[:, GAIN["lam"][0]:GAIN["lam"][0] + 256]
            link(nc.vector.tensor_tensor(lam[:, 0:P], lam[:, 0:P], lam[:, P:2 * P], ALU.mult))
            nc.vector.reduce_sum(small[:, 0:2], halves(lam[:, 0:P]), AX).then_inc(sem("lam_dots"), 1)
            link(nc.vector.tensor_scalar(small[:, 20:21], gain("g_subln"), 1.0 - LAM_INIT, None, ALU.mult))
            split(2)
            split(3)

            u0 = BASE["in"]
            dve.wait_ge(sem("trig"), 2)
            qk = [qT[:, 0:2, :], qT[:, 2:4, :], kT[:, 0:2, :], kT[:, 2:4, :]]
            for j in range(4):
                rope_cos(j, u0 + j, qk[j], "_a")
                if j >= 1:
                    rope_turn(j - 1, qk[j - 1], qraw, "_a")
                split(u0 + j + RING)
                if j == 1:
                    norm_mean(1, "mem", 0)
                    norm_mean(1, "mem", 1)
                    norm_diag("mem", 0)
                    norm_diag("mem", 1)
            norm_lo(1, memTh, memTl)
            rope_turn(3, qk[3], qraw, "_a")
            for j in range(3):
                split(u0 + 4 + j + RING)
            for g in range(4):
                if g % 2 == 0:
                    dve.wait_ge(sem("pool_hi"), g + 2)
                nc.vector.scalar_tensor_tensor(xTl[:, 4 + g, :], halves(DB[2 + g // 2][:])[:, g % 2, :],
                                               gain("pool_scale", g), xTh[:, 4 + g, :], ALU.mult,
                                               ALU.subtract).then_inc(sem("pool_lo"), 1)
            split(u0 + 7 + RING)
            dve.wait_ge(sem("lam_exp"), 1)
            link(nc.vector.scalar_tensor_tensor(small[:, 4:5], small[:, 3:4], -LAM_INIT, small[:, 2:3],
                                                ALU.add, ALU.subtract))

            def maxes(s):
                kend, b = P * (s % 2 + 1), s % 2
                dve.wait_ge(sem("da_scores"), s + 1)
                if s >= 2:
                    dve.wait_ge(sem("da_tr"), s - 1)
                for m in range(2):
                    ins = nc.vector.tensor_tensor_reduce(
                        sm[:, b, m, 0:kend], DB[2 * b + m][:, 0:kend], mask_full[:, 2 * P - kend:2 * P],
                        1.0, BIG_NEG, ALU.add, ALU.max, small[:, 6 + m:7 + m])
                link(ins)
                nc.vector.tensor_scalar(small[:, 8 + 2 * b:10 + 2 * b], small[:, 6:8], -0.125, None, ALU.mult)\
                    .then_inc(sem("da_max"), 1)

            kv0 = BASE["kv"]
            maxes(0)
            for s in range(8):
                h, t, b = s // 2, s % 2, s % 2
                kend = P * (t + 1)
                dve.wait_ge(sem("da_exp"), s + 1)
                link(nc.vector.reciprocal(small[:, 16:18], small[:, 12 + 2 * b:14 + 2 * b]))
                link(nc.vector.tensor_scalar(small[:, 18:19], small[:, 17:18], small[:, 4:5], None, ALU.mult))
                link(nc.vector.tensor_scalar(sm[:, b, 1, 0:kend], sm[:, b, 1, 0:kend], small[:, 18:19], None,
                                             ALU.mult))
                nc.vector.scalar_tensor_tensor(sm[:, b, 0, 0:kend], sm[:, b, 0, 0:kend], small[:, 16:17],
                                               sm[:, b, 1, 0:kend], ALU.mult, ALU.add)\
                    .then_inc(sem("da_probs"), 1)
                if s >= 1:
                    da_copy = (s - 1) // 2, (s - 1) % 2
                    dve.wait_ge(sem("da_out"), s)
                    nc.vector.tensor_copy(un[:, da_copy[1], P * da_copy[0]:P * da_copy[0] + P],
                                          TB[da_copy[1]][:, 256:384]).then_inc(sem("da_nat"), 1)
                if s < 7:
                    maxes(s + 1)
                split(kv0 + s + RING)
            dve.wait_ge(sem("da_out"), 8)
            nc.vector.tensor_copy(un[:, 1, 384:512], TB[1][:, 256:384]).then_inc(sem("da_nat"), 1)
            dve.wait_ge(sem("da_sq"), 1)
            heads = un[:].rearrange("p t (h n) -> p (t h) n", n=P)
            link(nc.vector.reduce_sum(ss[:, 32:40], sm[:].rearrange("p a b n -> p (a b n)")
                                      .rearrange("p (k n) -> p k n", n=P), AX))
            k = POW_COL["subln"]
            mean_square("subln", ss[:, 32:40], P)
            dve.wait_ge(rstd_ready, pow_at("subln") + 1)
            nc.vector.tensor_tensor(heads, heads, same_cols(rstd[:, k], P), ALU.mult)\
                .then_inc(sem("da_normed"), 1)
            for hp in range(2):
                dve.wait_ge(sem("da_hi"), hp + 1)
                nc.vector.scalar_tensor_tensor(xTl[:, 2 * hp:2 * hp + 2, :], halves(DB[hp][:]),
                                               small[:, 20:21], xTh[:, 2 * hp:2 * hp + 2, :], ALU.mult,
                                               ALU.subtract).then_inc(sem("da_lo"), 1)
            sum_splits("out")
            post_norm(0, "out", "p_mix", 2)

            norm_rest(2, BASE["out"] + 3)
            u0 = BASE["xq"]

            def x_max(h):
                dve.wait_ge(sem("x_scores"), h + 1)
                link(nc.vector.reduce_max(small[:, 22:24], halves(DB[h % 2][:]), AX))
                nc.vector.tensor_scalar(small[:, 24 + 2 * (h % 2):26 + 2 * (h % 2)], small[:, 22:24], -0.0625,
                                        None, ALU.mult).then_inc(sem("x_max"), 1)

            def x_probs(h):
                b = h % 2
                dve.wait_ge(sem("x_exp"), h + 1)
                link(nc.vector.reciprocal(small[:, 32:34], small[:, 28 + 2 * b:30 + 2 * b]))
                for t in range(NT):
                    ins = nc.vector.tensor_scalar(px[:, b, t, :], px[:, b, t, :], small[:, 32 + t:33 + t],
                                                  None, ALU.mult)
                ins.then_inc(sem("x_probs"), 1)

            def x_lo(h):
                dve.wait_ge(sem("x_hi"), h + 1)
                nc.vector.tensor_tensor(xTl[:, 2 * h:2 * h + 2, :], halves(DB[2 + h % 2][:]),
                                        xTh[:, 2 * h:2 * h + 2, :], ALU.subtract).then_inc(sem("x_lo"), 1)

            split(u0 + RING)
            x_max(0)
            split(u0 + 1 + RING)
            x_probs(0)
            x_max(1)
            split(u0 + 2 + RING)
            x_probs(1)
            x_max(2)
            split(u0 + 3 + RING)
            x_probs(2)
            x_lo(0)
            x_max(3)
            x_probs(3)
            x_lo(1)
            x_lo(2)
            x_lo(3)
            sum_splits("xo")
            post_norm(1, "xo", "p_x", 3)

            norm_rest(3, BASE["xo"] + 3)
            mlp(0)
            post_norm(2, "dn0", "p_ffn", 4)

            norm_rest(4, BASE["dn0"] + DN - 1)
            u0 = BASE["ev"]
            split(u0 + RING)
            split(u0 + 1 + RING)
            dve.wait_ge(bank_read[bank(u0 + 2)], bank_reads(u0 + 3)[bank(u0 + 2)])
            dve.wait_ge(sem("cmps_in"), 16)
            for kind in range(2):
                tok = kcT[:, kind, :].rearrange("p (m b) -> p m b", b=16)
                for a in range(2):
                    ins = nc.vector.tensor_tensor(
                        blk[:, kind, :, 16 * a:16 * a + 16], tok[:, a:a + NCMP, :],
                        same_rows(cmps[:, 32 * kind + 16 * a:32 * kind + 16 * a + 16], NCMP), ALU.add)
            ins.then_inc(sem("cmp_blocks"), 1)
            for j in range(2, 6):
                split(u0 + j + RING)
            dve.wait_ge(sem("rcos_in"), 16)
            dve.wait_ge(sem("rsin_in"), 16)
            qk = [rqT[:, 0:2, :], rqT[:, 2:4, :], rkT[:, 0:2, :], rkT[:, 2:4, :]]
            rope_cos(0, u0 + 6, qk[0], "_b")
            dve.wait_ge(sem("cmp_kv"), 1)
            for half in range(2):
                nc.vector.tensor_copy(kcm[64 * half:64 * half + 64, :, 0:NCMP],
                                      TB[0][0:64, 64:64 + 32].rearrange("p (g n) -> p g n", g=2)[:, :, 0:NCMP])
            nc.vector.tensor_copy(vcm[0:NCMP, :, :],
                                  TB[1][0:NCMP, 64:192].rearrange("p (g n) -> p g n", g=2))\
                .then_inc(sem("cmp_out"), 1)

            def n_max(s):
                t = s % 2
                kend = P * (t + 1)
                dve.wait_ge(sem("n_scores"), s + 1)
                if s >= 2:
                    dve.wait_ge(sem("n_tr"), s - 1)
                for br in range(2):
                    ins = nc.vector.tensor_tensor_reduce(
                        nsm[:, t, br, 0:kend], DB[t][:, 256 * br:256 * br + kend],
                        mask_full[:, 2 * P - kend:2 * P], 1.0, BIG_NEG, ALU.add, ALU.max,
                        small[:, 56 + 2 * t + br:57 + 2 * t + br])
                link(ins)
                nc.vector.tensor_scalar(small[:, 34 + 4 * t:36 + 4 * t], small[:, 56 + 2 * t:58 + 2 * t], -0.125,
                                        None, ALU.mult).then_inc(sem("n_max"), 1)

            def n_probs(s):
                h, t = s // 2, s % 2
                kend = P * (t + 1)
                dve.wait_ge(sem("n_exp"), s + 1)
                link(nc.vector.reciprocal(small[:, 52:54], small[:, 44 + 4 * t:46 + 4 * t]))
                link(nc.vector.tensor_tensor(
                    small[:, 54:56], small[:, 52:54],
                    gat[:, t, 8:24].rearrange("p (b h) -> p h b", b=2)[:, h, :], ALU.mult))
                for br in range(2):
                    ins = nc.vector.tensor_scalar(nsm[:, t, br, 0:kend], nsm[:, t, br, 0:kend],
                                                  small[:, 54 + br:55 + br], None, ALU.mult)
                ins.then_inc(sem("n_probs"), 1)

            def n_lo(hp):
                dve.wait_ge(sem("n_hi"), hp + 1)
                nc.vector.tensor_tensor(nl[:, hp, :], DB[2 + hp % 2][:, 0:S], nh[:, hp, :],
                                        ALU.subtract).then_inc(sem("n_lo"), 1)

            n_max(0)
            n_max(1)
            dve.wait_ge(sem("cmp_scores"), 1)
            a0 = CONST["cmpmask"][0]
            for par in range(2):
                ins = nc.vector.tensor_tensor(
                    pc[:, 8 * par:8 * par + 8, :].rearrange("p (h t) n -> p h (t n)", t=2),
                    TB[par][:, 256:256 + 8 * NCMP].rearrange("p (h n) -> p h n", h=4),
                    same_rows(cst[:, a0:a0 + 2 * NCMP], 4), ALU.add)
            link(ins)
            link(nc.vector.reduce_max(cmax[:], pc[:], AX))
            nc.vector.tensor_tensor(pc[:], pc[:], same_cols(cmax[:], NCMP), ALU.subtract)\
                .then_inc(sem("cmp_shift"), 1)
            n_probs(0)
            n_probs(1)
            gate0 = gat[:, :, 0:8]
            link(nc.vector.tensor_tensor(gate0, gate0, same_cols(const("cmpvalid"), 8), ALU.mult))
            dve.wait_ge(sem("cmp_exp"), 1)
            link(nc.vector.reduce_sum(ss[:, 0:16], pc[:], AX))
            link(nc.vector.reciprocal(ss[:, 0:16], ss[:, 0:16]))
            link(nc.vector.tensor_tensor(ss[:, 0:16].rearrange("p (a h t) -> p a h t", a=2, t=2),
                                         ss[:, 0:16].rearrange("p (a h t) -> p a h t", a=2, t=2),
                                         gate0.rearrange("p t (h a) -> p a h t", a=2), ALU.mult))
            nc.vector.tensor_tensor(pc[:], pc[:], same_cols(ss[:, 0:16], NCMP), ALU.mult)\
                .then_inc(sem("cmp_probs"), 1)
            split(u0 + 6 + RING)
            rope_turn(0, qk[0], braw, "_b")
            rope_cos(1, u0 + 7, qk[1], "_b")
            split(u0 + 7 + RING)

            for h in range(8):
                dve.wait_ge(sem("n_tr"), 2 * h + 2)
                if h >= 2:
                    dve.wait_ge(sem("n_out"), h - 1)
                nc.vector.tensor_copy(npT[:, h % 2, 1, :], TB[1][:, 0:384]).then_inc(sem("npT_b"), 1)
                if h < 7:
                    n_max(2 * h + 2)
                    n_max(2 * h + 3)
                if h < 3:
                    rope_turn(1 + h, qk[1 + h], braw, "_b")
                if h < 7:
                    n_probs(2 * h + 2)
                    n_probs(2 * h + 3)
                if h < 2:
                    rope_cos(2 + h, u0 + 8 + h, qk[2 + h], "_b")
                if h < 6:
                    split(u0 + 8 + h + RING)
                if h % 2 == 1:
                    n_lo(h // 2)

            def ret_decay(h):
                dve.wait_ge(sem("ret_scores"), h + 1)
                if h >= 2:
                    dve.wait_ge(sem("ret_out"), h - 1)
                nc.vector.tensor_tensor(rp[:, h % 2, :], DB[h % 2][:, 0:384], retd[:, h, :], ALU.mult)\
                    .then_inc(sem("ret_probs"), 1)

            def ret_copy(h):
                dve.wait_ge(sem("ret_out"), h + 1)
                nc.vector.tensor_copy(on[:].rearrange("p (t h) n -> p h t n", t=2)[:, h, :, :],
                                      halves(TB[h % 2][:, 0:256])).then_inc(sem("ret_nat"), 1)

            dve.wait_ge(sem("retd_in"), 16)
            ret_decay(0)
            ret_decay(1)
            ret_copy(0)
            ret_decay(2)
            ret_copy(1)
            ret_decay(3)
            ret_copy(2)
            ret_copy(3)
            dve.wait_ge(sem("ret_nat"), 4)
            link(nc.vector.reduce_sum(ss[:, 40:48], on[:], AX))
            link(nc.vector.tensor_scalar(ss[:, 40:48], ss[:, 40:48], 1.0 / P, None, ALU.mult))
            nc.vector.tensor_tensor(on[:], on[:], same_cols(ss[:, 40:48], P), ALU.subtract)\
                .then_inc(sem("gn_centred"), 1)
            split(BASE["eo"] + RING)
            dve.wait_ge(sem("gn_sq"), 1)
            link(nc.vector.reduce_sum(ss[:, 48:56], osq, AX))
            k = POW_COL["gn"]
            mean_square("gn", ss[:, 48:56], P, 1e-5)
            link(nc.vector.tensor_tensor(on[:], on[:], rg[:].rearrange("p t (h n) -> p (t h) n", n=P),
                                         ALU.mult))
            dve.wait_ge(rstd_ready, pow_at("gn") + 1)
            nc.vector.tensor_tensor(on[:], on[:], same_cols(rstd[:, k], P), ALU.mult)\
                .then_inc(sem("ret_normed"), 1)
            split(BASE["eo"] + 1 + RING)
            for hp in range(2):
                dve.wait_ge(sem("ret_hi"), hp + 1)
                nc.vector.tensor_tensor(xTl[:, 2 * hp:2 * hp + 2, :], halves(DB[hp][:]),
                                        xTh[:, 2 * hp:2 * hp + 2, :], ALU.subtract).then_inc(sem("ret_lo"), 1)
            split(BASE["eo"] + 2 + RING)
            add_sum("eo", 5, "f0")

            norm_rest(5, BASE["eo"] + 3)
            mlp(1)
            add_sum("dn1", 6, "o0")

            norm_rest(6, BASE["dn1"] + DN - 1)
            u0 = BASE["od"]
            nc.vector.memset(at[:], 0.0)
            for j in range(8):
                split(u0 + j + RING)
            dve.wait_ge(sem("hgm_in"), 16)
            t_of = {1: fT[:], 2: tot[:, 0:1024], 4: tot[:, 1024:1536], 8: tot[:, 0:256],
                    16: tot[:, 1024:1152], 32: tot[:, 0:64], 64: tot[:, 1024:1056]}

            def merge(idx, hg):
                dve.wait_ge(sem("hg_prod"), 2 * idx + hg + 1)
                q4, k4 = qd[:, 4 * hg:4 * hg + 4, :], kd[:, 4 * hg:4 * hg + 4, :]
                if idx == 0:
                    nc.vector.tensor_tensor(q4, q4, fT[:, 1024 * hg:1024 * hg + 1024]
                                            .rearrange("p (h n) -> p h n", h=4), ALU.mult)\
                        .then_inc(sem("hg_merged"), 1)
                    return
                s = LEVELS[idx - 1]
                nb = 1024 // (2 * s)
                tt = t_of[s][:, hg * 2 * nb:(hg + 1) * 2 * nb].rearrange("p (b two) -> p b two", two=2)
                qv = q4.rearrange("p h n -> p (h n)").rearrange("p (b two s) -> p b two s", two=2, s=s)
                kv = k4.rearrange("p h n -> p (h n)").rearrange("p (b two s) -> p b two s", two=2, s=s)
                nc.vector.tensor_tensor(qv[:, :, 1, :], qv[:, :, 1, :],
                                        tt[:, :, 0:1].broadcast_to([P, nb, s]), ALU.mult)
                if s < 64:
                    nc.vector.tensor_tensor(t_of[2 * s][:, hg * nb:(hg + 1) * nb], tt[:, :, 0], tt[:, :, 1],
                                            ALU.mult)
                nc.vector.tensor_tensor(kv[:, :, 0, :], kv[:, :, 0, :],
                                        tt[:, :, 1:2].broadcast_to([P, nb, s]), ALU.mult)\
                    .then_inc(sem("hg_merged"), 1)
                dve.wait_ge(sem("hg_merged"), 2 * idx + hg + 1)

            def keep(idx, hg):
                if idx == 8:
                    dve.wait_ge(sem("hg_prod"), 2 * idx + hg + 1)
                    nc.vector.tensor_copy(at[:, 4 * hg:4 * hg + 4, 2, :],
                                          DB[2 * hg][:].rearrange("p (h n) -> p h n", h=4))\
                        .then_inc(sem("hg_kept"), 1)
                    return
                for t in range(NT):
                    ins = nc.vector.copy_predicated(at[:, 4 * hg:4 * hg + 4, t, :],
                                                    same_rows(hgm[:, idx, :], 4),
                                                    DB[2 * hg + t][:].rearrange("p (h n) -> p h n", h=4))
                ins.then_inc(sem("hg_kept"), 1)

            for idx in range(9):
                for hg in range(2):
                    if idx < 8:
                        merge(idx, hg)
                    keep(idx, hg)
                if idx < 8:
                    split(u0 + 8 + idx + RING)
            for b in range(4):
                t, hh = b // 2, 4 * (b % 2)
                if b == 0:
                    dve.wait_ge(bank_read[0], bank_reads(u0 + 16)[0])
                    dve.wait_ge(bank_read[1], bank_reads(u0 + 16)[1])
                dve.wait_ge(sem("hg_sq"), b + 1)
                nc.vector.tensor_tensor(
                    oh[:, t, hh:hh + 4, :], DB[b][:].rearrange("p (h n) -> p h n", h=4),
                    gh[:, t, P * hh:P * hh + 512].rearrange("p (h n) -> p h n", h=4), ALU.mult)
                ins = nc.vector.reduce_sum(
                    ss[:, 4 * b:4 * b + 4], kd[:, 2 * b:2 * b + 2, :].rearrange("p a (c n) -> p (a c) n", n=P),
                    AX)
            link(ins)
            k = POW_COL["hg"]
            mean_square("hg", ss[:, 0:16], P)
            dve.wait_ge(rstd_ready, pow_at("hg") + 1)
            for t in range(NT):
                ins = nc.vector.tensor_tensor(oh[:, t, :, :], oh[:, t, :, :],
                                              same_cols(rstd[:, k.start + 8 * t:k.start + 8 * t + 8], P), ALU.mult)
            ins.then_inc(sem("hg_normed"), 1)
            for b in range(4):
                dve.wait_ge(sem("hg_hi"), b + 1)
                nc.vector.scalar_tensor_tensor(xTl[:, 2 * b:2 * b + 2, :], halves(DB[b][:]), gain("hgrn"),
                                               xTh[:, 2 * b:2 * b + 2, :], ALU.mult, ALU.subtract)\
                    .then_inc(sem("hg_lo"), 1)
            sum_splits("oo")
            add_sum("oo", 7, "f1")

            norm_rest(7, BASE["oo"] + 3)
            mlp(2)
            add_sum("dn2", 8, "fin")
            norm_mean(8, "fin", 1)
            dve.wait_ge(sem("gb_in"), 64)
            for t in range(NT):
                k = POW_COL[f"fin.{t}"]
                dve.wait_ge(rstd_ready, pow_at(f"fin.{t}") + 1)
                nc.vector.scalar_tensor_tensor(y[:, t, :], xn[:, t, :], rstd[:, k],
                                               gb[:], ALU.mult, ALU.mult).then_inc(sem("out_ready"), 1)

        @block.tensor
        def _(pe):
            def passes(out_, stat, mov, start, stop):
                (sh, sl), (mh, ml) = stat, mov
                nc.tensor.matmul(out_, sh, mh, start=start, stop=False)
                nc.tensor.matmul(out_, sh, ml, start=False, stop=False)
                return nc.tensor.matmul(out_, sl, mh, start=False, stop=stop)

            def wait_unit(u, i=None):
                k = 0 if i is None else i
                pe.wait_ge(lo_ready, k * RING + (u + 1))

            def wait_bank(u):
                n = bank_reads(u)[bank(u)]
                if n > 0:
                    pe.wait_ge(bank_read[bank(u)], n)

            def columns(u, act_h, act_l, ready=None):
                hi = whi[:, u % RING, :].rearrange("p (k n) -> p k n", k=KT)
                lo = wlo[:, u % RING, :].rearrange("p (k n) -> p k n", k=KT)
                for f in range(2):
                    for kt in range(KT):
                        if ready is not None and f == 0:
                            pe.wait_ge(ready[0], ready[1] + max(kt + 1, 2))
                        c = slice(P * f, P * f + P)
                        ins = passes(G[bank(u)][:, S * f:S * f + S], (hi[:, kt, c], lo[:, kt, c]),
                                     (act_h[:, kt, :], act_l[:, kt, :]), kt == 0, kt == KT - 1)
                return ins

            def rows(u, act_h, act_l, n=256):
                hi = whi[:, u % RING, 0:KT * n].rearrange("p (k n) -> p k n", k=KT)
                lo = wlo[:, u % RING, 0:KT * n].rearrange("p (k n) -> p k n", k=KT)
                for t in range(NT):
                    for kt in range(KT):
                        c = slice(P * t, P * t + P)
                        ins = passes(G[bank(u)][:, 256 * t:256 * t + n], (act_h[:, kt, c], act_l[:, kt, c]),
                                     (hi[:, kt, :], lo[:, kt, :]), kt == 0, kt == KT - 1)
                return ins

            def unit(u, kind, act_h=None, act_l=None, **kw):
                act_h = xTh if act_h is None else act_h
                act_l = xTl if act_l is None else act_l
                wait_unit(u)
                wait_bank(u)
                kind(u, act_h, act_l, **kw).then_inc(unit_done, 1)

            def norm_transposes(n, src=None):
                src = xn if src is None else src
                o = norm_banks(n)
                for t in range(NT):
                    pe.wait_ge(sem("diag_ready"), 2 * n + t + 1)
                    for kt in range(KT):
                        c = S * (kt % 2) + P * t
                        ins = nc.tensor.matmul(o[kt // 2][:, c:c + P], src[:, t, P * kt:P * kt + P], diag[:, t, :],
                                               start=True, stop=True)
                        if t == NT - 1 and kt % 2:
                            ins.then_inc(sem("norm_tr"), 1)

            def sum_unit(ph, j, act_h=None, act_l=None, first=None):
                act_h = xTh if act_h is None else act_h
                act_l = xTl if act_l is None else act_l
                u, last = BASE[ph] + j, N_OF[ph] - 1
                wait_unit(u)
                hi = whi[:, u % RING, :].rearrange("p (k n) -> p k n", k=2)
                lo = wlo[:, u % RING, :].rearrange("p (k n) -> p k n", k=2)
                if first is None:
                    first = 2 * (PAIRS[ph][j] if ph in PAIRS else j)
                for b, o in enumerate(sum_banks(ph)):
                    c, w = slice(P * (b // 2), P * (b // 2) + P), slice(512 * (b % 2), 512 * (b % 2) + 512)
                    for kk in range(2):
                        ins = passes(o[:], (act_h[:, first + kk, c], act_l[:, first + kk, c]),
                                     (hi[:, kk, w], lo[:, kk, w]), j == 0 and kk == 0, j == last and kk == 1)
                    if j == last and b < 3:
                        ins.then_inc(sem("sum_done"), 1)
                ins.then_inc(unit_done, 1)

            def rotate(j, m, buf, which):
                pe.wait_ge(sem("rope_raw" + which), j + 1)
                if which == "_b":
                    o, u = G[j % 2], BASE["ev"] + 6 + j
                    pe.wait_ge(bank_read[j % 2], bank_reads(u + 1)[j % 2])
                else:
                    o = TB[j % 2]
                    if j >= 2:
                        pe.wait_ge(sem("rope_done" + which), j - 1)
                nc.tensor.matmul(o[:], const(m), buf[:, j % 2, :], start=True, stop=True)\
                    .then_inc(sem("rope_rot" + which), 1)

            def mlp(f):
                u0, p0, n = BASE[f"gu{f}"], f * (GU // 2), [3, 5, 7][f]

                def pair(q, i=None):
                    k = 0 if i is None else i
                    for c, read in ((0, "silu_made"), (1, "h_made")):
                        u = u0 + 2 * q + c
                        wait_unit(u, i)
                        if i is not None or p0 + q >= 1:
                            pe.wait_ge(sem(read), k * 2 + (p0 + q))
                        first = i is None and q == 0 and c == 0
                        columns(u, xTh, xTl, ready=(sem("xT_ready"), KT * n) if first else None)\
                            .then_inc(unit_done, 1)

                for q in range(2):
                    pair(q)
                with pe.Fori(1, GU // 4) as i:
                    for q in range(2):
                        pair(q, i)
                for q in range(GU // 4 * 2, GU // 2):
                    pair(q)
                for d in range(DN):
                    pe.wait_ge(sem("h_lo"), p0 + d + 1)
                    sum_unit(f"dn{f}", d, hTh, hTl)

            pe.wait_ge(sem("cst_in"), 16)
            norm_transposes(0)
            u0 = BASE["in"]
            unit(u0, columns, ready=(sem("xT_ready"), 0))
            unit(u0 + 1, columns)
            rotate(0, "rot64", qraw, "_a")
            unit(u0 + 2, columns)
            rotate(1, "rot64", qraw, "_a")
            unit(u0 + 3, columns)
            rotate(2, "rot64", qraw, "_a")
            norm_transposes(1, y)
            unit(u0 + 4, rows)
            rotate(3, "rot64", qraw, "_a")
            unit(u0 + 5, rows)
            unit(u0 + 6, rows)
            unit(u0 + 7, rows)
            for b in range(2):
                pe.wait_ge(bank_read[b], bank_reads(u0 + 8)[b])
            pe.wait_ge(sem("xT_ready"), 16)
            pe.wait_ge(sem("poolm_in"), 16)
            pe.wait_ge(sem("wpool_in"), 16)
            for g in range(4):
                c = slice(P * g, P * g + P)
                o = halves(DB[g // 2][:])[:, g % 2, :]
                nc.tensor.matmul(o[:, 0:P], un[:, 0, c], poolm[:, g, 0:P], start=True, stop=True)
                nc.tensor.matmul(o[:, P:S], un[:, 0, c], poolm[:, g, P:2 * P], start=True, stop=False)
                ins = nc.tensor.matmul(o[:, P:S], un[:, 1, c], poolm[:, g, 2 * P:], start=False, stop=True)
                if g % 2:
                    ins.then_inc(sem("pooled"), 1)
            for g in range(4):
                if g % 2 == 0:
                    pe.wait_ge(sem("pooled_out"), g // 2 + 1)
                ins = nc.tensor.matmul(halves(DB[2 + g // 2][:])[:, g % 2, :], wpool[:, g, :],
                                       halves(qraw[:, g // 2, :])[:, g % 2, :], start=True, stop=True)
                if g % 2:
                    ins.then_inc(sem("pool_mix"), 1)

            def da_scores(s):
                h, t = s // 2, s % 2
                kend = P * (t + 1)
                if s == 0:
                    pe.wait_ge(sem("rope_done_a"), 4)
                    pe.wait_ge(sem("pool_lo"), 4)
                if s >= 2:
                    pe.wait_ge(sem("da_max"), s - 1)
                for m in range(2):
                    r = slice(64 * m, 64 * m + 64)
                    ins = nc.tensor.matmul(DB[2 * t + m][:, 0:kend], qT[r, h, P * t:P * t + P],
                                           kT[r, h, 0:kend], start=True, stop=True)
                ins.then_inc(sem("da_scores"), 1)

            def da_transposes(s):
                t = s % 2
                pe.wait_ge(sem("da_probs"), s + 1)
                if s >= 2:
                    pe.wait_ge(sem("da_nat"), s - 1)
                for b in range(t + 1):
                    ins = nc.tensor.transpose(TB[t][:, P * b:P * b + P], sm[:, t, 0, P * b:P * b + P], ident)
                ins.then_inc(sem("da_tr"), 1)

            def da_out(s):
                h, t = s // 2, s % 2
                pe.wait_ge(sem("aT"), s + 1)
                for b in range(t + 1):
                    ins = nc.tensor.matmul(TB[t][:, 256:384], aT[:, t, P * b:P * b + P],
                                           vn[:, b, P * h:P * h + P], start=(b == 0), stop=(b == t))
                ins.then_inc(sem("da_out"), 1)

            kv0 = BASE["kv"]
            da_scores(0)
            for s in range(8):
                unit(kv0 + s, columns if s < 4 else rows, memTh, memTl)
                if s >= 1:
                    da_out(s - 1)
                da_transposes(s)
                if s < 7:
                    da_scores(s + 1)
            da_out(7)

            def head_transposes(src, waits, signal, pairs):
                pe.wait_ge(*waits)
                for hp in range(pairs):
                    for h in (2 * hp, 2 * hp + 1):
                        for t in range(NT):
                            ins = nc.tensor.transpose(DB[hp][:, S * (h % 2) + P * t:S * (h % 2) + P * t + P],
                                                      src(t, h), ident)
                    ins.then_inc(signal, 1)

            for b in range(2):
                pe.wait_ge(bank_read[b], bank_reads(BASE["out"])[b])
            sum_unit("out", 0)
            sum_unit("out", 1)
            head_transposes(lambda t, h: un[:, t, P * h:P * h + P], (sem("da_normed"), 1), sem("da_T"), 2)
            for j in range(2):
                pe.wait_ge(sem("da_lo"), j + 1)
                sum_unit("out", 2 + j)

            norm_transposes(2)
            u0 = BASE["xq"]

            def x_scores(h):
                n = bank_reads(u0 + h + 1)
                pe.wait_ge(bank_read[bank(u0 + h)], n[bank(u0 + h)])
                if h == 0:
                    pe.wait_ge(sem("xT_ready"), 24)
                if h >= 2:
                    pe.wait_ge(sem("x_exp"), h - 1)
                for t in range(NT):
                    for dt in range(2):
                        ins = nc.tensor.matmul(halves(DB[h % 2][:])[:, t, :],
                                               xqT[:, 2 * h + dt, P * t:P * t + P], kxT[:, 2 * h + dt, :],
                                               start=(dt == 0), stop=(dt == 1))
                ins.then_inc(sem("x_scores"), 1)

            def x_transposes(h):
                pe.wait_ge(sem("x_probs"), h + 1)
                if h >= 2:
                    pe.wait_ge(sem("x_pT"), h - 1)
                for mt in range(2):
                    for t in range(NT):
                        ins = nc.tensor.transpose(TB[h % 2][:, S * mt + P * t:S * mt + P * t + P],
                                                  px[:, h % 2, t, P * mt:P * mt + P], ident)
                ins.then_inc(sem("x_tr"), 1)

            def x_out(h):
                pe.wait_ge(sem("x_pT"), h + 1)
                if h >= 2:
                    pe.wait_ge(sem("x_lo"), h - 1)
                for dt in range(2):
                    c = S * h + P * dt
                    for mt in range(2):
                        ins = nc.tensor.matmul(halves(DB[2 + h % 2][:])[:, dt, :], vx[:, mt, c:c + P],
                                               pxT[:, h % 2, mt, :], start=(mt == 0), stop=(mt == 1))
                ins.then_inc(sem("x_out"), 1)

            unit(u0, columns, ready=(sem("xT_ready"), 16))
            unit(u0 + 1, columns)
            x_scores(0)
            unit(u0 + 2, columns)
            x_scores(1)
            x_transposes(0)
            unit(u0 + 3, columns)
            x_scores(2)
            x_transposes(1)
            x_out(0)
            x_scores(3)
            x_transposes(2)
            x_out(1)
            x_transposes(3)
            x_out(2)
            x_out(3)
            pe.wait_ge(sem("x_exp"), 4)
            for j in range(4):
                pe.wait_ge(sem("x_lo"), j + 1)
                sum_unit("xo", j)

            norm_transposes(3)
            mlp(0)

            norm_transposes(4)
            u0 = BASE["ev"]

            def ret_scores(h):
                if h >= 2:
                    pe.wait_ge(sem("ret_probs"), h - 1)
                nc.tensor.matmul(DB[h % 2][:, 0:256], rkT[:, h, 0:P], rqT[:, h, :], start=True, stop=True)
                nc.tensor.matmul(DB[h % 2][:, 256:384], rkT[:, h, P:S], rqT[:, h, P:S], start=True, stop=True)\
                    .then_inc(sem("ret_scores"), 1)

            def ret_out(h):
                pe.wait_ge(sem("ret_probs"), h + 1)
                if h >= 2:
                    pe.wait_ge(sem("ret_nat"), h - 1)
                c = slice(P * h, P * h + P)
                o = TB[h % 2]
                nc.tensor.matmul(o[:, 0:P], rp[:, h % 2, 0:P], rv[:, 0, c], start=True, stop=True)
                nc.tensor.matmul(o[:, P:2 * P], rp[:, h % 2, P:2 * P], rv[:, 0, c], start=True, stop=False)
                nc.tensor.matmul(o[:, P:2 * P], rp[:, h % 2, 2 * P:3 * P], rv[:, 1, c], start=False, stop=True)\
                    .then_inc(sem("ret_out"), 1)

            unit(u0, columns, ready=(sem("xT_ready"), 32))
            for j in range(1, 4):
                unit(u0 + j, columns)
            unit(u0 + 4, rows)
            pe.wait_ge(sem("cmp_blocks"), 1)
            pe.wait_ge(sem("w1_in"), 16)
            for kind in range(2):
                for j in range(32):
                    for g in range(2):
                        r = slice(64 * g, 64 * g + 64)
                        ins = nc.tensor.matmul(TB[g][0:64, 16 * kind:16 * kind + NCMP], w1[r, kind, j, :],
                                               blk[r, kind, :, j], start=(j == 0), stop=(j == 31))
            ins.then_inc(sem("cmp_hid"), 1)
            unit(u0 + 5, rows, n=NG_COLS)
            unit(u0 + 6, columns)
            pe.wait_ge(sem("cmp_gelu"), 1)
            nc.tensor.matmul(TB[0][0:64, 64:96].rearrange("p (g n) -> p g n", g=2)[:, :, 0:NCMP],
                             cmps[0:64, 64:128], hid[0:64, 0, :, 0:NCMP], start=True, stop=True)
            for g in range(2):
                ins = nc.tensor.matmul(TB[1][0:NCMP, 64 + 64 * g:128 + 64 * g], hid[0:64, 1, g, 0:NCMP],
                                       cmps[0:64, 128:192], start=True, stop=True)
            ins.then_inc(sem("cmp_kv"), 1)
            def n_scores(s):
                h, t = s // 2, s % 2
                kend, g = P * (t + 1), h // 4
                r = slice(64 * (h % 2), 64 * (h % 2) + 64)
                if s >= 2:
                    pe.wait_ge(sem("n_max"), s - 1)
                for br in range(2):
                    ins = nc.tensor.matmul(DB[t][:, 256 * br:256 * br + kend], nqT[r, h // 2, P * t:P * t + P],
                                           ksT[r, br, g, 0:kend], start=True, stop=True)
                ins.then_inc(sem("n_scores"), 1)

            def n_transposes(s):
                h, t = s // 2, s % 2
                pe.wait_ge(sem("n_probs"), s + 1)
                if t == 0 and h >= 1:
                    pe.wait_ge(sem("npT_a"), h)
                    pe.wait_ge(sem("npT_b"), h)
                for br in range(2):
                    for b in range(t + 1):
                        c = P * t + P * b
                        ins = nc.tensor.transpose(TB[br][:, c:c + P], nsm[:, t, br, P * b:P * b + P], ident)
                ins.then_inc(sem("n_tr"), 1)

            def n_out(h):
                g, hp, par = h // 4, h // 2, h % 2
                r = slice(64 * par, 64 * par + 64)
                pe.wait_ge(sem("npT_a"), h + 1)
                pe.wait_ge(sem("npT_b"), h + 1)
                if hp >= 2 and par == 0:
                    pe.wait_ge(sem("n_lo"), hp - 1)
                o = DB[2 + hp % 2]
                idx = 8 * par + 2 * hp
                for br in range(2):
                    c = P * br + 64 * g
                    nc.tensor.matmul(o[r, 0:S], vsw[:, 0, c:c + 64], npT[:, h % 2, br, 0:S],
                                     start=(br == 0), stop=False)
                    nc.tensor.matmul(o[r, P:S], vsw[:, 1, c:c + 64], npT[:, h % 2, br, S:S + P],
                                     start=False, stop=False)
                nc.tensor.matmul(o[r, 0:S], vcm[0:NCMP, g, :], pcT[0:NCMP, idx:idx + 2, :]
                                 .rearrange("p a n -> p (a n)"), start=False, stop=True)\
                    .then_inc(sem("n_out"), 1)

            def cmp_transposes(b):
                if b >= 2:
                    pe.wait_ge(sem("pcT"), b - 1)
                o = DB[2 + b % 2]
                for k in range(4):
                    ins = nc.tensor.transpose(o[0:NCMP, P * k:P * k + P], pc[:, 4 * b + k, :], ident)
                ins.then_inc(sem("cmp_tr"), 1)

            n_scores(0)
            n_scores(1)
            pe.wait_ge(sem("cmp_out"), 1)
            for h in range(8):
                par, hp, g = h % 2, h // 2, h // 4
                r = slice(64 * par, 64 * par + 64)
                for t in range(NT):
                    c = 256 + (2 * hp + t) * NCMP
                    ins = nc.tensor.matmul(TB[par][:, c:c + NCMP], nqT[r, hp, P * t:P * t + P],
                                           kcm[r, g, 0:NCMP], start=True, stop=True)
            ins.then_inc(sem("cmp_scores"), 1)
            rotate(0, "rot128", braw, "_b")
            unit(u0 + 7, columns)
            pe.wait_ge(sem("cmp_probs"), 1)
            cmp_transposes(0)
            cmp_transposes(1)
            for h in range(8):
                if h < 7:
                    n_scores(2 * h + 2)
                    n_scores(2 * h + 3)
                n_transposes(2 * h)
                n_transposes(2 * h + 1)
                if h == 0:
                    cmp_transposes(2)
                    cmp_transposes(3)
                if h < 3:
                    rotate(1 + h, "rot128", braw, "_b")
                if h < 6:
                    if h < 4:
                        pe.wait_ge(sem("rope_done_b"), h + 1)
                    unit(u0 + 8 + h, columns if h < 2 else rows)
                if h == 0:
                    pe.wait_ge(sem("pcT"), 4)
                n_out(h)
            pe.wait_ge(bank_read[bank(u0 + 11)], bank_reads(u0 + 12)[bank(u0 + 11)])
            ret_scores(0)
            ret_scores(1)
            for b in range(2):
                pe.wait_ge(bank_read[b], bank_reads(BASE["eo"])[b])
            pe.wait_ge(sem("n_lo"), 4)
            sum_unit("eo", 0, nh, nl, 0)
            for h in range(4):
                ret_out(h)
                if h < 2:
                    ret_scores(h + 2)
            sum_unit("eo", 1, nh, nl, 2)
            head_transposes(lambda t, h: on[:, 4 * t + h, :], (sem("ret_normed"), 1), sem("ret_T"), 2)
            for j in range(2):
                pe.wait_ge(sem("ret_lo"), j + 1)
                sum_unit("eo", 2 + j)

            norm_transposes(5)
            mlp(1)

            norm_transposes(6)
            u0 = BASE["od"]
            unit(u0, columns, ready=(sem("xT_ready"), 48))
            for j in range(1, 8):
                unit(u0 + j, columns)

            def level(idx, hg):
                if idx == 0 and hg == 0:
                    for b in range(2):
                        pe.wait_ge(bank_read[b], bank_reads(u0 + 8)[b])
                    pe.wait_ge(sem("xT_ready"), 56)
                if idx >= 1:
                    pe.wait_ge(sem("hg_merged"), 2 * (idx - 1) + hg + 1)
                    pe.wait_ge(sem("hg_kept"), 2 * (idx - 1) + hg + 1)
                for h in range(4 * hg, 4 * hg + 4):
                    c = P * (h % 4)
                    if idx == 8:
                        ins = nc.tensor.matmul(DB[2 * hg][:, c:c + P], kd[:, h, 0:P], qd[:, h, P:S],
                                               start=True, stop=True)
                    else:
                        for t in range(NT):
                            tk = slice(P * t, P * t + P)
                            ins = nc.tensor.matmul(DB[2 * hg + t][:, c:c + P], kd[:, h, tk], qd[:, h, tk],
                                                   start=True, stop=True)
                ins.then_inc(sem("hg_prod"), 1)

            for idx in range(9):
                for hg in range(2):
                    level(idx, hg)
                if idx < 8:
                    unit(u0 + 8 + idx, rows)
            pe.wait_ge(sem("hg_kept"), 18)
            for b in range(2):
                pe.wait_ge(bank_read[b], bank_reads(u0 + 16)[b])
            for b in range(4):
                t = b // 2
                for h in range(4 * (b % 2), 4 * (b % 2) + 4):
                    o, c = DB[b][:, P * (h % 4):P * (h % 4) + P], slice(P * h, P * h + P)
                    if t == 0:
                        ins = nc.tensor.matmul(o, at[:, h, 0, :], vh[:, 0, c], start=True, stop=True)
                    else:
                        nc.tensor.matmul(o, at[:, h, 2, :], vh[:, 0, c], start=True, stop=False)
                        ins = nc.tensor.matmul(o, at[:, h, 1, :], vh[:, 1, c], start=False, stop=True)
                ins.then_inc(sem("hg_out"), 1)
            head_transposes(lambda t, h: oh[:, t, h, :], (sem("hg_normed"), 1), sem("hg_T"), 4)
            for j in range(4):
                pe.wait_ge(sem("hg_lo"), j + 1)
                sum_unit("oo", j)

            norm_transposes(7)
            mlp(2)


def _constants():
    p = np.arange(P)
    cf = np.zeros((P, N_CONST), np.float32)

    def put(name, a):
        at, n = CONST[name]
        cf[:, at:at + n] = a

    put("ident", np.eye(P))
    put("causal", np.where(p[None, :] <= p[:, None], 0.0, NEG))
    t = np.arange(S)
    ends = np.arange(NCMP) * 16 + 31
    m = np.where(ends[None, :] <= t[:, None], 0.0, NEG).reshape(NT, P, NCMP)
    put("cmpmask", m.transpose(1, 0, 2).reshape(P, NT * NCMP))
    put("cmpvalid", (t >= 31).astype(np.float32).reshape(NT, P).T)
    r64, r128 = np.zeros((P, P)), np.zeros((P, P))
    for b in (0, 64):
        for i in range(8):
            r64[b + i + 8, b + i] = -1.0
            r64[b + i, b + i + 8] = 1.0
    for i in range(64):
        r128[i + 64, i] = -1.0
        r128[i, i + 64] = 1.0
    put("rot64", r64)
    put("rot128", r128)
    freq = np.zeros((P, 1), np.float32)
    inv = (np.float32(500000.0) ** (-np.arange(0, 16, 2, dtype=np.float32) / np.float32(16))).astype(np.float32)
    for b in (0, 8, 64, 72):
        freq[b:b + 8, 0] = inv
    put("invfreq", freq)
    put("half", -0.5)

    pool = np.zeros((P, 4, 3 * P))
    for g, w in enumerate(POOL_WINDOWS):
        s_, t_ = np.arange(S)[:, None], np.arange(S)[None, :]
        full = np.where((s_ <= t_) & (s_ > t_ - w), 1.0 / np.minimum(t_ + 1, w), 0.0) - (s_ == t_)
        pool[:, g, 0:P] = full[0:P, 0:P]
        pool[:, g, P:2 * P] = full[0:P, P:]
        pool[:, g, 2 * P:] = full[P:, P:]

    inv2 = (np.float32(10000.0) ** (-np.arange(64, dtype=np.float32) / np.float32(64))).astype(np.float32)
    ang = (np.arange(S, dtype=np.float32)[None, :] * np.tile(inv2, 2)[:, None]).astype(np.float32)
    ret = np.zeros((P, 2 * S + 4 * 384))
    ret[:, 0:S], ret[:, S:2 * S] = np.cos(ang.astype(np.float64)), np.sin(ang.astype(np.float64))
    for h in range(4):
        lg = np.log(1.0 - 2.0 ** (-5.0 - h))
        diff = p[None, :] - p[:, None]
        diag = np.where(diff >= 0, np.exp(lg * np.maximum(diff, 0)), 0.0)
        off = np.exp(lg * (diff + P))
        ret[:, 2 * S + 384 * h:2 * S + 384 * (h + 1)] = np.concatenate([diag, off, diag], 1) * 128 ** -0.5

    hg = np.zeros((P, 8, P), np.int32)
    hg[:, 0, :] = np.eye(P)
    for i, s_ in enumerate(LEVELS):
        kb, qb = p[:, None] // s_, p[None, :] // s_
        hg[:, i + 1, :] = (kb // 2 == qb // 2) & (kb % 2 == 0) & (qb % 2 == 1)
    return cf, pool.astype(np.float32), ret.astype(np.float32), hg


def _wide(w):
    n = w.shape[1] // 256
    return w.reshape(KT, P, n, 256).transpose(2, 1, 0, 3).reshape(n, P, UNIT)


def _down(w):
    return w.reshape(DN, 2, P, D).transpose(0, 2, 1, 3).reshape(DN, P, UNIT)


def _sum(w, ph):
    return w.reshape(4, 2, P, D).transpose(0, 2, 1, 3).reshape(4, P, UNIT)[list(PAIRS[ph])]


def _stream(i):
    def gate_up(g, u):
        return np.stack([_wide(g), _wide(u)], 1).reshape(GU, P, UNIT)

    def cols(w, *ranges):
        return np.concatenate([w[:, a:b] for a, b in ranges], 1)

    ev = i["even_w_in_2"][0]
    ng = np.zeros((1, P, UNIT), np.float32)
    ng[0, :, 0:KT * NG_COLS] = ev[:, 3328:].reshape(KT, P, NG_COLS).transpose(1, 0, 2).reshape(P, -1)
    parts = [
        _wide(i["w_in"]), _wide(i["w_xkv"]), _sum(i["w_out"], "out"), _wide(i["w_xq"]), _sum(i["w_xo"], "xo"),
        gate_up(i["w_gate"], i["w_up"]), _down(i["w_down"]),
        _wide(ev[:, 2048:2816]), _wide(cols(ev, (2816, 2944), (3072, 3200))),
        _wide(cols(ev, (2944, 3072), (3200, 3328))), ng, _wide(ev[:, 0:2048]),
        _sum(i["even_w_out_2"][0], "eo"), gate_up(i["ffn_w1_2"][0], i["ffn_w3_2"][0]), _down(i["ffn_w2_2"][0]),
        _wide(i["odd_w_in_2"][0]), _sum(i["odd_w_out_2"][0], "oo"),
        gate_up(i["ffn_w1_2"][1], i["ffn_w3_2"][1]), _down(i["ffn_w2_2"][1]),
    ]
    out = np.concatenate(parts, 0)
    assert out.shape == (N_UNITS, P, UNIT)
    return out


def kernel(**inputs):
    import concourse.bacc as bacc
    from concourse.bass_utils import run_bass_kernel_spmd

    i = {k: np.asarray(v) for k, v in inputs.items()}
    gains = np.zeros((P, N_GAIN), np.float32)

    def put(name, a):
        at, n = GAIN[name]
        gains[:, at:at + n] = a

    for name, g in (("g_mix_pre", i["g_mix_pre"]), ("g_x_pre", i["g_x_pre"]), ("g_mem", i["g_mem"]),
                    ("g_ffn_pre", i["g_ffn_pre"]), ("mix0", i["norm_mix_g_2"][0]),
                    ("mix1", i["norm_mix_g_2"][1]), ("ffn0", i["norm_ffn_g_2"][0]),
                    ("ffn1", i["norm_ffn_g_2"][1])):
        put(name, g.reshape(KT, P).T)
    put("g_subln", i["g_subln"][:, None])
    put("hgrn", i["hgrn_norm_g_2"][0][:, None])
    put("pool_scale", i["pool_scale"].reshape(4, P).T)
    put("lam", np.concatenate([i["lambda_q1"], i["lambda_q2"], i["lambda_k1"], i["lambda_k2"]])[None, :])
    cf, pool, ret, hg = _constants()

    def both(a):
        return np.concatenate([a, a], 0)

    cmpw = np.stack([both(i[k][0].reshape(32, 64, 64).transpose(1, 0, 2))
                     for k in ("cmp_w1_k_2", "cmp_w1_v_2")], 1)
    cmps = np.concatenate([both(i["cmp_pos_k_2"][0].T), both(i["cmp_pos_v_2"][0].T),
                           both(i["cmp_w2_k_2"][0]), both(i["cmp_w2_v_2"][0])], 1)
    arrays = {
        "stream": _stream(i), "x": i["x"][0], "mem": i["mem"][0], "pos": i["positions"][0], "gains": gains,
        "rows": np.stack([i["g_mix_post"], i["g_x_post"], i["g_ffn_post"], i["final_norm_g_2"]]),
        "consts": cf, "poolm": pool, "wpool": i["w_pool"].transpose(1, 0, 2), "retm": ret, "hgm": hg,
        "cmpw": cmpw, "cmps": cmps,
    }
    arrays = {f"in_{k}": np.ascontiguousarray(v) for k, v in arrays.items()}
    nc = bacc.Bacc("TRN2", target_bir_lowering=False, num_devices=1)
    args = [nc.dram_tensor(k, v.shape, mybir.dt.from_np(v.dtype), kind="ExternalInput").ap()
            for k, v in arrays.items()]
    out = nc.dram_tensor("out", (S, D), F32, kind="ExternalOutput").ap()
    build(nc, *args, out)
    r = run_bass_kernel_spmd(nc, [arrays], core_ids=[0])
    return r.results[0]["out"].reshape(1, S, D)
```

```python
import math
from contextlib import ExitStack

import numpy as np
import concourse.bass as bass
from concourse import mybir

ALU = mybir.AluOpType
ACT = mybir.ActivationFunctionType
AX = mybir.AxisListType.X
F32 = mybir.dt.float32
F32R = mybir.dt.float32r
I32 = mybir.dt.int32

P = 128
D = 1024
S = 256
NT = S // P
KT = D // P
EPS = 1e-6
NEG = -1.0e30
BIG_NEG = -3.0e38
FF = 2816
FT = FF // P
UNIT = 2048
RING = 4
HEADS_NSA = 8
LAM_INIT = 0.8 - 0.6 * math.exp(-0.3 * 0)
NCMP = S // 16 - 1
POOL_WINDOWS = (2, 4, 8, 16)
LEVELS = (1, 2, 4, 8, 16, 32, 64)
DK_HG = 128

GU, DN = 2 * (FF // 256), FF // 256
PHASES = [("in", 8), ("kv", 8), ("out", 4), ("xq", 4), ("xo", 4), ("gu0", GU), ("dn0", DN),
          ("ev", 14), ("eo", 4), ("gu1", GU), ("dn1", DN), ("od", 16), ("oo", 4),
          ("gu2", GU), ("dn2", DN)]
BASE = {}
N_UNITS = 0
for _name, _n in PHASES:
    BASE[_name] = N_UNITS
    N_UNITS += _n
NG_UNIT = BASE["ev"] + 5
NG_COLS = 3 * HEADS_NSA
SUMS = {"out": ("D2", "D3", "G0", "G1"), "xo": ("G0", "G1", "D0", "D1"), "dn0": ("D0", "D1", "D2", "D3"),
        "eo": ("G0", "G1", "D2", "D3"), "dn1": ("D0", "D1", "D2", "D3"), "oo": ("G0", "G1", "T0", "T1"),
        "dn2": ("D0", "D1", "D2", "D3")}
PAIRS = {"out": (2, 3, 0, 1), "xo": (0, 1, 2, 3), "eo": (2, 3, 0, 1), "oo": (0, 1, 2, 3)}
N_OF = dict(PHASES)

POW_N = {"subln": 8, "gn": 8, "hg0": 8, "hg1": 8}
POWS = []
for _name in ("x0", "mem", "subln", "p_mix", "x1", "p_x", "x2", "p_ffn", "e0", "gn", "f0", "o0", "hg0",
              "hg1", "f1", "fin"):
    POWS += [_name] if _name in POW_N else [_name + ".0", _name + ".1"]
POW_COL = {}
_at = 0
for _name in POWS:
    POW_COL[_name] = slice(_at, _at + POW_N.get(_name, 1))
    _at += POW_N.get(_name, 1)
N_POW = _at

CONST = {}
_at = 0
for _name, _n in [("ident", 128), ("half", 8), ("zeros", 128), ("causal", 128), ("cmpmask", NT * NCMP),
                  ("cmpvalid", NT), ("rot64", 128), ("rot128", 128), ("invfreq", 1)]:
    CONST[_name] = (_at, _n)
    _at += _n
CONST_FIRST = CONST["zeros"][0]
N_CONST = _at
GAIN = {}
_at = 0
for _name, _n in [("g_mix_pre", KT), ("g_x_pre", KT), ("g_mem", KT), ("g_ffn_pre", KT), ("mix0", KT),
                  ("mix1", KT), ("ffn0", KT), ("ffn1", KT), ("g_subln", 1), ("hgrn", 1), ("pool_scale", 4),
                  ("lam", 256)]:
    GAIN[_name] = (_at, _n)
    _at += _n
N_GAIN = _at


def bank_reads(u):
    n = [0, 0]
    at = 0
    for name, count in PHASES:
        if not name.startswith("gu") and name not in SUMS:
            for j in range(min(max(u - at, 0), count)):
                n[j % 2] += 1
        at += count
    return n


def build(nc, stream, x_in, mem_in, pos_in, gains_in, rows_in, consts_in, poolm_in, wpool_in, retm_in,
          hgm_in, cmpw_in, cmps_in, out):
    ctx = ExitStack()
    sems = {}

    def sem(name):
        if name not in sems:
            sems[name] = ctx.enter_context(nc.semaphore(name))
        return sems[name]

    def sb(stack, name, shape, dt=F32):
        return stack.enter_context(nc.sbuf_tensor("s_" + name, shape, dt))

    with ctx:
        raw = sb(ctx, "raw", [P, RING, UNIT])
        whi = sb(ctx, "whi", [P, RING, UNIT], F32R)
        wlo = sb(ctx, "wlo", [P, RING, UNIT], F32R)
        xn = sb(ctx, "xn", [P, NT, D])
        y = sb(ctx, "y", [P, NT, D])
        xTh = sb(ctx, "xTh", [P, KT, S], F32R)
        xTl = sb(ctx, "xTl", [P, KT, S], F32R)
        cst = sb(ctx, "cst", [P, N_CONST])
        gains = sb(ctx, "gains", [P, N_GAIN])
        gb = sb(ctx, "gb", [P, D])
        ms = sb(ctx, "ms", [P, N_POW])
        rstd = sb(ctx, "rstd", [P, N_POW])
        cmax = sb(ctx, "cmax", [P, 16])
        ss = sb(ctx, "ss", [P, 64])
        small = sb(ctx, "small", [P, 64])
        diag = sb(ctx, "diag", [P, NT, P])

        def const(name):
            a, n = CONST[name]
            return cst[:, a:a + n]

        def gain(name, k=0):
            a, _ = GAIN[name]
            return gains[:, a + k:a + k + 1]

        ident = const("ident")
        mask_full = cst[:, CONST["zeros"][0]:CONST["zeros"][0] + 256]

        a_ = ExitStack()
        memTh = sb(a_, "memTh", [P, KT, S], F32R)
        memTl = sb(a_, "memTl", [P, KT, S], F32R)
        kxT = sb(a_, "kxT", [P, KT, S])
        vx = sb(a_, "vx", [P, NT, D])
        a2 = ExitStack()
        qT = sb(a2, "qT", [P, 4, S])
        kT = sb(a2, "kT", [P, 4, S])
        vn = sb(a2, "vn", [P, NT, 512])
        un = sb(a2, "un", [P, NT, 512])
        cosT = sb(a2, "cosT", [P, S])
        sinT = sb(a2, "sinT", [P, S])
        qraw = sb(a2, "qraw", [P, 2, 512])
        sm = sb(a2, "sm", [P, 2, 2, S])
        aT = sb(a2, "aT", [P, 2, 256])
        poolm = sb(a2, "poolm", [P, 4, 3 * P])
        wpool = aT[:].rearrange("p a (b n) -> p (a b) n", n=P)
        posi = sb(a2, "posi", [P, S], I32)
        a2.close()
        a3 = ExitStack()
        xqT = sb(a3, "xqT", [P, KT, S])
        px = sb(a3, "px", [P, 2, 2, S])
        pxT = sb(a3, "pxT", [P, 2, 2, S])
        a3.close()
        a_.close()
        f_ = ExitStack()
        hTh = sb(f_, "hTh", [P, FT, S], F32R)
        hTl = sb(f_, "hTl", [P, FT, S], F32R)
        sg = sb(f_, "sg", [P, 2, 512])
        hb = sb(f_, "hb", [P, 2, 512])
        f_.close()
        b_ = ExitStack()
        rqT = sb(b_, "rqT", [P, 4, S])
        rkT = sb(b_, "rkT", [P, 4, S])
        rv = sb(b_, "rv", [P, NT, 512])
        rg = sb(b_, "rg", [P, NT, 512])
        nqT = sb(b_, "nqT", [P, 4, S])
        kc2 = y[:].rearrange("p t n -> p (t n)")[:, 1024:2048].rearrange("p (k g n) -> p k g n", k=2, g=2)
        ksT = sb(b_, "ksT", [P, 2, 2, S])
        vsw = sb(b_, "vsw", [P, NT, 256])
        gat = sb(b_, "gat", [P, NT, NG_COLS])
        cmps = sb(b_, "cmps", [P, 32 + 128])
        hid = sb(b_, "hid", [64, 2, 2, 16])
        kcm = sb(b_, "kcm", [P, 2, 16])
        vcm = sb(b_, "vcm", [16, 2, 64])
        pc = sb(b_, "pc", [P, HEADS_NSA * NT, NCMP])
        braw = sb(b_, "braw", [P, 2, 512])
        rcos = sb(b_, "rcos", [P, S])
        rsin = sb(b_, "rsin", [P, S])
        retd = sb(b_, "retd", [P, 4, 384])
        on = sb(b_, "on", [P, NT * 4, P])
        rp = sb(b_, "rp", [P, 2, 384])
        b2 = ExitStack()
        w1 = sb(b2, "w1", [P, 2, 16, 64])
        blk = y[:].rearrange("p t n -> p (t n)")[:, 0:4 * NCMP * 16].rearrange("p (k g n j) -> p k g n j", k=2,
                                                                              g=2, j=16)
        b2.close()
        b4 = ExitStack()
        nsm = sb(b4, "nsm", [P, 2, 2, S])
        npT = sb(b4, "npT", [P, 2, 2, 384])
        nh = sb(b4, "nh", [P, 4, S], F32R)
        nl = sb(b4, "nl", [P, 4, S], F32R)
        gT = npT[0:NG_COLS, 0, 0, 0:S]
        pcT = y[0:16, :, :].rearrange("p t (k n) -> p (t k) n", n=P)
        b4.close()
        osq = braw[:].rearrange("p a (b n) -> p (a b) n", n=P)
        b_.close()
        c_ = ExitStack()
        qd = sb(c_, "qd", [P, 8, S])
        kd = sb(c_, "kd", [P, 8, S])
        fT = sb(c_, "fT", [P, 8 * S])
        tot = sb(c_, "tot", [P, 8 * S // 2 + 8 * S // 4])
        vh = sb(c_, "vh", [P, NT, D])
        gh = sb(c_, "gh", [P, NT, D])
        hgm = sb(c_, "hgm", [P, 8, P], I32)
        at = sb(c_, "at", [P, 8, 3, P])
        oh = qd[:].rearrange("p (t a) (b n) -> p t (a b) n", t=NT, n=P)
        c_.close()

        G = [ctx.enter_context(nc.psum_tensor(f"G{i}", [P, 512], F32)) for i in range(2)]
        DB = [ctx.enter_context(nc.psum_tensor(f"D{i}", [P, 512], F32)) for i in range(4)]
        TB = [ctx.enter_context(nc.psum_tensor(f"T{i}", [P, 512], F32)) for i in range(2)]

        hi_ready, lo_ready, unit_done = sem("hi_ready"), sem("lo_ready"), sem("unit_done")
        landed = [sem(f"raw_landed{i}") for i in range(RING)]
        bank_read = [sem("bank_read0"), sem("bank_read1")]
        ms_ready, rstd_ready = sem("ms_ready"), sem("rstd_ready")
        NORMS = [("g_mix_pre", "x0", None), ("g_mem", "mem", None), ("g_x_pre", "x1", 1),
                 ("g_ffn_pre", "x2", 2), ("mix0", "e0", 3), ("ffn0", "f0", 4), ("mix1", "o0", 5),
                 ("ffn1", "f1", 6)]

        def halves(ap):
            return ap.rearrange("p (a b) -> p a b", a=2)

        def same_rows(ap, n):
            return ap.rearrange("p (a b) -> p a b", a=1).broadcast_to([P, n, ap.shape[-1]])

        def second_blocks(ap, s):
            return ap.rearrange("p (b two s) -> p b two s", two=2, s=s)[:, :, 1, :]

        def same_cols(ap, n):
            return ap.rearrange("p (a b) -> p a b", b=1).broadcast_to([P, ap.shape[-1], n])

        def bank(u):
            base = max(b for b in BASE.values() if b <= u)
            return (u - base) % 2

        def pow_at(name):
            return POWS.index(name)

        banks = {f"{k}{i}": b[i] for k, b in (("G", G), ("D", DB), ("T", TB)) for i in range(len(b))}

        def sum_banks(ph):
            return [banks[k] for k in SUMS[ph]]

        def norm_banks(n):
            ph = {2: "out", 3: "xo", 4: "dn0", 5: "eo", 6: "dn1", 7: "oo"}.get(n)
            return DB if ph is None else [b for k, b in banks.items() if k not in SUMS[ph]]

        def wait_sum(eng, ph, c):
            if c < 3:
                eng.wait_ge(sem("sum_done"), 3 * list(SUMS).index(ph) + c + 1)
            else:
                eng.wait_ge(unit_done, BASE[ph] + N_OF[ph])

        def chunk(t_, c):
            return t_[:, c // 2, 512 * (c % 2):512 * (c % 2) + 512]

        block = ctx.enter_context(nc.Block())

        @block.sync
        def _(sp):
            for t in range(NT):
                sp.dma_start(xn[:, t, :], x_in[t * P:(t + 1) * P, :]).then_inc(sem(f"x_in{t}"), 16)
            sp.dma_start(cst[:, 0:CONST_FIRST], consts_in[:, 0:CONST_FIRST]).then_inc(sem("cst_first_in"), 16)
            for j in range(RING):
                sp.dma_start(raw[:, j, :], stream[j, :, :]).then_inc(landed[j], 16)
                if j == 1:
                    sp.dma_start(cst[:, CONST_FIRST:], consts_in[:, CONST_FIRST:]).then_inc(sem("cst_in"), 16)
            with sp.Fori(1, N_UNITS // RING) as i:
                for j in range(RING):
                    sp.wait_ge(lo_ready, i * RING + (j - RING + 1))
                    sp.dma_start(raw[:, j, :], stream[bass.ds(i * RING + j, 1), :, :]
                                 .rearrange("a p n -> p (a n)")).then_inc(landed[j], 16)
            for u in range(N_UNITS // RING * RING, N_UNITS):
                sp.wait_ge(lo_ready, u - RING + 1)
                sp.dma_start(raw[:, u % RING, :], stream[u, :, :]).then_inc(landed[u % RING], 16)
            for c in range(4):
                sp.wait_ge(sem("out_ready"), c + 1)
                sp.dma_start(out[c // 2 * P:c // 2 * P + P, 512 * (c % 2):512 * (c % 2) + 512], chunk(y, c))\
                    .then_inc(sem("stored"), 16)
            sp.wait_ge(sem("stored"), 16 * 4)

        @block.gpsimd
        def _(pool):
            pool.dma_start(posi[:], pos_in.partition_broadcast(P)).then_inc(sem("pos_in"), 16)
            pool.dma_start(gains[:], gains_in).then_inc(sem("gains_in"), 16)
            pool.wait_ge(sem("cst_first_in"), 16)

            def power(name):
                c, n = POW_COL[name], POW_N.get(name, 1)
                pool.wait_ge(ms_ready, pow_at(name) + 1)
                nc.gpsimd.tensor_tensor(rstd[:, c], ms[:, c], const("half")[:, 0:n],
                                        ALU.pow).then_inc(rstd_ready, 1)

            def load_row(r, version):
                pool.wait_ge(sem("x_part"), 4 * version)
                pool.dma_start(gb[:], rows_in[r, :].partition_broadcast(P)).then_inc(sem("gb_in"), 16)

            power("x0.0")
            power("x0.1")
            pool.wait_ge(sem("norm_sq"), 4)
            pool.wait_ge(lo_ready, 5)
            pool.dma_start(y[:], mem_in.rearrange("(t p) d -> p t d", p=P)).then_inc(sem("mem_in"), 16)
            pool.dma_start(gb[:], rows_in[0, :].partition_broadcast(P)).then_inc(sem("gb_in"), 16)
            pool.dma_start(poolm[:], poolm_in).then_inc(sem("poolm_in"), 16)
            pool.dma_start(wpool, wpool_in).then_inc(sem("wpool_in"), 16)
            power("mem.0")
            power("mem.1")
            power("subln")
            power("p_mix.0")
            power("p_mix.1")
            power("x1.0")
            power("x1.1")
            load_row(1, 1)
            power("p_x.0")
            power("p_x.1")
            power("x2.0")
            power("x2.1")
            load_row(2, 2)
            power("p_ffn.0")
            power("p_ffn.1")
            power("e0.0")
            power("e0.1")
            load_row(3, 3)
            pool.dma_start(rcos[:], retm_in[:, 0:S]).then_inc(sem("rcos_in"), 16)
            pool.dma_start(rsin[:], retm_in[:, S:2 * S]).then_inc(sem("rsin_in"), 16)
            pool.dma_start(retd[:], retm_in[:, 2 * S:].rearrange("p (h n) -> p h n", h=4))\
                .then_inc(sem("retd_in"), 16)
            pool.dma_start(w1[:], cmpw_in).then_inc(sem("w1_in"), 16)
            pool.dma_start(cmps[:], cmps_in).then_inc(sem("cmps_in"), 16)
            power("gn")
            power("f0.0")
            power("f0.1")
            power("o0.0")
            power("o0.1")
            pool.wait_ge(sem("x_part"), 4 * 5)
            pool.dma_start(hgm[:], hgm_in).then_inc(sem("hgm_in"), 16)
            power("hg0")
            power("hg1")
            power("f1.0")
            power("f1.1")
            power("fin.0")
            power("fin.1")

        @block.scalar
        def _(act):
            def split(u, i=None):
                if u >= N_UNITS:
                    return
                k = 0 if i is None else i
                act.wait_ge(landed[u % RING], k * 16 + 16 * (u // RING + 1))
                if u >= RING:
                    act.wait_ge(unit_done, k * RING + (u - RING + 1))
                n = KT * NG_COLS if u == NG_UNIT else UNIT
                nc.scalar.activation(whi[:, u % RING, 0:n], raw[:, u % RING, 0:n], ACT.Copy)\
                    .then_inc(hi_ready, 1)

            def norm_squares(n, src, scratch, version=None, parts=range(4)):
                for c in parts:
                    if version is not None:
                        act.wait_ge(sem("x_part"), 4 * (version - 1) + c + 1)
                    if n == 0 and c % 2 == 0:
                        act.wait_ge(sem(f"x_in{c // 2}"), 16)
                    nc.scalar.activation(scratch(c), chunk(src, c), ACT.Square, scale=D ** -0.5,
                                         accum_out=ss[:, 16 + c:17 + c]).then_inc(sem("norm_sq"), 1)

            def norm_hi(n, dst):
                for kt in range(KT):
                    if kt % 2 == 0:
                        act.wait_ge(sem("norm_tr"), 4 * n + kt // 2 + 1)
                    nc.scalar.activation(dst[:, kt, :], halves(norm_banks(n)[kt // 2][:])[:, kt % 2, :], ACT.Copy,
                                         scale=gain(NORMS[n][0], kt)).then_inc(sem("norm_hi"), 1)

            def norm(n, last, parts=range(4)):
                norm_squares(n, xn, lambda c: chunk(y, c), NORMS[n][2], parts)
                norm_hi(n, xTh)
                split(last - 1 + RING)
                split(last + RING)

            def evac(u, dst, func=ACT.Copy, scale=1.0):
                act.wait_ge(unit_done, u + 1)
                nc.scalar.activation(dst, halves(G[bank(u)][:]), func, scale=scale)\
                    .then_inc(bank_read[bank(u)], 1)

            def rope_raw(j, u, buf, which):
                act.wait_ge(unit_done, u + 1)
                if j >= 2:
                    act.wait_ge(sem("rope_done" + which), j - 1)
                nc.scalar.activation(buf[:, j % 2, :], G[bank(u)][:], ACT.Copy)\
                    .then_inc(sem("rope_raw" + which), 1)

            def post_squares(k0, ph, n):
                for c in range(4):
                    if c == 3:
                        norm_squares(n, xn, lambda c: chunk(y, c), NORMS[n][2], range(1))
                    wait_sum(act, ph, c)
                    nc.scalar.activation(chunk(y, c), sum_banks(ph)[c][:], ACT.Square, scale=D ** -0.5,
                                         accum_out=ss[:, 24 + c:25 + c]).then_inc(sem("post_sq"), 1)

            def sum_splits(ph):
                for j in range(N_OF[ph] - 2):
                    split(BASE[ph] + j + RING)

            def mlp(f):
                u0, p0 = BASE[f"gu{f}"], f * (GU // 2)

                def pair(q, i=None):
                    k = 0 if i is None else i
                    act.wait_ge(unit_done, k * 4 + (u0 + 2 * q + 1))
                    if i is not None or p0 + q >= 2:
                        act.wait_ge(sem("h_made"), k * 2 + (p0 + q - 1))
                    nc.scalar.activation(sg[:, q % 2, :], G[0][:], ACT.Silu).then_inc(sem("silu_made"), 1)
                    split(u0 + 2 * q + RING, i)
                    split(u0 + 2 * q + 1 + RING, i)
                    act.wait_ge(sem("h_made"), k * 2 + (p0 + q + 1))
                    dst = hTh[:, 2 * q:2 * q + 2, :] if i is None else hTh[:, bass.ds(i * 4 + 2 * q, 2), :]
                    nc.scalar.activation(dst, halves(hb[:, q % 2, :]), ACT.Copy).then_inc(sem("h_hi"), 1)

                for q in range(2):
                    pair(q)
                with act.Fori(1, GU // 4) as i:
                    for q in range(2):
                        pair(q, i)
                for q in range(GU // 4 * 2, GU // 2):
                    pair(q)
                sum_splits(f"dn{f}")

            norm_squares(0, xn, lambda c: chunk(y, c), parts=range(2))
            split(0)
            act.wait_ge(sem("gains_in"), 16)
            norm_hi(0, xTh)
            for j in range(1, 4):
                split(j)
            u0 = BASE["in"]
            evac(u0, vn[:, :, 0:256])
            split(u0 + RING)
            evac(u0 + 1, vn[:, :, 256:512])
            split(u0 + 1 + RING)
            act.wait_ge(sem("angles"), 2)
            nc.scalar.activation(sinT[:], sinT[:], ACT.Sin).then_inc(sem("trig"), 1)
            nc.scalar.activation(cosT[:], cosT[:], ACT.Sin).then_inc(sem("trig"), 1)
            for j in range(2):
                evac(u0 + 2 + j, un[:, :, 256 * j:256 * j + 256])
                split(u0 + 2 + j + RING)
            act.wait_ge(sem("mem_in"), 16)
            mem_scratch = kxT[:].rearrange("p (c k) n -> p c (k n)", c=4)
            norm_squares(1, y, lambda c: mem_scratch[:, c, :])
            rope_raw(0, u0 + 4, qraw, "_a")
            split(u0 + 4 + RING)
            rope_raw(1, u0 + 5, qraw, "_a")
            split(u0 + 5 + RING)
            norm_hi(1, memTh)
            rope_raw(2, u0 + 6, qraw, "_a")
            split(u0 + 6 + RING)
            for gp in range(2):
                act.wait_ge(sem("pooled"), gp + 1)
                nc.scalar.activation(sm[:, gp, :, :], halves(DB[gp][:]), ACT.Copy).then_inc(sem("pooled_out"), 1)
            rope_raw(3, u0 + 7, qraw, "_a")
            for g in range(4):
                if g % 2 == 0:
                    act.wait_ge(sem("pool_mix"), g // 2 + 1)
                nc.scalar.activation(xTh[:, 4 + g, :], halves(DB[2 + g // 2][:])[:, g % 2, :], ACT.Copy,
                                     scale=gain("pool_scale", g)).then_inc(sem("pool_hi"), 1)
            split(u0 + 7 + RING)
            act.wait_ge(sem("lam_dots"), 1)
            nc.scalar.activation(small[:, 2:4], small[:, 0:2], ACT.Exp).then_inc(sem("lam_exp"), 1)

            def exps(s):
                kend = P * (s % 2 + 1)
                act.wait_ge(sem("da_max"), s + 1)
                for m in range(2):
                    ins = nc.scalar.activation(sm[:, s % 2, m, 0:kend], sm[:, s % 2, m, 0:kend], ACT.Exp,
                                               bias=small[:, 8 + 2 * (s % 2) + m:9 + 2 * (s % 2) + m],
                                               scale=0.125,
                                               accum_out=small[:, 12 + 2 * (s % 2) + m:13 + 2 * (s % 2) + m])
                ins.then_inc(sem("da_exp"), 1)

            kv0 = BASE["kv"]

            def kv_evac(j):
                if j < 4:
                    evac(kv0 + j, kxT[:, 2 * j:2 * j + 2, :])
                else:
                    evac(kv0 + j, vx[:, :, 256 * (j - 4):256 * (j - 3)])

            kv_evac(0)
            split(kv0 + RING)
            exps(0)
            exps(1)
            for s in range(8):
                if s < 7:
                    kv_evac(s + 1)
                act.wait_ge(sem("da_tr"), s + 1)
                if s >= 2:
                    act.wait_ge(sem("da_out"), s - 1)
                n = P * (s % 2 + 1)
                nc.scalar.activation(aT[:, s % 2, 0:n], TB[s % 2][:, 0:n], ACT.Copy).then_inc(sem("aT"), 1)
                if s < 6:
                    exps(s + 2)
                if s < 7:
                    split(kv0 + 1 + s + RING)
            act.wait_ge(sem("da_nat"), 8)
            nc.scalar.activation(sm[:].rearrange("p a b n -> p (a b n)"), un[:].rearrange("p t n -> p (t n)"),
                                 ACT.Square).then_inc(sem("da_sq"), 1)
            split(BASE["out"] + RING)
            for hp in range(2):
                act.wait_ge(sem("da_T"), hp + 1)
                nc.scalar.activation(xTh[:, 2 * hp:2 * hp + 2, :], halves(DB[hp][:]), ACT.Copy,
                                     scale=small[:, 20:21]).then_inc(sem("da_hi"), 1)
            split(BASE["out"] + 1 + RING)
            post_squares(0, "out", 2)

            norm(2, BASE["out"] + 3, range(1, 4))
            u0 = BASE["xq"]

            def x_exp(h):
                act.wait_ge(sem("x_max"), h + 1)
                for t in range(NT):
                    ins = nc.scalar.activation(px[:, h % 2, t, :], halves(DB[h % 2][:])[:, t, :], ACT.Exp,
                                               bias=small[:, 24 + 2 * (h % 2) + t:25 + 2 * (h % 2) + t],
                                               scale=0.0625,
                                               accum_out=small[:, 28 + 2 * (h % 2) + t:29 + 2 * (h % 2) + t])
                ins.then_inc(sem("x_exp"), 1)

            def x_T(h):
                act.wait_ge(sem("x_tr"), h + 1)
                if h >= 2:
                    act.wait_ge(sem("x_out"), h - 1)
                nc.scalar.activation(pxT[:, h % 2, :, :], halves(TB[h % 2][:]), ACT.Copy)\
                    .then_inc(sem("x_pT"), 1)

            def x_hi(h):
                act.wait_ge(sem("x_out"), h + 1)
                nc.scalar.activation(xTh[:, 2 * h:2 * h + 2, :], halves(DB[2 + h % 2][:]), ACT.Copy)\
                    .then_inc(sem("x_hi"), 1)

            evac(u0, xqT[:, 0:2, :])
            split(u0 + RING)
            evac(u0 + 1, xqT[:, 2:4, :])
            split(u0 + 1 + RING)
            x_exp(0)
            evac(u0 + 2, xqT[:, 4:6, :])
            split(u0 + 2 + RING)
            x_exp(1)
            x_T(0)
            evac(u0 + 3, xqT[:, 6:8, :])
            split(u0 + 3 + RING)
            x_exp(2)
            x_T(1)
            x_hi(0)
            x_exp(3)
            x_T(2)
            x_hi(1)
            x_T(3)
            x_hi(2)
            x_hi(3)
            sum_splits("xo")
            post_squares(1, "xo", 3)

            norm(3, BASE["xo"] + 3, range(1, 4))
            mlp(0)
            post_squares(2, "dn0", 4)

            norm(4, BASE["dn0"] + DN - 1, range(1, 4))
            u0 = BASE["ev"]
            for j in range(2):
                evac(u0 + j, nqT[:, 2 * j:2 * j + 2, :])
                split(u0 + j + RING)
            act.wait_ge(unit_done, u0 + 3)
            for half in range(2):
                for g in range(2):
                    ins = nc.scalar.activation(kc2[64 * half:64 * half + 64, :, g, :],
                                               halves(G[bank(u0 + 2)][64 * g:64 * g + 64, :]), ACT.Copy)
            ins.then_inc(bank_read[bank(u0 + 2)], 1)
            split(u0 + 2 + RING)
            act.wait_ge(unit_done, u0 + 4)
            for half in range(2):
                for g in range(2):
                    ins = nc.scalar.activation(ksT[64 * half:64 * half + 64, :, g, :],
                                               halves(G[bank(u0 + 3)][64 * g:64 * g + 64, :]), ACT.Copy)
            ins.then_inc(bank_read[bank(u0 + 3)], 1)
            split(u0 + 3 + RING)
            evac(u0 + 4, vsw[:])
            split(u0 + 4 + RING)
            act.wait_ge(sem("cmp_hid"), 1)
            for kind in range(2):
                ins = nc.scalar.activation(hid[0:64, kind, :, 0:NCMP],
                                           TB[kind][0:64, 0:2 * NCMP].rearrange("p (g n) -> p g n", g=2),
                                           ACT.Gelu_apprx_tanh)
            ins.then_inc(sem("cmp_gelu"), 1)
            act.wait_ge(unit_done, u0 + 6)
            nc.scalar.activation(gT, G[bank(u0 + 5)][0:NG_COLS, 0:S], ACT.Sigmoid)\
                .then_inc(bank_read[bank(u0 + 5)], 1)
            split(u0 + 5 + RING)
            rope_raw(0, u0 + 6, braw, "_b")
            split(u0 + 6 + RING)

            def n_exp(s):
                t = s % 2
                kend = P * (t + 1)
                act.wait_ge(sem("n_max"), s + 1)
                for br in range(2):
                    ins = nc.scalar.activation(nsm[:, t, br, 0:kend], nsm[:, t, br, 0:kend], ACT.Exp,
                                               bias=small[:, 34 + 4 * t + br:35 + 4 * t + br], scale=0.125,
                                               accum_out=small[:, 44 + 4 * t + br:45 + 4 * t + br])
                ins.then_inc(sem("n_exp"), 1)

            def n_hi(hp):
                act.wait_ge(sem("n_out"), 2 * hp + 2)
                nc.scalar.activation(nh[:, hp, :], DB[2 + hp % 2][:, 0:S], ACT.Copy)\
                    .then_inc(sem("n_hi"), 1)

            def pcT_half(b):
                act.wait_ge(sem("cmp_tr"), b + 1)
                nc.scalar.activation(pcT[0:NCMP, 4 * b:4 * b + 4, :],
                                     DB[2 + b % 2][0:NCMP, :].rearrange("p (k n) -> p k n", k=4), ACT.Copy)\
                    .then_inc(sem("pcT"), 1)

            n_exp(0)
            n_exp(1)
            act.wait_ge(sem("cmp_shift"), 1)
            nc.scalar.activation(pc[:], pc[:], ACT.Exp, scale=0.125).then_inc(sem("cmp_exp"), 1)
            rope_raw(1, u0 + 7, braw, "_b")
            split(u0 + 7 + RING)
            pcT_half(0)
            pcT_half(1)
            for h in range(8):
                act.wait_ge(sem("n_tr"), 2 * h + 2)
                if h >= 2:
                    act.wait_ge(sem("n_out"), h - 1)
                nc.scalar.activation(npT[:, h % 2, 0, :], TB[0][:, 0:384], ACT.Copy)\
                    .then_inc(sem("npT_a"), 1)
                if h == 0:
                    pcT_half(2)
                    pcT_half(3)
                if h < 7:
                    n_exp(2 * h + 2)
                    n_exp(2 * h + 3)
                u = u0 + 8 + h
                if h < 2:
                    rope_raw(2 + h, u, braw, "_b")
                elif h < 4:
                    evac(u, rv[:, :, 256 * (h - 2):256 * (h - 1)])
                if h < 5:
                    split(u + RING)
                if h % 2 == 1:
                    n_hi(h // 2)
            for j in range(2):
                evac(u0 + 12 + j, rg[:, :, 256 * j:256 * j + 256], ACT.Silu)
            act.wait_ge(sem("gn_centred"), 1)
            nc.scalar.activation(osq, on[:], ACT.Square).then_inc(sem("gn_sq"), 1)
            split(u0 + 13 + RING)
            split(BASE["eo"] + RING)
            for hp in range(2):
                act.wait_ge(sem("ret_T"), hp + 1)
                nc.scalar.activation(xTh[:, 2 * hp:2 * hp + 2, :], halves(DB[hp][:]), ACT.Copy)\
                    .then_inc(sem("ret_hi"), 1)
            split(BASE["eo"] + 1 + RING)

            norm(5, BASE["eo"] + 3)
            mlp(1)

            norm(6, BASE["dn1"] + DN - 1)
            u0 = BASE["od"]
            for j in range(4):
                evac(u0 + j, qd[:, 2 * j:2 * j + 2, :], ACT.Silu)
                split(u0 + j + RING)
            for j in range(4):
                u = u0 + 4 + j
                act.wait_ge(unit_done, u + 1)
                nc.scalar.activation(fT[:, 512 * j:512 * j + 512], G[bank(u)][:], ACT.Sigmoid)\
                    .then_inc(sem("f_made"), 1)
                evac(u, kd[:, 2 * j:2 * j + 2, :], ACT.Sigmoid, scale=-1.0)
                split(u + RING)
            for j in range(4):
                evac(u0 + 8 + j, vh[:, :, 256 * j:256 * j + 256], ACT.Copy, scale=DK_HG ** -0.5)
                split(u0 + 8 + j + RING)
            for j in range(4):
                evac(u0 + 12 + j, gh[:, :, 256 * j:256 * j + 256], ACT.Sigmoid)
                if j < 2:
                    split(u0 + 12 + j + RING)
            for b in range(4):
                act.wait_ge(sem("hg_out"), b + 1)
                nc.scalar.activation(kd[:, 2 * b:2 * b + 2, :], halves(DB[b][:]), ACT.Square)\
                    .then_inc(sem("hg_sq"), 1)
            split(u0 + 14 + RING)

            def hg_hi(b):
                act.wait_ge(sem("hg_T"), b + 1)
                nc.scalar.activation(xTh[:, 2 * b:2 * b + 2, :], halves(DB[b][:]), ACT.Copy,
                                     scale=gain("hgrn")).then_inc(sem("hg_hi"), 1)

            hg_hi(0)
            hg_hi(1)
            hg_hi(2)
            hg_hi(3)
            split(u0 + 15 + RING)
            sum_splits("oo")

            norm(7, BASE["oo"] + 3)
            mlp(2)
            norm_squares(8, xn, lambda c: chunk(y, c), 7)

        @block.vector
        def _(dve):
            chain = [0]

            def link(ins):
                chain[0] += 1
                ins.then_inc(sem("dve_chain"), 1)
                dve.wait_ge(sem("dve_chain"), chain[0])

            def split(u, i=None):
                if u >= N_UNITS:
                    return
                k = 0 if i is None else i
                dve.wait_ge(hi_ready, k * RING + (u + 1))
                n = KT * NG_COLS if u == NG_UNIT else UNIT
                nc.vector.tensor_tensor(wlo[:, u % RING, 0:n], raw[:, u % RING, 0:n],
                                        whi[:, u % RING, 0:n], ALU.subtract).then_inc(lo_ready, 1)

            def mean_square(name, sums, count, eps=EPS):
                nc.vector.tensor_scalar(ms[:, POW_COL[name]], sums, 1.0 / count, eps, ALU.mult, ALU.add)\
                    .then_inc(ms_ready, 1)

            def tile_mean(name, t, at_):
                nc.vector.scalar_tensor_tensor(ms[:, POW_COL[f"{name}.{t}"]], ss[:, at_ + 2 * t:at_ + 2 * t + 1],
                                               EPS, ss[:, at_ + 2 * t + 1:at_ + 2 * t + 2], ALU.add, ALU.add)\
                    .then_inc(ms_ready, 1)

            def norm_mean(n, name, t):
                dve.wait_ge(sem("norm_sq"), 4 * n + 2 * t + 2 if n else 4)
                tile_mean(name, t, 16)

            def norm_diag(name, t):
                k = POW_COL[f"{name}.{t}"]
                dve.wait_ge(rstd_ready, pow_at(f"{name}.{t}") + 1)
                nc.vector.tensor_scalar(diag[:, t, :], ident, rstd[:, k], None, ALU.mult)\
                    .then_inc(sem("diag_ready"), 1)

            def norm_lo(n, dst_h, dst_l):
                for kt in range(KT):
                    if kt % 2 == 0:
                        dve.wait_ge(sem("norm_hi"), KT * n + kt + 2)
                    nc.vector.scalar_tensor_tensor(
                        dst_l[:, kt, :], halves(norm_banks(n)[kt // 2][:])[:, kt % 2, :], gain(NORMS[n][0], kt),
                        dst_h[:, kt, :], ALU.mult, ALU.subtract).then_inc(sem("xT_ready"), 1)

            def norm_rest(n, last):
                name = NORMS[n][1]
                norm_mean(n, name, 1)
                norm_diag(name, 1)
                norm_lo(n, xTh, xTl)
                split(last - 1 + RING)
                split(last + RING)

            def rope_turn(j, dst, buf, which):
                dve.wait_ge(sem("rope_rot" + which), j + 1)
                sin = sinT if which == "_a" else rsin
                link(nc.vector.tensor_tensor(halves(buf[:, j % 2, :]), halves((TB if which == "_a" else G)[j % 2][:]),
                                             same_rows(sin[:], 2), ALU.mult))
                nc.vector.tensor_tensor(dst, dst, halves(buf[:, j % 2, :]), ALU.add)\
                    .then_inc(sem("rope_done" + which), 1)

            def rope_cos(j, u, dst, which):
                dve.wait_ge(sem("rope_raw" + which), j + 1)
                cos = cosT if which == "_a" else rcos
                nc.vector.tensor_tensor(dst, halves(G[bank(u)][:]), same_rows(cos[:], 2), ALU.mult)\
                    .then_inc(bank_read[bank(u)], 1)

            def post_norm(k0, ph, name, n):
                o = sum_banks(ph)

                def gained(c):
                    dve.wait_ge(sem("post_sq"), 4 * k0 + c + 1)
                    ins = nc.vector.tensor_tensor(chunk(y, c), o[c][:], gb[:, 512 * (c % 2):512 * (c % 2) + 512],
                                                  ALU.mult)
                    if c % 2:
                        link(ins)

                def update(c):
                    k = POW_COL[f"{name}.{c // 2}"]
                    dve.wait_ge(rstd_ready, pow_at(f"{name}.{c // 2}") + 1)
                    nc.vector.scalar_tensor_tensor(chunk(xn, c), chunk(y, c), rstd[:, k], chunk(xn, c),
                                                   ALU.mult, ALU.add).then_inc(sem("x_part"), 1)

                dve.wait_ge(sem("gb_in"), 16 * (k0 + 1))
                gained(0)
                dve.wait_ge(sem("post_sq"), 4 * k0 + 2)
                tile_mean(name, 0, 24)
                gained(1)
                update(0)
                gained(2)
                update(1)
                dve.wait_ge(sem("post_sq"), 4 * k0 + 4)
                tile_mean(name, 1, 24)
                gained(3)
                norm_mean(n, NORMS[n][1], 0)
                update(2)
                norm_diag(NORMS[n][1], 0)
                update(3)

            def add_sum(ph, n, name):
                for c in range(4):
                    wait_sum(dve, ph, c)
                    nc.vector.tensor_tensor(chunk(xn, c), sum_banks(ph)[c][:], chunk(xn, c), ALU.add)\
                        .then_inc(sem("x_part"), 1)
                    if c == 1:
                        norm_mean(n, name, 0)
                    if c == 2 and n < 8:
                        norm_diag(name, 0)

            def sum_splits(ph):
                for j in range(N_OF[ph] - 2):
                    split(BASE[ph] + j + RING)

            def mlp(f):
                u0, p0 = BASE[f"gu{f}"], f * (GU // 2)

                def pair(q, i=None):
                    k = 0 if i is None else i
                    dve.wait_ge(sem("silu_made"), k * 2 + (p0 + q + 1))
                    dve.wait_ge(unit_done, k * 4 + (u0 + 2 * q + 2))
                    if i is not None or p0 + q >= 2:
                        dve.wait_ge(sem("h_hi"), k * 2 + (p0 + q - 1))
                    nc.vector.tensor_tensor(hb[:, q % 2, :], G[1][:], sg[:, q % 2, :], ALU.mult)\
                        .then_inc(sem("h_made"), 1)
                    split(u0 + 2 * q + RING, i)
                    split(u0 + 2 * q + 1 + RING, i)
                    dve.wait_ge(sem("h_hi"), k * 2 + (p0 + q + 1))
                    at_ = slice(2 * q, 2 * q + 2) if i is None else bass.ds(i * 4 + 2 * q, 2)
                    nc.vector.tensor_tensor(hTl[:, at_, :], halves(hb[:, q % 2, :]), hTh[:, at_, :],
                                            ALU.subtract).then_inc(sem("h_lo"), 1)

                for q in range(2):
                    pair(q)
                with dve.Fori(1, GU // 4) as i:
                    for q in range(2):
                        pair(q, i)
                for q in range(GU // 4 * 2, GU // 2):
                    pair(q)
                sum_splits(f"dn{f}")

            dve.wait_ge(sem("x_in1"), 16)
            for c in range(2, 4):
                nc.vector.tensor_tensor_reduce(chunk(y, c), chunk(xn, c), chunk(xn, c), 1.0 / D, 0.0,
                                               ALU.mult, ALU.add, ss[:, 16 + c:17 + c])\
                    .then_inc(sem("norm_sq"), 1)
            norm_mean(0, "x0", 0)
            norm_mean(0, "x0", 1)
            dve.wait_ge(sem("cst_first_in"), 16)
            norm_diag("x0", 0)
            norm_diag("x0", 1)
            split(0)
            dve.wait_ge(sem("gains_in"), 16)
            norm_lo(0, xTh, xTl)
            split(1)
            split(2)
            dve.wait_ge(sem("pos_in"), 16)
            dve.wait_ge(sem("cst_in"), 16)
            two_pi = 2.0 * math.pi
            c1, c2 = 201 / 32, 2029 / 2 ** 20
            c3 = two_pi - c1 - c2
            magic = 12582912.0
            ang, turns = qraw[:, 0, 0:S], qraw[:, 1, 0:S]
            link(nc.vector.tensor_copy(ang, posi[:]))
            link(nc.vector.tensor_scalar(ang, ang, const("invfreq"), None, ALU.mult))

            def angle(out_, shift, turn):
                link(nc.vector.tensor_scalar(turns, ang, 1.0 / two_pi, turn, ALU.mult, ALU.add))
                link(nc.vector.tensor_scalar(turns, turns, magic, None, ALU.add))
                link(nc.vector.tensor_scalar(turns, turns, -magic, None, ALU.add))
                link(nc.vector.scalar_tensor_tensor(out_[:], turns, -c1, ang, ALU.mult, ALU.add))
                link(nc.vector.scalar_tensor_tensor(out_[:], turns, -c2, out_[:], ALU.mult, ALU.add))
                link(nc.vector.scalar_tensor_tensor(out_[:], turns, -c3, out_[:], ALU.mult, ALU.add))
                link(nc.vector.tensor_scalar(out_[:], out_[:], shift, 3.1415925, ALU.add, ALU.min))
                nc.vector.tensor_scalar(out_[:], out_[:], -3.1415925, None, ALU.max).then_inc(sem("angles"), 1)

            angle(sinT, 0.0, 0.0)
            split(3)
            u0 = BASE["in"]
            split(u0 + RING)
            split(u0 + 1 + RING)
            dve.wait_ge(sem("angles"), 1)
            angle(cosT, math.pi / 2, 0.25)
            for j in range(2):
                split(u0 + 2 + j + RING)
            norm_mean(1, "mem", 0)
            norm_mean(1, "mem", 1)
            norm_diag("mem", 0)
            norm_diag("mem", 1)
            lam = gains[:, GAIN["lam"][0]:GAIN["lam"][0] + 256]
            link(nc.vector.tensor_tensor(lam[:, 0:P], lam[:, 0:P], lam[:, P:2 * P], ALU.mult))
            nc.vector.reduce_sum(small[:, 0:2], halves(lam[:, 0:P]), AX).then_inc(sem("lam_dots"), 1)
            link(nc.vector.tensor_scalar(small[:, 20:21], gain("g_subln"), 1.0 - LAM_INIT, None, ALU.mult))

            dve.wait_ge(sem("trig"), 2)
            qk = [qT[:, 0:2, :], qT[:, 2:4, :], kT[:, 0:2, :], kT[:, 2:4, :]]
            for j in range(4):
                rope_cos(j, u0 + 4 + j, qk[j], "_a")
                if j >= 1:
                    rope_turn(j - 1, qk[j - 1], qraw, "_a")
                if j == 3:
                    for g in range(4):
                        if g % 2 == 0:
                            dve.wait_ge(sem("pool_hi"), g + 2)
                        nc.vector.scalar_tensor_tensor(xTl[:, 4 + g, :], halves(DB[2 + g // 2][:])[:, g % 2, :],
                                                       gain("pool_scale", g), xTh[:, 4 + g, :], ALU.mult,
                                                       ALU.subtract).then_inc(sem("pool_lo"), 1)
                split(u0 + 4 + j + RING)
                if j == 1:
                    norm_lo(1, memTh, memTl)
            rope_turn(3, qk[3], qraw, "_a")
            dve.wait_ge(sem("lam_exp"), 1)
            link(nc.vector.scalar_tensor_tensor(small[:, 4:5], small[:, 3:4], -LAM_INIT, small[:, 2:3],
                                                ALU.add, ALU.subtract))

            def maxes(s):
                kend, b = P * (s % 2 + 1), s % 2
                dve.wait_ge(sem("da_scores"), s + 1)
                if s >= 2:
                    dve.wait_ge(sem("da_tr"), s - 1)
                for m in range(2):
                    ins = nc.vector.tensor_tensor_reduce(
                        sm[:, b, m, 0:kend], DB[2 * b + m][:, 0:kend], mask_full[:, 2 * P - kend:2 * P],
                        1.0, BIG_NEG, ALU.add, ALU.max, small[:, 36 + 2 * b + m:37 + 2 * b + m])
                link(ins)
                nc.vector.tensor_scalar(small[:, 8 + 2 * b:10 + 2 * b], small[:, 36 + 2 * b:38 + 2 * b], -0.125,
                                        None, ALU.mult)\
                    .then_inc(sem("da_max"), 1)

            kv0 = BASE["kv"]
            def probs(s):
                kend, b = P * (s % 2 + 1), s % 2
                dve.wait_ge(sem("da_exp"), s + 1)
                inv, lam_inv = small[:, 40 + 4 * b:42 + 4 * b], small[:, 42 + 4 * b:43 + 4 * b]
                link(nc.vector.reciprocal(inv, small[:, 12 + 2 * b:14 + 2 * b]))
                link(nc.vector.tensor_scalar(lam_inv, inv[:, 1:2], small[:, 4:5], None, ALU.mult))
                link(nc.vector.tensor_scalar(sm[:, b, 1, 0:kend], sm[:, b, 1, 0:kend], lam_inv, None, ALU.mult))
                nc.vector.scalar_tensor_tensor(sm[:, b, 0, 0:kend], sm[:, b, 0, 0:kend], inv[:, 0:1],
                                               sm[:, b, 1, 0:kend], ALU.mult, ALU.add)\
                    .then_inc(sem("da_probs"), 1)

            def da_copy(s):
                h, t = s // 2, s % 2
                dve.wait_ge(sem("da_out"), s + 1)
                nc.vector.tensor_copy(un[:, t, P * h:P * h + P], TB[t][:, 256:384]).then_inc(sem("da_nat"), 1)

            split(kv0 + RING)
            maxes(0)
            maxes(1)
            probs(0)
            probs(1)
            for s in range(8):
                if s >= 1:
                    da_copy(s - 1)
                if s < 6:
                    maxes(s + 2)
                if s < 6:
                    split(kv0 + 1 + s + RING)
                    probs(s + 2)
            da_copy(7)
            dve.wait_ge(sem("da_sq"), 1)
            heads = un[:].rearrange("p t (h n) -> p (t h) n", n=P)
            link(nc.vector.reduce_sum(ss[:, 32:40], sm[:].rearrange("p a b n -> p (a b n)")
                                      .rearrange("p (k n) -> p k n", n=P), AX))
            k = POW_COL["subln"]
            mean_square("subln", ss[:, 32:40], P)
            split(BASE["out"] - 1 + RING)
            dve.wait_ge(rstd_ready, pow_at("subln") + 1)
            nc.vector.tensor_tensor(heads, heads, same_cols(rstd[:, k], P), ALU.mult)\
                .then_inc(sem("da_normed"), 1)
            for hp in range(2):
                dve.wait_ge(sem("da_hi"), hp + 1)
                nc.vector.scalar_tensor_tensor(xTl[:, 2 * hp:2 * hp + 2, :], halves(DB[hp][:]),
                                               small[:, 20:21], xTh[:, 2 * hp:2 * hp + 2, :], ALU.mult,
                                               ALU.subtract).then_inc(sem("da_lo"), 1)
            split(BASE["out"] + RING)
            split(BASE["out"] + 1 + RING)
            post_norm(0, "out", "p_mix", 2)

            norm_rest(2, BASE["out"] + 3)
            u0 = BASE["xq"]

            def x_max(h):
                dve.wait_ge(sem("x_scores"), h + 1)
                link(nc.vector.reduce_max(small[:, 22:24], halves(DB[h % 2][:]), AX))
                nc.vector.tensor_scalar(small[:, 24 + 2 * (h % 2):26 + 2 * (h % 2)], small[:, 22:24], -0.0625,
                                        None, ALU.mult).then_inc(sem("x_max"), 1)

            def x_probs(h):
                b = h % 2
                dve.wait_ge(sem("x_exp"), h + 1)
                link(nc.vector.reciprocal(small[:, 32:34], small[:, 28 + 2 * b:30 + 2 * b]))
                for t in range(NT):
                    ins = nc.vector.tensor_scalar(px[:, b, t, :], px[:, b, t, :], small[:, 32 + t:33 + t],
                                                  None, ALU.mult)
                ins.then_inc(sem("x_probs"), 1)

            def x_lo(h):
                dve.wait_ge(sem("x_hi"), h + 1)
                nc.vector.tensor_tensor(xTl[:, 2 * h:2 * h + 2, :], halves(DB[2 + h % 2][:]),
                                        xTh[:, 2 * h:2 * h + 2, :], ALU.subtract).then_inc(sem("x_lo"), 1)

            split(u0 + RING)
            x_max(0)
            split(u0 + 1 + RING)
            x_probs(0)
            x_max(1)
            split(u0 + 2 + RING)
            x_probs(1)
            x_max(2)
            split(u0 + 3 + RING)
            x_probs(2)
            x_lo(0)
            x_max(3)
            x_probs(3)
            x_lo(1)
            x_lo(2)
            x_lo(3)
            sum_splits("xo")
            post_norm(1, "xo", "p_x", 3)

            norm_rest(3, BASE["xo"] + 3)
            mlp(0)
            post_norm(2, "dn0", "p_ffn", 4)

            norm_rest(4, BASE["dn0"] + DN - 1)
            u0 = BASE["ev"]
            split(u0 + RING)
            split(u0 + 1 + RING)
            dve.wait_ge(bank_read[bank(u0 + 2)], bank_reads(u0 + 3)[bank(u0 + 2)])
            dve.wait_ge(sem("cmps_in"), 16)
            for half in range(2):
                r = slice(64 * half, 64 * half + 64)
                for kind in range(2):
                    tok = kc2[r, kind, :, :].rearrange("p g (m c two) -> p g m c two", c=8, two=2)
                    for a in range(2):
                        term = cmps[r, 16 * kind + 8 * a:16 * kind + 8 * a + 8]
                        ins = nc.vector.tensor_tensor(
                            blk[r, kind, :, :, 8 * a:8 * a + 8], tok[:, :, a:a + NCMP, :, half],
                            term.rearrange("p (a b c) -> p a b c", a=1, b=1).broadcast_to([64, 2, NCMP, 8]), ALU.add)
            ins.then_inc(sem("cmp_blocks"), 1)
            for j in range(2, 6):
                split(u0 + j + RING)
            dve.wait_ge(sem("rcos_in"), 16)
            dve.wait_ge(sem("rsin_in"), 16)
            qk = [rqT[:, 0:2, :], rqT[:, 2:4, :], rkT[:, 0:2, :], rkT[:, 2:4, :]]
            rope_cos(0, u0 + 6, qk[0], "_b")
            dve.wait_ge(sem("cmp_kv"), 1)
            for half in range(2):
                nc.vector.tensor_copy(kcm[64 * half:64 * half + 64, :, 0:NCMP],
                                      TB[0][0:64, 64:64 + 32].rearrange("p (g n) -> p g n", g=2)[:, :, 0:NCMP])
            nc.vector.tensor_copy(vcm[0:NCMP, :, :],
                                  TB[1][0:NCMP, 64:192].rearrange("p (g n) -> p g n", g=2))\
                .then_inc(sem("cmp_out"), 1)
            dve.wait_ge(sem("gates_T"), 1)
            nc.vector.tensor_copy(gat[:], G[1][:, 0:NT * NG_COLS].rearrange("p (t n) -> p t n", t=NT))\
                .then_inc(sem("gates_read"), 1)
            dve.wait_ge(sem("gates_read"), 1)

            def n_max(s):
                t = s % 2
                kend = P * (t + 1)
                dve.wait_ge(sem("n_scores"), s + 1)
                if s >= 2:
                    dve.wait_ge(sem("n_tr"), s - 1)
                for br in range(2):
                    ins = nc.vector.tensor_tensor_reduce(
                        nsm[:, t, br, 0:kend], DB[t][:, 256 * br:256 * br + kend],
                        mask_full[:, 2 * P - kend:2 * P], 1.0, BIG_NEG, ALU.add, ALU.max,
                        small[:, 56 + 2 * t + br:57 + 2 * t + br])
                link(ins)
                nc.vector.tensor_scalar(small[:, 34 + 4 * t:36 + 4 * t], small[:, 56 + 2 * t:58 + 2 * t], -0.125,
                                        None, ALU.mult).then_inc(sem("n_max"), 1)

            def n_probs(s):
                h, t = s // 2, s % 2
                kend = P * (t + 1)
                dve.wait_ge(sem("n_exp"), s + 1)
                link(nc.vector.reciprocal(small[:, 52:54], small[:, 44 + 4 * t:46 + 4 * t]))
                link(nc.vector.tensor_tensor(
                    small[:, 54:56], small[:, 52:54],
                    gat[:, t, 8:24].rearrange("p (b h) -> p h b", b=2)[:, h, :], ALU.mult))
                for br in range(2):
                    ins = nc.vector.tensor_scalar(nsm[:, t, br, 0:kend], nsm[:, t, br, 0:kend],
                                                  small[:, 54 + br:55 + br], None, ALU.mult)
                ins.then_inc(sem("n_probs"), 1)

            def n_lo(hp):
                dve.wait_ge(sem("n_hi"), hp + 1)
                nc.vector.tensor_tensor(nl[:, hp, :], DB[2 + hp % 2][:, 0:S], nh[:, hp, :],
                                        ALU.subtract).then_inc(sem("n_lo"), 1)

            n_max(0)
            n_max(1)
            dve.wait_ge(sem("cmp_scores"), 1)
            a0 = CONST["cmpmask"][0]
            for par in range(2):
                ins = nc.vector.tensor_tensor(
                    pc[:, 8 * par:8 * par + 8, :].rearrange("p (h t) n -> p h (t n)", t=2),
                    TB[par][:, 256:256 + 8 * NCMP].rearrange("p (h n) -> p h n", h=4),
                    same_rows(cst[:, a0:a0 + 2 * NCMP], 4), ALU.add)
            link(ins)
            link(nc.vector.reduce_max(cmax[:], pc[:], AX))
            nc.vector.tensor_tensor(pc[:], pc[:], same_cols(cmax[:], NCMP), ALU.subtract)\
                .then_inc(sem("cmp_shift"), 1)
            n_probs(0)
            n_probs(1)
            gate0 = gat[:, :, 0:8]
            link(nc.vector.tensor_tensor(gate0, gate0, same_cols(const("cmpvalid"), 8), ALU.mult))
            dve.wait_ge(sem("cmp_exp"), 1)
            link(nc.vector.reduce_sum(ss[:, 0:16], pc[:], AX))
            link(nc.vector.reciprocal(ss[:, 0:16], ss[:, 0:16]))
            link(nc.vector.tensor_tensor(ss[:, 0:16].rearrange("p (a h t) -> p a h t", a=2, t=2),
                                         ss[:, 0:16].rearrange("p (a h t) -> p a h t", a=2, t=2),
                                         gate0.rearrange("p t (h a) -> p a h t", a=2), ALU.mult))
            nc.vector.tensor_tensor(pc[:], pc[:], same_cols(ss[:, 0:16], NCMP), ALU.mult)\
                .then_inc(sem("cmp_probs"), 1)
            split(u0 + 6 + RING)
            rope_turn(0, qk[0], braw, "_b")
            rope_cos(1, u0 + 7, qk[1], "_b")
            split(u0 + 7 + RING)

            for h in range(8):
                dve.wait_ge(sem("n_tr"), 2 * h + 2)
                if h >= 2:
                    dve.wait_ge(sem("n_out"), h - 1)
                nc.vector.tensor_copy(npT[:, h % 2, 1, :], TB[1][:, 0:384]).then_inc(sem("npT_b"), 1)
                if h < 7:
                    n_max(2 * h + 2)
                    n_max(2 * h + 3)
                if h < 3:
                    rope_turn(1 + h, qk[1 + h], braw, "_b")
                if h < 7:
                    n_probs(2 * h + 2)
                    n_probs(2 * h + 3)
                if h < 2:
                    rope_cos(2 + h, u0 + 8 + h, qk[2 + h], "_b")
                if h < 5:
                    split(u0 + 8 + h + RING)
                if h % 2 == 1 and h < 7:
                    n_lo(h // 2)

            def ret_decay(h):
                dve.wait_ge(sem("ret_scores"), h + 1)
                if h >= 2:
                    dve.wait_ge(sem("ret_out"), h - 1)
                nc.vector.tensor_tensor(rp[:, h % 2, :], DB[h % 2][:, 0:384], retd[:, h, :], ALU.mult)\
                    .then_inc(sem("ret_probs"), 1)

            def ret_copy(h):
                dve.wait_ge(sem("ret_out"), h + 1)
                nc.vector.tensor_copy(on[:].rearrange("p (t h) n -> p h t n", t=2)[:, h, :, :],
                                      halves(TB[h % 2][:, 0:256])).then_inc(sem("ret_nat"), 1)

            dve.wait_ge(sem("retd_in"), 16)
            ret_decay(0)
            ret_decay(1)
            n_lo(3)
            ret_copy(0)
            ret_decay(2)
            ret_copy(1)
            ret_decay(3)
            ret_copy(2)
            ret_copy(3)
            dve.wait_ge(sem("ret_nat"), 4)
            link(nc.vector.reduce_sum(ss[:, 40:48], on[:], AX))
            link(nc.vector.tensor_scalar(ss[:, 40:48], ss[:, 40:48], 1.0 / P, None, ALU.mult))
            nc.vector.tensor_tensor(on[:], on[:], same_cols(ss[:, 40:48], P), ALU.subtract)\
                .then_inc(sem("gn_centred"), 1)
            dve.wait_ge(sem("gn_sq"), 1)
            link(nc.vector.reduce_sum(ss[:, 48:56], osq, AX))
            k = POW_COL["gn"]
            mean_square("gn", ss[:, 48:56], P, 1e-5)
            link(nc.vector.tensor_tensor(on[:], on[:], rg[:].rearrange("p t (h n) -> p (t h) n", n=P),
                                         ALU.mult))
            dve.wait_ge(rstd_ready, pow_at("gn") + 1)
            nc.vector.tensor_tensor(on[:], on[:], same_cols(rstd[:, k], P), ALU.mult)\
                .then_inc(sem("ret_normed"), 1)
            split(u0 + 13 + RING)
            for hp in range(2):
                dve.wait_ge(sem("ret_hi"), hp + 1)
                nc.vector.tensor_tensor(xTl[:, 2 * hp:2 * hp + 2, :], halves(DB[hp][:]),
                                        xTh[:, 2 * hp:2 * hp + 2, :], ALU.subtract).then_inc(sem("ret_lo"), 1)
            split(BASE["eo"] + RING)
            split(BASE["eo"] + 1 + RING)
            add_sum("eo", 5, "f0")

            norm_rest(5, BASE["eo"] + 3)
            mlp(1)
            add_sum("dn1", 6, "o0")

            norm_rest(6, BASE["dn1"] + DN - 1)
            u0 = BASE["od"]
            nc.vector.memset(at[:], 0.0)
            for j in range(8):
                split(u0 + j + RING)
            dve.wait_ge(sem("hgm_in"), 16)
            t_of = {1: fT[:], 2: tot[:, 0:1024], 4: tot[:, 1024:1536], 8: tot[:, 0:256],
                    16: tot[:, 1024:1152], 32: tot[:, 0:64], 64: tot[:, 1024:1056]}

            def merge(idx, hg):
                dve.wait_ge(sem("hg_prod"), 2 * idx + hg + 1)
                q4, k4 = qd[:, 4 * hg:4 * hg + 4, :], kd[:, 4 * hg:4 * hg + 4, :]
                if idx == 0:
                    nc.vector.tensor_tensor(q4, q4, fT[:, 1024 * hg:1024 * hg + 1024]
                                            .rearrange("p (h n) -> p h n", h=4), ALU.mult)\
                        .then_inc(sem("hg_merged"), 1)
                    return
                s = LEVELS[idx - 1]
                nb = 1024 // (2 * s)
                tt = t_of[s][:, hg * 2 * nb:(hg + 1) * 2 * nb].rearrange("p (b two) -> p b two", two=2)
                qv = q4.rearrange("p h n -> p (h n)").rearrange("p (b two s) -> p b two s", two=2, s=s)
                kv = k4.rearrange("p h n -> p (h n)").rearrange("p (b two s) -> p b two s", two=2, s=s)
                nc.vector.tensor_tensor(qv[:, :, 1, :], qv[:, :, 1, :],
                                        tt[:, :, 0:1].broadcast_to([P, nb, s]), ALU.mult)
                if s < 64:
                    nc.vector.tensor_tensor(t_of[2 * s][:, hg * nb:(hg + 1) * nb], tt[:, :, 0], tt[:, :, 1],
                                            ALU.mult)
                nc.vector.tensor_tensor(kv[:, :, 0, :], kv[:, :, 0, :],
                                        tt[:, :, 1:2].broadcast_to([P, nb, s]), ALU.mult)\
                    .then_inc(sem("hg_merged"), 1)
                dve.wait_ge(sem("hg_merged"), 2 * idx + hg + 1)

            def keep(idx, hg):
                if idx == 8:
                    dve.wait_ge(sem("hg_prod"), 2 * idx + hg + 1)
                    nc.vector.tensor_copy(at[:, 4 * hg:4 * hg + 4, 2, :],
                                          DB[2 * hg][:].rearrange("p (h n) -> p h n", h=4))\
                        .then_inc(sem("hg_kept"), 1)
                    return
                for t in range(NT):
                    dst, mask = at[:, 4 * hg:4 * hg + 4, t, :], same_rows(hgm[:, idx, :], 4)
                    if idx == 0:
                        ins = nc.vector.copy_predicated(dst, mask, DB[2 * hg + t][:].rearrange(
                            "p (h n) -> p h n", h=4))
                    else:
                        s = LEVELS[idx - 1]
                        ins = nc.vector.copy_predicated(
                            dst.rearrange("p h (b two s) -> p h b two s", two=2, s=s)[:, :, :, 1, :],
                            mask.rearrange("p h (b two s) -> p h b two s", two=2, s=s)[:, :, :, 1, :],
                            DB[2 * hg + t][:, 0:256].rearrange("p (h b s) -> p h b s", h=4, s=s))
                ins.then_inc(sem("hg_kept"), 1)

            for idx in range(9):
                for hg in range(2):
                    if idx < 8:
                        merge(idx, hg)
                    keep(idx, hg)
                if idx < 6:
                    split(u0 + 8 + idx + RING)
            dve.wait_ge(bank_read[0], bank_reads(u0 + 16)[0])
            dve.wait_ge(bank_read[1], bank_reads(u0 + 16)[1])

            def hg_lo(b):
                dve.wait_ge(sem("hg_hi"), b + 1)
                nc.vector.scalar_tensor_tensor(xTl[:, 2 * b:2 * b + 2, :], halves(DB[b][:]), gain("hgrn"),
                                               xTh[:, 2 * b:2 * b + 2, :], ALU.mult, ALU.subtract)\
                    .then_inc(sem("hg_lo"), 1)

            def hg_gated(b):
                t, hh = b % 2, 4 * (b // 2)
                dve.wait_ge(sem("hg_sq"), b + 1)
                ins = nc.vector.reduce_sum(
                    ss[:, 4 * b:4 * b + 4], kd[:, 2 * b:2 * b + 2, :].rearrange("p a (c n) -> p (a c) n", n=P),
                    AX)
                if t == 1:
                    link(ins)
                    mean_square(f"hg{b // 2}", ss[:, 4 * b - 4:4 * b + 4], P)
                nc.vector.tensor_tensor(
                    oh[:, t, hh:hh + 4, :], DB[b][:].rearrange("p (h n) -> p h n", h=4),
                    gh[:, t, P * hh:P * hh + 512].rearrange("p (h n) -> p h n", h=4), ALU.mult)\
                    .then_inc(sem("hg_gated"), 1)

            def hg_scaled(half):
                k = POW_COL[f"hg{half}"]
                dve.wait_ge(rstd_ready, pow_at(f"hg{half}") + 1)
                dve.wait_ge(sem("hg_gated"), 2 * half + 2)
                for t in range(NT):
                    o = oh[:, t, 4 * half:4 * half + 4, :]
                    nc.vector.tensor_tensor(o, o, same_cols(rstd[:, k.start + 4 * t:k.start + 4 * t + 4], P),
                                            ALU.mult).then_inc(sem("hg_normed"), 1)

            hg_gated(0)
            hg_gated(1)
            hg_gated(2)
            hg_scaled(0)
            hg_gated(3)
            hg_lo(0)
            hg_lo(1)
            hg_scaled(1)
            split(u0 + 14 + RING)
            hg_lo(2)
            hg_lo(3)
            split(u0 + 15 + RING)
            sum_splits("oo")
            add_sum("oo", 7, "f1")

            norm_rest(7, BASE["oo"] + 3)
            mlp(2)
            dve.wait_ge(sem("gb_in"), 64)
            add_sum("dn2", 8, "fin")
            for c in range(4):
                if c == 1:
                    norm_mean(8, "fin", 1)
                k = POW_COL[f"fin.{c // 2}"]
                dve.wait_ge(rstd_ready, pow_at(f"fin.{c // 2}") + 1)
                nc.vector.scalar_tensor_tensor(chunk(y, c), chunk(xn, c), rstd[:, k],
                                               gb[:, 512 * (c % 2):512 * (c % 2) + 512], ALU.mult, ALU.mult)\
                    .then_inc(sem("out_ready"), 1)

        @block.tensor
        def _(pe):
            def passes(out_, stat, mov, start, stop):
                (sh, sl), (mh, ml) = stat, mov
                nc.tensor.matmul(out_, sh, mh, start=start, stop=False)
                nc.tensor.matmul(out_, sh, ml, start=False, stop=False)
                return nc.tensor.matmul(out_, sl, mh, start=False, stop=stop)

            def wait_unit(u, i=None):
                k = 0 if i is None else i
                pe.wait_ge(lo_ready, k * RING + (u + 1))

            def wait_bank(u):
                n = bank_reads(u)[bank(u)]
                if n > 0:
                    pe.wait_ge(bank_read[bank(u)], n)

            def columns(u, act_h, act_l, ready=None):
                hi = whi[:, u % RING, :].rearrange("p (k n) -> p k n", k=KT)
                lo = wlo[:, u % RING, :].rearrange("p (k n) -> p k n", k=KT)
                for f in range(2):
                    for kt in range(KT):
                        if ready is not None and f == 0:
                            pe.wait_ge(ready[0], ready[1] + max(kt + 1, 2))
                        c = slice(P * f, P * f + P)
                        ins = passes(G[bank(u)][:, S * f:S * f + S], (hi[:, kt, c], lo[:, kt, c]),
                                     (act_h[:, kt, :], act_l[:, kt, :]), kt == 0, kt == KT - 1)
                return ins

            def gates(u, act_h, act_l):
                hi = whi[:, u % RING, 0:KT * NG_COLS].rearrange("p (k n) -> p k n", k=KT)
                lo = wlo[:, u % RING, 0:KT * NG_COLS].rearrange("p (k n) -> p k n", k=KT)
                for kt in range(KT):
                    ins = passes(G[bank(u)][0:NG_COLS, 0:S], (hi[:, kt, :], lo[:, kt, :]),
                                 (act_h[:, kt, :], act_l[:, kt, :]), kt == 0, kt == KT - 1)
                return ins

            def rows(u, act_h, act_l, ready=None):
                hi = whi[:, u % RING, :].rearrange("p (k n) -> p k n", k=KT)
                lo = wlo[:, u % RING, :].rearrange("p (k n) -> p k n", k=KT)
                for t in range(NT):
                    for kt in range(KT):
                        if ready is not None and t == 0:
                            pe.wait_ge(ready[0], ready[1] + kt + 1)
                        c = slice(P * t, P * t + P)
                        ins = passes(G[bank(u)][:, 256 * t:256 * t + 256], (act_h[:, kt, c], act_l[:, kt, c]),
                                     (hi[:, kt, :], lo[:, kt, :]), kt == 0, kt == KT - 1)
                return ins

            def unit(u, kind, act_h=None, act_l=None, **kw):
                act_h = xTh if act_h is None else act_h
                act_l = xTl if act_l is None else act_l
                wait_unit(u)
                wait_bank(u)
                kind(u, act_h, act_l, **kw).then_inc(unit_done, 1)

            def keep_clock(bank_, times):
                for _ in range(times):
                    nc.tensor.matmul(bank_[:], ident, cst[:, 0:512], start=True, stop=True)

            def norm_transposes(n, src=None):
                src = xn if src is None else src
                o = norm_banks(n)
                if 2 <= n <= 4:
                    keep_clock(o[3], 2)
                for t in range(NT):
                    pe.wait_ge(sem("diag_ready"), 2 * n + t + 1)
                    for kt in range(KT):
                        c = S * (kt % 2) + P * t
                        ins = nc.tensor.matmul(o[kt // 2][:, c:c + P], src[:, t, P * kt:P * kt + P], diag[:, t, :],
                                               start=True, stop=True)
                        if t == NT - 1 and kt % 2:
                            ins.then_inc(sem("norm_tr"), 1)

            def sum_unit(ph, j, act_h=None, act_l=None, first=None, late=False):
                act_h = xTh if act_h is None else act_h
                act_l = xTl if act_l is None else act_l
                u, last = BASE[ph] + j, N_OF[ph] - 1
                wait_unit(u)
                hi = whi[:, u % RING, :].rearrange("p (k n) -> p k n", k=2)
                lo = wlo[:, u % RING, :].rearrange("p (k n) -> p k n", k=2)
                if first is None:
                    first = 2 * (PAIRS[ph][j] if ph in PAIRS else j)
                for b, o in enumerate(sum_banks(ph)):
                    c, w = slice(P * (b // 2), P * (b // 2) + P), slice(512 * (b % 2), 512 * (b % 2) + 512)
                    if late and SUMS[ph][b][0] == "G":
                        k = int(SUMS[ph][b][1])
                        pe.wait_ge(bank_read[k], bank_reads(BASE[ph])[k])
                    for kk in range(2):
                        ins = passes(o[:], (act_h[:, first + kk, c], act_l[:, first + kk, c]),
                                     (hi[:, kk, w], lo[:, kk, w]), j == 0 and kk == 0, j == last and kk == 1)
                    if j == last and b < 3:
                        ins.then_inc(sem("sum_done"), 1)
                ins.then_inc(unit_done, 1)

            def rotate(j, m, buf, which):
                pe.wait_ge(sem("rope_raw" + which), j + 1)
                if which == "_b":
                    o, u = G[j % 2], BASE["ev"] + 6 + j
                    pe.wait_ge(bank_read[j % 2], bank_reads(u + 1)[j % 2])
                else:
                    o = TB[j % 2]
                    if j >= 2:
                        pe.wait_ge(sem("rope_done" + which), j - 1)
                nc.tensor.matmul(o[:], const(m), buf[:, j % 2, :], start=True, stop=True)\
                    .then_inc(sem("rope_rot" + which), 1)

            def mlp(f):
                u0, p0, n = BASE[f"gu{f}"], f * (GU // 2), [3, 5, 7][f]

                def pair(q, i=None):
                    k = 0 if i is None else i
                    for c, read in ((0, "silu_made"), (1, "h_made")):
                        u = u0 + 2 * q + c
                        wait_unit(u, i)
                        if i is not None or p0 + q >= 1:
                            pe.wait_ge(sem(read), k * 2 + (p0 + q))
                        first = i is None and q == 0 and c == 0
                        columns(u, xTh, xTl, ready=(sem("xT_ready"), KT * n) if first else None)\
                            .then_inc(unit_done, 1)

                for q in range(2):
                    pair(q)
                with pe.Fori(1, GU // 4) as i:
                    for q in range(2):
                        pair(q, i)
                for q in range(GU // 4 * 2, GU // 2):
                    pair(q)
                for d in range(DN):
                    pe.wait_ge(sem("h_lo"), p0 + d + 1)
                    sum_unit(f"dn{f}", d, hTh, hTl)

            norm_transposes(0)
            u0 = BASE["in"]
            unit(u0, rows, ready=(sem("xT_ready"), 0))
            unit(u0 + 1, rows)
            unit(u0 + 2, rows)
            unit(u0 + 3, rows)
            unit(u0 + 4, columns)
            unit(u0 + 5, columns)
            pe.wait_ge(sem("cst_in"), 16)
            rotate(0, "rot64", qraw, "_a")
            norm_transposes(1, y)
            unit(u0 + 6, columns)
            rotate(1, "rot64", qraw, "_a")
            for b in range(2):
                pe.wait_ge(bank_read[b], bank_reads(u0 + 4)[b])
            pe.wait_ge(sem("xT_ready"), 16)
            pe.wait_ge(sem("poolm_in"), 16)
            pe.wait_ge(sem("wpool_in"), 16)
            for g in range(4):
                c = slice(P * g, P * g + P)
                o = halves(DB[g // 2][:])[:, g % 2, :]
                nc.tensor.matmul(o[:, 0:P], un[:, 0, c], poolm[:, g, 0:P], start=True, stop=True)
                nc.tensor.matmul(o[:, P:S], un[:, 0, c], poolm[:, g, P:2 * P], start=True, stop=False)
                ins = nc.tensor.matmul(o[:, P:S], un[:, 1, c], poolm[:, g, 2 * P:], start=False, stop=True)
                if g % 2:
                    ins.then_inc(sem("pooled"), 1)
            unit(u0 + 7, columns)
            rotate(2, "rot64", qraw, "_a")
            for g in range(4):
                if g % 2 == 0:
                    pe.wait_ge(sem("pooled_out"), g // 2 + 1)
                ins = nc.tensor.matmul(halves(DB[2 + g // 2][:])[:, g % 2, :], wpool[:, g, :],
                                       sm[:, g // 2, g % 2, :], start=True, stop=True)
                if g % 2:
                    ins.then_inc(sem("pool_mix"), 1)
            unit(BASE["kv"], columns, memTh, memTl)
            rotate(3, "rot64", qraw, "_a")

            def da_scores(s):
                h, t = s // 2, s % 2
                kend = P * (t + 1)
                if s == 0:
                    pe.wait_ge(sem("rope_done_a"), 3)
                    pe.wait_ge(sem("pool_lo"), 4)
                if s == 4:
                    pe.wait_ge(sem("rope_done_a"), 4)
                if s >= 2:
                    pe.wait_ge(sem("da_max"), s - 1)
                for m in range(2):
                    r = slice(64 * m, 64 * m + 64)
                    ins = nc.tensor.matmul(DB[2 * t + m][:, 0:kend], qT[r, h, P * t:P * t + P],
                                           kT[r, h, 0:kend], start=True, stop=True)
                ins.then_inc(sem("da_scores"), 1)

            def da_transposes(s):
                t = s % 2
                pe.wait_ge(sem("da_probs"), s + 1)
                if s >= 2:
                    pe.wait_ge(sem("da_nat"), s - 1)
                for b in range(t + 1):
                    ins = nc.tensor.transpose(TB[t][:, P * b:P * b + P], sm[:, t, 0, P * b:P * b + P], ident)
                ins.then_inc(sem("da_tr"), 1)

            def da_out(s):
                h, t = s // 2, s % 2
                pe.wait_ge(sem("aT"), s + 1)
                for b in range(t + 1):
                    ins = nc.tensor.matmul(TB[t][:, 256:384], aT[:, t, P * b:P * b + P],
                                           vn[:, b, P * h:P * h + P], start=(b == 0), stop=(b == t))
                ins.then_inc(sem("da_out"), 1)

            kv0 = BASE["kv"]
            da_scores(0)
            da_scores(1)
            for s in range(8):
                if s < 7:
                    unit(kv0 + s + 1, columns if s < 3 else rows, memTh, memTl)
                else:
                    pe.wait_ge(sem("da_max"), 8)
                    sum_unit("out", 0, late=True)
                if s >= 1:
                    da_out(s - 1)
                da_transposes(s)
                if s < 6:
                    da_scores(s + 2)
            da_out(7)

            def head_transposes(src, waits, signal, pairs, first=0):
                pe.wait_ge(*waits)
                for hp in range(first, first + pairs):
                    for h in (2 * hp, 2 * hp + 1):
                        for t in range(NT):
                            ins = nc.tensor.transpose(DB[hp][:, S * (h % 2) + P * t:S * (h % 2) + P * t + P],
                                                      src(t, h), ident)
                    ins.then_inc(signal, 1)

            sum_unit("out", 1)
            head_transposes(lambda t, h: un[:, t, P * h:P * h + P], (sem("da_normed"), 1), sem("da_T"), 2)
            for j in range(2):
                pe.wait_ge(sem("da_lo"), j + 1)
                sum_unit("out", 2 + j)

            norm_transposes(2)
            u0 = BASE["xq"]

            def x_scores(h):
                n = bank_reads(u0 + h + 1)
                pe.wait_ge(bank_read[bank(u0 + h)], n[bank(u0 + h)])
                if h == 0:
                    pe.wait_ge(sem("xT_ready"), 24)
                if h >= 2:
                    pe.wait_ge(sem("x_exp"), h - 1)
                for t in range(NT):
                    for dt in range(2):
                        ins = nc.tensor.matmul(halves(DB[h % 2][:])[:, t, :],
                                               xqT[:, 2 * h + dt, P * t:P * t + P], kxT[:, 2 * h + dt, :],
                                               start=(dt == 0), stop=(dt == 1))
                ins.then_inc(sem("x_scores"), 1)

            def x_transposes(h):
                pe.wait_ge(sem("x_probs"), h + 1)
                if h >= 2:
                    pe.wait_ge(sem("x_pT"), h - 1)
                for mt in range(2):
                    for t in range(NT):
                        ins = nc.tensor.transpose(TB[h % 2][:, S * mt + P * t:S * mt + P * t + P],
                                                  px[:, h % 2, t, P * mt:P * mt + P], ident)
                ins.then_inc(sem("x_tr"), 1)

            def x_out(h):
                pe.wait_ge(sem("x_pT"), h + 1)
                if h >= 2:
                    pe.wait_ge(sem("x_lo"), h - 1)
                for dt in range(2):
                    c = S * h + P * dt
                    for mt in range(2):
                        ins = nc.tensor.matmul(halves(DB[2 + h % 2][:])[:, dt, :], vx[:, mt, c:c + P],
                                               pxT[:, h % 2, mt, :], start=(mt == 0), stop=(mt == 1))
                ins.then_inc(sem("x_out"), 1)

            unit(u0, columns, ready=(sem("xT_ready"), 16))
            unit(u0 + 1, columns)
            x_scores(0)
            unit(u0 + 2, columns)
            x_scores(1)
            x_transposes(0)
            unit(u0 + 3, columns)
            x_scores(2)
            x_transposes(1)
            x_out(0)
            x_scores(3)
            x_transposes(2)
            x_out(1)
            x_transposes(3)
            x_out(2)
            x_out(3)
            pe.wait_ge(sem("x_exp"), 4)
            for j in range(4):
                pe.wait_ge(sem("x_lo"), j + 1)
                sum_unit("xo", j)

            norm_transposes(3)
            mlp(0)

            norm_transposes(4)
            u0 = BASE["ev"]

            def ret_scores(h):
                if h >= 2:
                    pe.wait_ge(sem("ret_probs"), h - 1)
                nc.tensor.matmul(DB[h % 2][:, 0:256], rkT[:, h, 0:P], rqT[:, h, :], start=True, stop=True)
                nc.tensor.matmul(DB[h % 2][:, 256:384], rkT[:, h, P:S], rqT[:, h, P:S], start=True, stop=True)\
                    .then_inc(sem("ret_scores"), 1)

            def ret_out(h):
                pe.wait_ge(sem("ret_probs"), h + 1)
                if h >= 2:
                    pe.wait_ge(sem("ret_nat"), h - 1)
                c = slice(P * h, P * h + P)
                o = TB[h % 2]
                nc.tensor.matmul(o[:, 0:P], rp[:, h % 2, 0:P], rv[:, 0, c], start=True, stop=True)
                nc.tensor.matmul(o[:, P:2 * P], rp[:, h % 2, P:2 * P], rv[:, 0, c], start=True, stop=False)
                nc.tensor.matmul(o[:, P:2 * P], rp[:, h % 2, 2 * P:3 * P], rv[:, 1, c], start=False, stop=True)\
                    .then_inc(sem("ret_out"), 1)

            unit(u0, columns, ready=(sem("xT_ready"), 32))
            for j in range(1, 4):
                unit(u0 + j, columns)
            unit(u0 + 4, rows)
            pe.wait_ge(sem("cmp_blocks"), 1)
            pe.wait_ge(sem("w1_in"), 16)
            for kind in range(2):
                for j in range(16):
                    ins = nc.tensor.matmul(TB[kind][0:64, 0:2 * NCMP].rearrange("p (g n) -> p g n", g=2),
                                           w1[:, kind, j, :], blk[:, kind, :, :, j], start=(j == 0), stop=(j == 15))
            ins.then_inc(sem("cmp_hid"), 1)
            unit(u0 + 5, gates)
            unit(u0 + 6, columns)
            pe.wait_ge(bank_read[1], bank_reads(u0 + 6)[1])
            for t in range(NT):
                ins = nc.tensor.transpose(G[1][:, NG_COLS * t:NG_COLS * t + NG_COLS], gT[:, P * t:P * t + P],
                                          ident[0:NG_COLS, 0:NG_COLS])
            ins.then_inc(sem("gates_T"), 1)
            pe.wait_ge(sem("cmp_gelu"), 1)
            nc.tensor.matmul(TB[0][0:64, 64:96].rearrange("p (g n) -> p g n", g=2)[:, :, 0:NCMP],
                             cmps[0:64, 32:96], hid[0:64, 0, :, 0:NCMP], start=True, stop=True)
            for g in range(2):
                ins = nc.tensor.matmul(TB[1][0:NCMP, 64 + 64 * g:128 + 64 * g], hid[0:64, 1, g, 0:NCMP],
                                       cmps[0:64, 96:160], start=True, stop=True)
            ins.then_inc(sem("cmp_kv"), 1)
            def n_scores(s):
                h, t = s // 2, s % 2
                kend, g = P * (t + 1), h // 4
                r = slice(64 * (h % 2), 64 * (h % 2) + 64)
                if s >= 2:
                    pe.wait_ge(sem("n_max"), s - 1)
                for br in range(2):
                    ins = nc.tensor.matmul(DB[t][:, 256 * br:256 * br + kend], nqT[r, h // 2, P * t:P * t + P],
                                           ksT[r, br, g, 0:kend], start=True, stop=True)
                ins.then_inc(sem("n_scores"), 1)

            def n_transposes(s):
                h, t = s // 2, s % 2
                pe.wait_ge(sem("n_probs"), s + 1)
                if t == 0 and h >= 1:
                    pe.wait_ge(sem("npT_a"), h)
                    pe.wait_ge(sem("npT_b"), h)
                for br in range(2):
                    for b in range(t + 1):
                        c = P * t + P * b
                        ins = nc.tensor.transpose(TB[br][:, c:c + P], nsm[:, t, br, P * b:P * b + P], ident)
                ins.then_inc(sem("n_tr"), 1)

            def n_out(h):
                g, hp, par = h // 4, h // 2, h % 2
                r = slice(64 * par, 64 * par + 64)
                pe.wait_ge(sem("npT_a"), h + 1)
                pe.wait_ge(sem("npT_b"), h + 1)
                if hp >= 2 and par == 0:
                    pe.wait_ge(sem("n_lo"), hp - 1)
                o = DB[2 + hp % 2]
                idx = 8 * par + 2 * hp
                for br in range(2):
                    c = P * br + 64 * g
                    nc.tensor.matmul(o[r, 0:S], vsw[:, 0, c:c + 64], npT[:, h % 2, br, 0:S],
                                     start=(br == 0), stop=False)
                    nc.tensor.matmul(o[r, P:S], vsw[:, 1, c:c + 64], npT[:, h % 2, br, S:S + P],
                                     start=False, stop=False)
                nc.tensor.matmul(o[r, 0:S], vcm[0:NCMP, g, :], pcT[0:NCMP, idx:idx + 2, :]
                                 .rearrange("p a n -> p (a n)"), start=False, stop=True)\
                    .then_inc(sem("n_out"), 1)

            def cmp_transposes(b):
                if b >= 2:
                    pe.wait_ge(sem("pcT"), b - 1)
                o = DB[2 + b % 2]
                for k in range(4):
                    ins = nc.tensor.transpose(o[0:NCMP, P * k:P * k + P], pc[:, 4 * b + k, :], ident)
                ins.then_inc(sem("cmp_tr"), 1)

            n_scores(0)
            n_scores(1)
            pe.wait_ge(sem("cmp_out"), 1)
            for h in range(8):
                par, hp, g = h % 2, h // 2, h // 4
                r = slice(64 * par, 64 * par + 64)
                for t in range(NT):
                    c = 256 + (2 * hp + t) * NCMP
                    ins = nc.tensor.matmul(TB[par][:, c:c + NCMP], nqT[r, hp, P * t:P * t + P],
                                           kcm[r, g, 0:NCMP], start=True, stop=True)
            ins.then_inc(sem("cmp_scores"), 1)
            rotate(0, "rot128", braw, "_b")
            pe.wait_ge(sem("gates_read"), 1)
            unit(u0 + 7, columns)
            pe.wait_ge(sem("cmp_probs"), 1)
            cmp_transposes(0)
            cmp_transposes(1)
            for h in range(8):
                if h < 7:
                    n_scores(2 * h + 2)
                    n_scores(2 * h + 3)
                n_transposes(2 * h)
                n_transposes(2 * h + 1)
                if h == 0:
                    cmp_transposes(2)
                    cmp_transposes(3)
                if h < 3:
                    rotate(1 + h, "rot128", braw, "_b")
                if h < 6:
                    if h < 4:
                        pe.wait_ge(sem("rope_done_b"), h + 1)
                    unit(u0 + 8 + h, columns if h < 2 else rows)
                if h == 0:
                    pe.wait_ge(sem("pcT"), 4)
                if h == 7:
                    pe.wait_ge(sem("n_max"), 16)
                    ret_scores(0)
                    ret_scores(1)
                n_out(h)
            pe.wait_ge(bank_read[bank(u0 + 11)], bank_reads(u0 + 12)[bank(u0 + 11)])
            for h in range(4):
                ret_out(h)
                if h < 2:
                    ret_scores(h + 2)
            for b in range(2):
                pe.wait_ge(bank_read[b], bank_reads(BASE["eo"])[b])
            pe.wait_ge(sem("n_lo"), 4)
            sum_unit("eo", 0, nh, nl, 0)
            sum_unit("eo", 1, nh, nl, 2)
            head_transposes(lambda t, h: on[:, 4 * t + h, :], (sem("ret_normed"), 1), sem("ret_T"), 2)
            for j in range(2):
                pe.wait_ge(sem("ret_lo"), j + 1)
                sum_unit("eo", 2 + j)

            norm_transposes(5)
            mlp(1)

            norm_transposes(6)
            u0 = BASE["od"]
            unit(u0, columns, ready=(sem("xT_ready"), 48))
            for j in range(1, 8):
                unit(u0 + j, columns)

            def level(idx, hg):
                if idx == 0 and hg == 0:
                    for b in range(2):
                        pe.wait_ge(bank_read[b], bank_reads(u0 + 8)[b])
                    pe.wait_ge(sem("xT_ready"), 56)
                if idx >= 1:
                    pe.wait_ge(sem("hg_merged"), 2 * (idx - 1) + hg + 1)
                    pe.wait_ge(sem("hg_kept"), 2 * (idx - 1) + hg + 1)
                for h in range(4 * hg, 4 * hg + 4):
                    c = P * (h % 4)
                    if idx == 8:
                        ins = nc.tensor.matmul(DB[2 * hg][:, c:c + P], kd[:, h, 0:P], qd[:, h, P:S],
                                               start=True, stop=True)
                    else:
                        for t in range(NT):
                            tk = slice(P * t, P * t + P)
                            if idx == 0:
                                queries, w = qd[:, h, tk], P
                            else:
                                queries, w = second_blocks(qd[:, h, tk], LEVELS[idx - 1]), P // 2
                            c = w * (h % 4)
                            ins = nc.tensor.matmul(DB[2 * hg + t][:, c:c + w], kd[:, h, tk], queries,
                                                   start=True, stop=True)
                ins.then_inc(sem("hg_prod"), 1)

            for idx in range(9):
                for hg in range(2):
                    level(idx, hg)
                if idx < 8:
                    unit(u0 + 8 + idx, rows)
            pe.wait_ge(sem("hg_kept"), 18)
            for b in range(2):
                pe.wait_ge(bank_read[b], bank_reads(u0 + 16)[b])
            for b in range(4):
                t = b % 2
                for h in range(4 * (b // 2), 4 * (b // 2) + 4):
                    o, c = DB[b][:, P * (h % 4):P * (h % 4) + P], slice(P * h, P * h + P)
                    if t == 0:
                        ins = nc.tensor.matmul(o, at[:, h, 0, :], vh[:, 0, c], start=True, stop=True)
                    else:
                        nc.tensor.matmul(o, at[:, h, 2, :], vh[:, 0, c], start=True, stop=False)
                        ins = nc.tensor.matmul(o, at[:, h, 1, :], vh[:, 1, c], start=False, stop=True)
                ins.then_inc(sem("hg_out"), 1)
            keep_clock(TB[0], 2)
            for j in range(4):
                if j < 2:
                    head_transposes(lambda t, h: oh[:, t, h, :], (sem("hg_normed"), 2 * j + 2), sem("hg_T"),
                                    2, 2 * j)
                pe.wait_ge(sem("hg_lo"), j + 1)
                sum_unit("oo", j)

            norm_transposes(7)
            mlp(2)


def _constants():
    p = np.arange(P)
    cf = np.zeros((P, N_CONST), np.float32)

    def put(name, a):
        at, n = CONST[name]
        cf[:, at:at + n] = a

    put("ident", np.eye(P))
    put("causal", np.where(p[None, :] <= p[:, None], 0.0, NEG))
    t = np.arange(S)
    ends = np.arange(NCMP) * 16 + 31
    m = np.where(ends[None, :] <= t[:, None], 0.0, NEG).reshape(NT, P, NCMP)
    put("cmpmask", m.transpose(1, 0, 2).reshape(P, NT * NCMP))
    put("cmpvalid", (t >= 31).astype(np.float32).reshape(NT, P).T)
    r64, r128 = np.zeros((P, P)), np.zeros((P, P))
    for b in (0, 64):
        for i in range(8):
            r64[b + i + 8, b + i] = -1.0
            r64[b + i, b + i + 8] = 1.0
    for i in range(64):
        r128[i + 64, i] = -1.0
        r128[i, i + 64] = 1.0
    put("rot64", r64)
    put("rot128", r128)
    freq = np.zeros((P, 1), np.float32)
    inv = (np.float32(500000.0) ** (-np.arange(0, 16, 2, dtype=np.float32) / np.float32(16))).astype(np.float32)
    for b in (0, 8, 64, 72):
        freq[b:b + 8, 0] = inv
    put("invfreq", freq)
    put("half", -0.5)

    pool = np.zeros((P, 4, 3 * P))
    for g, w in enumerate(POOL_WINDOWS):
        s_, t_ = np.arange(S)[:, None], np.arange(S)[None, :]
        full = np.where((s_ <= t_) & (s_ > t_ - w), 1.0 / np.minimum(t_ + 1, w), 0.0) - (s_ == t_)
        pool[:, g, 0:P] = full[0:P, 0:P]
        pool[:, g, P:2 * P] = full[0:P, P:]
        pool[:, g, 2 * P:] = full[P:, P:]

    inv2 = (np.float32(10000.0) ** (-np.arange(64, dtype=np.float32) / np.float32(64))).astype(np.float32)
    ang = (np.arange(S, dtype=np.float32)[None, :] * np.tile(inv2, 2)[:, None]).astype(np.float32)
    ret = np.zeros((P, 2 * S + 4 * 384))
    ret[:, 0:S], ret[:, S:2 * S] = np.cos(ang.astype(np.float64)), np.sin(ang.astype(np.float64))
    for h in range(4):
        lg = np.log(1.0 - 2.0 ** (-5.0 - h))
        diff = p[None, :] - p[:, None]
        diag = np.where(diff >= 0, np.exp(lg * np.maximum(diff, 0)), 0.0)
        off = np.exp(lg * (diff + P))
        ret[:, 2 * S + 384 * h:2 * S + 384 * (h + 1)] = np.concatenate([diag, off, diag], 1) * 128 ** -0.5

    hg = np.zeros((P, 8, P), np.int32)
    hg[:, 0, :] = np.eye(P)
    for i, s_ in enumerate(LEVELS):
        kb, qb = p[:, None] // s_, p[None, :] // s_
        hg[:, i + 1, :] = (kb // 2 == qb // 2) & (kb % 2 == 0) & (qb % 2 == 1)
    return cf, pool.astype(np.float32), ret.astype(np.float32), hg


def _wide(w):
    n = w.shape[1] // 256
    return w.reshape(KT, P, n, 256).transpose(2, 1, 0, 3).reshape(n, P, UNIT)


def _down(w):
    return w.reshape(DN, 2, P, D).transpose(0, 2, 1, 3).reshape(DN, P, UNIT)


def _sum(w, ph):
    return w.reshape(4, 2, P, D).transpose(0, 2, 1, 3).reshape(4, P, UNIT)[list(PAIRS[ph])]


def _stream(i):
    def gate_up(g, u):
        return np.stack([_wide(g), _wide(u)], 1).reshape(GU, P, UNIT)

    def cols(w, *ranges):
        return np.concatenate([w[:, a:b] for a, b in ranges], 1)

    ev = i["even_w_in_2"][0]
    ng = np.zeros((1, P, UNIT), np.float32)
    ng[0, :, 0:KT * NG_COLS] = ev[:, 3328:].reshape(KT, P, NG_COLS).transpose(1, 0, 2).reshape(P, -1)
    parts = [
        _wide(cols(i["w_in"], (1024, 2048), (0, 1024))), _wide(i["w_xkv"]), _sum(i["w_out"], "out"),
        _wide(i["w_xq"]), _sum(i["w_xo"], "xo"),
        gate_up(i["w_gate"], i["w_up"]), _down(i["w_down"]),
        _wide(ev[:, 2048:2816]), _wide(cols(ev, (2816, 2944), (3072, 3200))),
        _wide(cols(ev, (2944, 3072), (3200, 3328))), ng, _wide(ev[:, 0:2048]),
        _sum(i["even_w_out_2"][0], "eo"), gate_up(i["ffn_w1_2"][0], i["ffn_w3_2"][0]), _down(i["ffn_w2_2"][0]),
        _wide(i["odd_w_in_2"][0]), _sum(i["odd_w_out_2"][0], "oo"),
        gate_up(i["ffn_w1_2"][1], i["ffn_w3_2"][1]), _down(i["ffn_w2_2"][1]),
    ]
    out = np.concatenate(parts, 0)
    assert out.shape == (N_UNITS, P, UNIT)
    return out


def kernel(**inputs):
    import concourse.bacc as bacc
    from concourse.bass_utils import run_bass_kernel_spmd

    i = {k: np.asarray(v) for k, v in inputs.items()}
    gains = np.zeros((P, N_GAIN), np.float32)

    def put(name, a):
        at, n = GAIN[name]
        gains[:, at:at + n] = a

    for name, g in (("g_mix_pre", i["g_mix_pre"]), ("g_x_pre", i["g_x_pre"]), ("g_mem", i["g_mem"]),
                    ("g_ffn_pre", i["g_ffn_pre"]), ("mix0", i["norm_mix_g_2"][0]),
                    ("mix1", i["norm_mix_g_2"][1]), ("ffn0", i["norm_ffn_g_2"][0]),
                    ("ffn1", i["norm_ffn_g_2"][1])):
        put(name, g.reshape(KT, P).T)
    put("g_subln", i["g_subln"][:, None])
    put("hgrn", i["hgrn_norm_g_2"][0][:, None])
    put("pool_scale", i["pool_scale"].reshape(4, P).T)
    put("lam", np.concatenate([i["lambda_q1"], i["lambda_q2"], i["lambda_k1"], i["lambda_k2"]])[None, :])
    cf, pool, ret, hg = _constants()

    def both(a):
        return np.concatenate([a, a], 0)

    def by_offset(w, axis):
        return np.concatenate([w[0::2].swapaxes(0, axis), w[1::2].swapaxes(0, axis)], 0)

    cmpw = np.stack([by_offset(i[k][0].reshape(32, 64, 64), 1) for k in ("cmp_w1_k_2", "cmp_w1_v_2")], 1)
    cmps = np.concatenate([by_offset(i["cmp_pos_k_2"][0], 1), by_offset(i["cmp_pos_v_2"][0], 1),
                           both(i["cmp_w2_k_2"][0]), both(i["cmp_w2_v_2"][0])], 1)
    arrays = {
        "stream": _stream(i), "x": i["x"][0], "mem": i["mem"][0], "pos": i["positions"][0], "gains": gains,
        "rows": np.stack([i["g_mix_post"], i["g_x_post"], i["g_ffn_post"], i["final_norm_g_2"]]),
        "consts": cf, "poolm": pool, "wpool": i["w_pool"].transpose(1, 0, 2), "retm": ret, "hgm": hg,
        "cmpw": cmpw, "cmps": cmps,
    }
    arrays = {f"in_{k}": np.ascontiguousarray(v) for k, v in arrays.items()}
    nc = bacc.Bacc("TRN2", target_bir_lowering=False, num_devices=1)
    args = [nc.dram_tensor(k, v.shape, mybir.dt.from_np(v.dtype), kind="ExternalInput").ap()
            for k, v in arrays.items()]
    out = nc.dram_tensor("out", (S, D), F32, kind="ExternalOutput").ap()
    build(nc, *args, out)
    r = run_bass_kernel_spmd(nc, [arrays], core_ids=[0])
    return r.results[0]["out"].reshape(1, S, D)
```
